# Optimizing a Trainium2 kernel written in Bass

```python
import jax, jax.numpy as jnp
from jax import lax
import numpy as np

D_MODEL = 1024
BATCH = 1
SEQ = 256
DEPTH = 2

NSA_HEADS = 8
NSA_GROUPS = 2
NSA_HPG = NSA_HEADS // NSA_GROUPS
NSA_DK = 64
NSA_DV = 64
CMP_BLOCK = 32
CMP_STRIDE = 16
SLC_BLOCK = 64
N_SELECT = 16
WINDOW = 512
MLA_HEADS = 8
MLA_NOPE = 64
MLA_ROPE = 32
MLA_V = 64
MLA_Q_RANK = 384
MLA_KV_RANK = 256
ROPE_THETA = 10000.0
D_FF = 2816
N_MOD = 9
Q_BLOCK = 128
NORM_EPS = 1e-6

IN_SPLITS = (
    NSA_HEADS * NSA_DK,
    NSA_GROUPS * NSA_DK,
    NSA_GROUPS * NSA_DV,
    NSA_GROUPS * NSA_DK,
    NSA_GROUPS * NSA_DV,
    NSA_GROUPS * NSA_DK,
    NSA_GROUPS * NSA_DV,
    3 * NSA_HEADS,
    MLA_Q_RANK,
    MLA_KV_RANK,
    MLA_ROPE,
    2 * D_MODEL,
)
IN_TOTAL = sum(IN_SPLITS)


def rms_norm(x):
    xf = x.astype(jnp.float32)
    return (xf * lax.rsqrt(jnp.mean(xf * xf, -1, keepdims=True) + NORM_EPS)).astype(x.dtype)

def modulate(x, shift, scale):
    return rms_norm(x) * (1 + scale[:, None, :]) + shift[:, None, :]

def swiglu(u, w_gate, w_up, w_down):
    return (jax.nn.silu(u @ w_gate) * (u @ w_up)) @ w_down

def masked_softmax(scores, mask):
    s = jnp.where(mask, scores.astype(jnp.float32), -jnp.inf)
    m = jnp.max(s, -1, keepdims=True)
    m = jnp.where(jnp.isfinite(m), m, 0.0)
    p = jnp.exp(s - m)
    return p / jnp.maximum(jnp.sum(p, -1, keepdims=True), 1.0)

def rope(x, cos, sin):
    half = x.shape[-1] // 2
    x1, x2 = x[..., :half], x[..., half:]
    return jnp.concatenate([x1 * cos - x2 * sin, x1 * sin + x2 * cos], -1).astype(x.dtype)

def alibi_slopes(n):
    return 2.0 ** (-8.0 * jnp.arange(1, n + 1, dtype=jnp.float32) / n)

def compress(k, w1, w2, pe):
    B, G, S, d = k.shape
    n_chunks = S // CMP_STRIDE
    r = CMP_BLOCK // CMP_STRIDE
    n_cmp = n_chunks - r + 1
    chunks = k.reshape(B, G, n_chunks, CMP_STRIDE, d)
    blocks = jnp.concatenate([chunks[:, :, j:j + n_cmp] for j in range(r)], axis=3)
    blocks = (blocks + pe).reshape(B, G, n_cmp, CMP_BLOCK * d)
    return jax.nn.gelu(blocks @ w1) @ w2

def nsa_attention(q, k_c, v_c, k_s, v_s, k_w, v_w, gates):
    B, G, HPG, S, dk = q.shape
    dv = v_c.shape[-1]
    nq = S // Q_BLOCK
    n_slc = S // SLC_BLOCK
    n_top = min(N_SELECT, n_slc)
    n_cmp = k_c.shape[2]
    ratio = SLC_BLOCK // CMP_STRIDE
    r = CMP_BLOCK // CMP_STRIDE
    cmp_end = jnp.arange(n_cmp) * CMP_STRIDE + CMP_BLOCK - 1
    ks_blocks = k_s.reshape(B, G, n_slc, SLC_BLOCK, dk)
    vs_blocks = v_s.reshape(B, G, n_slc, SLC_BLOCK, dv)
    kw_pad = jnp.pad(k_w, ((0, 0), (0, 0), (WINDOW, 0), (0, 0)))
    vw_pad = jnp.pad(v_w, ((0, 0), (0, 0), (WINDOW, 0), (0, 0)))
    slope = alibi_slopes(NSA_HEADS).reshape(1, G, HPG, 1, 1)
    scale = dk ** -0.5
    b_ix = jnp.arange(B)[:, None, None, None]
    g_ix = jnp.arange(G)[None, :, None, None]
    blk = jnp.arange(n_slc)

    def block(i):
        q0 = i * Q_BLOCK
        qb = lax.dynamic_slice_in_dim(q, q0, Q_BLOCK, axis=3)
        gb = lax.dynamic_slice_in_dim(gates, q0, Q_BLOCK, axis=3)
        t = q0 + jnp.arange(Q_BLOCK)
        d_c = (t[:, None] - cmp_end[None, :]).astype(jnp.float32)
        s_c = jnp.einsum('bghqd,bgnd->bghqn', qb, k_c).astype(jnp.float32) * scale - slope * d_c
        p_c = masked_softmax(s_c, cmp_end[None, :] <= t[:, None])
        o_c = jnp.einsum('bghqn,bgnd->bghqd', p_c.astype(v_c.dtype), v_c)
        imp = jnp.pad(p_c.sum(axis=2), ((0, 0), (0, 0), (0, 0), (r - 1, n_slc * ratio - n_cmp)))
        imp_s = imp[..., 0:ratio * n_slc:ratio]
        for j in range(1, ratio + r - 1):
            imp_s = imp_s + imp[..., j:j + ratio * n_slc:ratio]
        cur = t // SLC_BLOCK
        forced = (blk[None, :] == 0) | (blk[None, :] == cur[:, None]) | (blk[None, :] == cur[:, None] - 1)
        valid = blk[None, :] * SLC_BLOCK <= t[:, None]
        imp_s = jnp.where(forced, jnp.inf, jnp.where(valid, imp_s, -jnp.inf))
        _, idx = lax.top_k(imp_s, n_top)
        ks = ks_blocks[b_ix, g_ix, idx].reshape(B, G, Q_BLOCK, n_top * SLC_BLOCK, dk)
        vs = vs_blocks[b_ix, g_ix, idx].reshape(B, G, Q_BLOCK, n_top * SLC_BLOCK, dv)
        pos_s = (idx[..., None] * SLC_BLOCK + jnp.arange(SLC_BLOCK)).reshape(B, G, Q_BLOCK, n_top * SLC_BLOCK)
        d_s = (t[:, None] - pos_s).astype(jnp.float32)[:, :, None]
        s_s = jnp.einsum('bghqd,bgqkd->bghqk', qb, ks).astype(jnp.float32) * scale - slope * d_s
        p_s = masked_softmax(s_s, (pos_s <= t[:, None])[:, :, None])
        o_s = jnp.einsum('bghqk,bgqkd->bghqd', p_s.astype(vs.dtype), vs)
        kw = lax.dynamic_slice_in_dim(kw_pad, q0, WINDOW + Q_BLOCK, axis=2)
        vw = lax.dynamic_slice_in_dim(vw_pad, q0, WINDOW + Q_BLOCK, axis=2)
        pos_w = q0 - WINDOW + jnp.arange(WINDOW + Q_BLOCK)
        d_w = t[:, None] - pos_w[None, :]
        mask_w = (d_w >= 0) & (d_w < WINDOW) & (pos_w[None, :] >= 0)
        s_w = jnp.einsum('bghqd,bgkd->bghqk', qb, kw).astype(jnp.float32) * scale - slope * d_w.astype(jnp.float32)
        p_w = masked_softmax(s_w, mask_w)
        o_w = jnp.einsum('bghqk,bgkd->bghqd', p_w.astype(vw.dtype), vw)
        return gb[..., 0:1] * o_c + gb[..., 1:2] * o_s + gb[..., 2:3] * o_w

    out = lax.map(block, jnp.arange(nq))
    return out.transpose(1, 0, 4, 2, 3, 5).reshape(B, S, G * HPG * dv)

def mla_attention(q_nope, q_rope, k_nope, k_rope, v):
    B, H, S, _ = q_nope.shape
    dv = v.shape[-1]
    nq = S // Q_BLOCK
    scale = (MLA_NOPE + MLA_ROPE) ** -0.5
    kpos = jnp.arange(S)

    def block(i):
        q0 = i * Q_BLOCK
        qn = lax.dynamic_slice_in_dim(q_nope, q0, Q_BLOCK, axis=2)
        qr = lax.dynamic_slice_in_dim(q_rope, q0, Q_BLOCK, axis=2)
        s = (jnp.einsum('bhqd,bhkd->bhqk', qn, k_nope)
             + jnp.einsum('bhqd,bkd->bhqk', qr, k_rope)).astype(jnp.float32) * scale
        qpos = q0 + jnp.arange(Q_BLOCK)
        p = masked_softmax(s, kpos[None, :] <= qpos[:, None])
        return jnp.einsum('bhqk,bhkd->bhqd', p.astype(v.dtype), v)

    out = lax.map(block, jnp.arange(nq))
    return out.transpose(1, 0, 3, 2, 4).reshape(B, S, H * dv)

def token_mix(u, cos, sin, w_in, cmpk_w1, cmpk_w2, cmpk_pe, cmpv_w1, cmpv_w2, cmpv_pe,
              mla_q_norm, mla_w_uq, mla_kv_norm, mla_w_uk, mla_w_uv,
              w_branch_a, w_branch_b, w_out):
    B, S, _ = u.shape
    points = np.cumsum(IN_SPLITS)[:-1].tolist()
    (q_a, kc, vc, ks, vs, kw, vw, g_nsa, cq, ckv, kr, g_merge) = jnp.split(u @ w_in, points, axis=-1)
    q_a = q_a.reshape(B, S, NSA_GROUPS, NSA_HPG, NSA_DK).transpose(0, 2, 3, 1, 4)
    grp = lambda t: t.reshape(B, S, NSA_GROUPS, -1).transpose(0, 2, 1, 3)
    g_nsa = jax.nn.sigmoid(g_nsa).reshape(B, S, NSA_GROUPS, NSA_HPG, 3).transpose(0, 2, 3, 1, 4)
    k_c = compress(grp(kc), cmpk_w1, cmpk_w2, cmpk_pe)
    v_c = compress(grp(vc), cmpv_w1, cmpv_w2, cmpv_pe)
    o_a = nsa_attention(q_a, k_c, v_c, grp(ks), grp(vs), grp(kw), grp(vw), g_nsa)
    q = (rms_norm(cq) * mla_q_norm) @ mla_w_uq
    q = q.reshape(B, S, MLA_HEADS, MLA_NOPE + MLA_ROPE)
    q_nope = q[..., :MLA_NOPE].transpose(0, 2, 1, 3)
    q_rope = rope(q[..., MLA_NOPE:], cos[:, None, :], sin[:, None, :]).transpose(0, 2, 1, 3)
    ckv = rms_norm(ckv) * mla_kv_norm
    k_nope = (ckv @ mla_w_uk).reshape(B, S, MLA_HEADS, MLA_NOPE).transpose(0, 2, 1, 3)
    v = (ckv @ mla_w_uv).reshape(B, S, MLA_HEADS, MLA_V).transpose(0, 2, 1, 3)
    k_rope = rope(kr, cos, sin)
    o_b = mla_attention(q_nope, q_rope, k_nope, k_rope, v)
    g_a, g_b = jnp.split(g_merge, 2, axis=-1)
    y = jax.nn.sigmoid(g_a) * (o_a @ w_branch_a) + jax.nn.sigmoid(g_b) * (o_b @ w_branch_b)
    return y @ w_out

def first_inputs(seed: int = 0) -> dict:
    key = jax.random.key(seed)
    keys = iter(jax.random.split(key, 40))
    nrm = lambda shape, s: jax.random.normal(next(keys), shape, jnp.float32) * s
    L, D = DEPTH, D_MODEL
    return {
        "x": nrm((BATCH, SEQ, D), 1.0),
        "c": nrm((BATCH, D), 1.0),
        "w_ada": nrm((L, D, N_MOD * D), D ** -0.5),
        "b_ada": nrm((L, N_MOD * D), 0.02),
        "ffn1_gate": nrm((L, D, D_FF), D ** -0.5),
        "ffn1_up": nrm((L, D, D_FF), D ** -0.5),
        "ffn1_down": nrm((L, D_FF, D), D_FF ** -0.5),
        "ffn2_gate": nrm((L, D, D_FF), D ** -0.5),
        "ffn2_up": nrm((L, D, D_FF), D ** -0.5),
        "ffn2_down": nrm((L, D_FF, D), D_FF ** -0.5),
        "w_in": nrm((L, D, IN_TOTAL), D ** -0.5),
        "cmpk_w1": nrm((L, CMP_BLOCK * NSA_DK, NSA_DK), (CMP_BLOCK * NSA_DK) ** -0.5),
        "cmpk_w2": nrm((L, NSA_DK, NSA_DK), NSA_DK ** -0.5),
        "cmpk_pe": nrm((L, CMP_BLOCK, NSA_DK), 0.5),
        "cmpv_w1": nrm((L, CMP_BLOCK * NSA_DV, NSA_DV), (CMP_BLOCK * NSA_DV) ** -0.5),
        "cmpv_w2": nrm((L, NSA_DV, NSA_DV), NSA_DV ** -0.5),
        "cmpv_pe": nrm((L, CMP_BLOCK, NSA_DV), 0.5),
        "mla_q_norm": 1.0 + nrm((L, MLA_Q_RANK), 0.02),
        "mla_w_uq": nrm((L, MLA_Q_RANK, MLA_HEADS * (MLA_NOPE + MLA_ROPE)), MLA_Q_RANK ** -0.5),
        "mla_kv_norm": 1.0 + nrm((L, MLA_KV_RANK), 0.02),
        "mla_w_uk": nrm((L, MLA_KV_RANK, MLA_HEADS * MLA_NOPE), MLA_KV_RANK ** -0.5),
        "mla_w_uv": nrm((L, MLA_KV_RANK, MLA_HEADS * MLA_V), MLA_KV_RANK ** -0.5),
        "w_branch_a": nrm((L, NSA_HEADS * NSA_DV, D), (NSA_HEADS * NSA_DV) ** -0.5),
        "w_branch_b": nrm((L, MLA_HEADS * MLA_V, D), (MLA_HEADS * MLA_V) ** -0.5),
        "w_out": nrm((L, D, D), D ** -0.5),
        "final_norm": 1.0 + nrm((D,), 0.02),
    }

def first_block(x, c, w_ada, b_ada, ffn1_gate, ffn1_up, ffn1_down, ffn2_gate, ffn2_up, ffn2_down,
              w_in, cmpk_w1, cmpk_w2, cmpk_pe, cmpv_w1, cmpv_w2, cmpv_pe,
              mla_q_norm, mla_w_uq, mla_kv_norm, mla_w_uk, mla_w_uv,
              w_branch_a, w_branch_b, w_out, final_norm):
    S = x.shape[1]
    half = MLA_ROPE // 2
    inv_freq = ROPE_THETA ** (-jnp.arange(half, dtype=jnp.float32) / half)
    ang = jnp.arange(S, dtype=jnp.float32)[:, None] * inv_freq[None, :]
    cos, sin = jnp.cos(ang).astype(x.dtype), jnp.sin(ang).astype(x.dtype)
    c_act = jax.nn.silu(c)
    for l in range(DEPTH):
        mod = c_act @ w_ada[l] + b_ada[l]
        sh1, sc1, g1, sh2, sc2, g2, sh3, sc3, g3 = jnp.split(mod, N_MOD, axis=-1)
        x = x + 0.5 * g1[:, None, :] * swiglu(modulate(x, sh1, sc1), ffn1_gate[l], ffn1_up[l], ffn1_down[l])
        x = x + g2[:, None, :] * token_mix(
            modulate(x, sh2, sc2), cos, sin, w_in[l],
            cmpk_w1[l], cmpk_w2[l], cmpk_pe[l], cmpv_w1[l], cmpv_w2[l], cmpv_pe[l],
            mla_q_norm[l], mla_w_uq[l], mla_kv_norm[l], mla_w_uk[l], mla_w_uv[l],
            w_branch_a[l], w_branch_b[l], w_out[l])
        x = x + 0.5 * g3[:, None, :] * swiglu(modulate(x, sh3, sc3), ffn2_gate[l], ffn2_up[l], ffn2_down[l])
    return rms_norm(x) * final_norm


DEPTH_2 = 1

CONV_WIDTH = 512
CONV_K = 3
N_HEADS = 8
HEAD_DIM = 64
ATTN_WIDTH = N_HEADS * HEAD_DIM
N_GROUPS = 4
EXPERTS_PER_GROUP = 8
N_EXPERTS = N_GROUPS * EXPERTS_PER_GROUP
TOP_K_IN_GROUP = 2
D_EXPERT = 256
EPS = 1e-6
IN_COLS = 3 * CONV_WIDTH + 3 * ATTN_WIDTH + N_HEADS + 2 * D_MODEL


def rmsnorm(x, w):
    xf = x.astype(jnp.float32)
    y = xf * lax.rsqrt(jnp.mean(xf * xf, axis=-1, keepdims=True) + EPS)
    return (y * w.astype(jnp.float32)).astype(x.dtype)

def modulate_2(x, norm_w, shift, scale):
    return rmsnorm(x, norm_w) * (1 + scale[:, None, :]) + shift[:, None, :]

def causal_depthwise_conv(u, w):
    S = u.shape[1]
    up = jnp.pad(u, ((0, 0), (CONV_K - 1, 0), (0, 0)))
    out = w[0] * up[:, 0:S]
    for j in range(1, CONV_K):
        out = out + w[j] * up[:, j:j + S]
    return out

def forgetting_attention(q, k, v, log_f):
    B, H, S, Dh = q.shape
    nblk = S // Q_BLOCK
    F = jnp.cumsum(log_f, axis=-1)
    scale = HEAD_DIM ** -0.5
    k_pos = jnp.arange(S)
    q_blocks = q.reshape(B, H, nblk, Q_BLOCK, Dh).transpose(2, 0, 1, 3, 4)
    F_blocks = F.reshape(B, H, nblk, Q_BLOCK).transpose(2, 0, 1, 3)

    def one_block(args):
        i, q_i, F_i = args
        s = jnp.einsum('bhqd,bhkd->bhqk', q_i, k,
                       preferred_element_type=jnp.float32) * scale
        s = s + (F_i[..., :, None] - F[..., None, :])
        q_pos = i * Q_BLOCK + jnp.arange(Q_BLOCK)
        s = jnp.where(k_pos[None, :] <= q_pos[:, None], s, -jnp.inf)
        p = jax.nn.softmax(s, axis=-1)
        return jnp.einsum('bhqk,bhkd->bhqd', p.astype(v.dtype), v)

    o = lax.map(one_block, (jnp.arange(nblk), q_blocks, F_blocks))
    return o.transpose(1, 0, 3, 2, 4).reshape(B, S, H * Dh)

def hierarchical_moe(h, w_rg, b_rg, w_re, b_re, w_gate, w_up, w_down):
    B, S, _ = h.shape
    lg = (h @ w_rg).astype(jnp.float32) + b_rg.astype(jnp.float32)
    p_g = jax.nn.softmax(lg, axis=-1)
    g_idx = jnp.argmax(lg, axis=-1)
    p_sel = jnp.take_along_axis(p_g, g_idx[..., None], axis=-1)
    le = ((h @ w_re).astype(jnp.float32) + b_re.astype(jnp.float32)
          ).reshape(B, S, N_GROUPS, EXPERTS_PER_GROUP)
    le_g = jnp.take_along_axis(le, g_idx[..., None, None], axis=2)[:, :, 0]
    top_v, top_i = lax.top_k(le_g, TOP_K_IN_GROUP)
    w_k = jax.nn.softmax(top_v, axis=-1) * p_sel
    e_idx = g_idx[..., None] * EXPERTS_PER_GROUP + top_i
    comb = jnp.sum(jax.nn.one_hot(e_idx, N_EXPERTS, dtype=jnp.float32)
                   * w_k[..., None], axis=-2).astype(h.dtype)
    out = jnp.zeros_like(h)
    for e in range(N_EXPERTS):
        a = jax.nn.silu(h @ w_gate[e]) * (h @ w_up[e])
        out = out + comb[..., e:e + 1] * (a @ w_down[e])
    return out

def hybrid_layer(x, c, w_ada, b_ada, norm1_w, w_in, b_forget, conv_w,
                 q_norm_w, k_norm_w, w_out_conv, w_out_attn, w_o, norm2_w,
                 w_router_group, b_router_group, w_router_expert, b_router_expert,
                 w_gate, w_up, w_down):
    B, S, _ = x.shape
    mod = jax.nn.silu(c) @ w_ada + b_ada
    shift1, scale1, gate1, shift2, scale2, gate2 = jnp.split(mod, 6, axis=-1)

    h = modulate_2(x, norm1_w, shift1, scale1)
    proj = h @ w_in
    sizes = [CONV_WIDTH, CONV_WIDTH, CONV_WIDTH, ATTN_WIDTH, ATTN_WIDTH,
             ATTN_WIDTH, N_HEADS, D_MODEL]
    cuts = [int(v) for v in np.cumsum(sizes)]
    x_in, conv_b, conv_c, q, k, v, f_logit, gate_conv_l, gate_attn_l = jnp.split(
        proj, cuts, axis=-1)

    y_a = conv_b * causal_depthwise_conv(conv_c * x_in, conv_w)
    p_a = y_a @ w_out_conv

    q = rmsnorm(q.reshape(B, S, N_HEADS, HEAD_DIM), q_norm_w).transpose(0, 2, 1, 3)
    k = rmsnorm(k.reshape(B, S, N_HEADS, HEAD_DIM), k_norm_w).transpose(0, 2, 1, 3)
    v = v.reshape(B, S, N_HEADS, HEAD_DIM).transpose(0, 2, 1, 3)
    log_f = jax.nn.log_sigmoid((f_logit + b_forget).astype(jnp.float32)).transpose(0, 2, 1)
    y_b = forgetting_attention(q, k, v, log_f)
    p_b = y_b @ w_out_attn

    merged = jax.nn.sigmoid(gate_conv_l) * p_a + jax.nn.sigmoid(gate_attn_l) * p_b
    x = x + gate1[:, None, :] * (merged @ w_o)

    h2 = modulate_2(x, norm2_w, shift2, scale2)
    moe = hierarchical_moe(h2, w_router_group, b_router_group, w_router_expert,
                           b_router_expert, w_gate, w_up, w_down)
    return x + gate2[:, None, :] * moe

def second_inputs(seed: int = 0) -> dict:
    key = jax.random.key(seed)
    ks = jax.random.split(key, 22)
    f32 = jnp.float32
    L = DEPTH_2

    def nrm(k, shape, scale):
        return jax.random.normal(k, shape, f32) * scale

    return {
        "x": nrm(ks[0], (BATCH, SEQ, D_MODEL), 1.0),
        "c": nrm(ks[1], (BATCH, D_MODEL), 1.0),
        "w_ada": nrm(ks[2], (L, D_MODEL, 6 * D_MODEL), 0.5 * D_MODEL ** -0.5),
        "b_ada": nrm(ks[3], (L, 6 * D_MODEL), 0.02),
        "norm1_w": 1.0 + nrm(ks[4], (L, D_MODEL), 0.02),
        "w_in": nrm(ks[5], (L, D_MODEL, IN_COLS), D_MODEL ** -0.5),
        "b_forget": 4.0 + nrm(ks[6], (L, N_HEADS), 0.5),
        "conv_w": nrm(ks[7], (L, CONV_K, CONV_WIDTH), CONV_K ** -0.5),
        "q_norm_w": 1.0 + nrm(ks[8], (L, HEAD_DIM), 0.02),
        "k_norm_w": 1.0 + nrm(ks[9], (L, HEAD_DIM), 0.02),
        "w_out_conv": nrm(ks[10], (L, CONV_WIDTH, D_MODEL), CONV_WIDTH ** -0.5),
        "w_out_attn": nrm(ks[11], (L, ATTN_WIDTH, D_MODEL), ATTN_WIDTH ** -0.5),
        "w_o": nrm(ks[12], (L, D_MODEL, D_MODEL), D_MODEL ** -0.5),
        "norm2_w": 1.0 + nrm(ks[13], (L, D_MODEL), 0.02),
        "w_router_group": nrm(ks[14], (L, D_MODEL, N_GROUPS), D_MODEL ** -0.5),
        "b_router_group": nrm(ks[15], (L, N_GROUPS), 0.01),
        "w_router_expert": nrm(ks[16], (L, D_MODEL, N_EXPERTS), D_MODEL ** -0.5),
        "b_router_expert": nrm(ks[17], (L, N_EXPERTS), 0.01),
        "w_gate": nrm(ks[18], (L, N_EXPERTS, D_MODEL, D_EXPERT), D_MODEL ** -0.5),
        "w_up": nrm(ks[19], (L, N_EXPERTS, D_MODEL, D_EXPERT), D_MODEL ** -0.5),
        "w_down": nrm(ks[20], (L, N_EXPERTS, D_EXPERT, D_MODEL), D_EXPERT ** -0.5),
    }

def second_block(x, c, w_ada, b_ada, norm1_w, w_in, b_forget, conv_w, q_norm_w,
              k_norm_w, w_out_conv, w_out_attn, w_o, norm2_w, w_router_group,
              b_router_group, w_router_expert, b_router_expert, w_gate, w_up,
              w_down):
    for l in range(DEPTH_2):
        x = hybrid_layer(x, c, w_ada[l], b_ada[l], norm1_w[l], w_in[l], b_forget[l],
                         conv_w[l], q_norm_w[l], k_norm_w[l], w_out_conv[l],
                         w_out_attn[l], w_o[l], norm2_w[l], w_router_group[l],
                         b_router_group[l], w_router_expert[l], b_router_expert[l],
                         w_gate[l], w_up[l], w_down[l])
    return x


def setup_inputs(seed=0):
    out = dict(first_inputs(seed))
    for name, value in second_inputs(seed + 1).items():
        if name != "x":
            out[name + "_2"] = value
    return out


def reference(
    x, c, w_ada, b_ada, ffn1_gate, ffn1_up, ffn1_down, ffn2_gate, ffn2_up, ffn2_down, w_in,
    cmpk_w1, cmpk_w2, cmpk_pe, cmpv_w1, cmpv_w2, cmpv_pe, mla_q_norm, mla_w_uq, mla_kv_norm,
    mla_w_uk, mla_w_uv, w_branch_a, w_branch_b, w_out, final_norm, c_2, w_ada_2, b_ada_2,
    norm1_w_2, w_in_2, b_forget_2, conv_w_2, q_norm_w_2, k_norm_w_2, w_out_conv_2, w_out_attn_2,
    w_o_2, norm2_w_2, w_router_group_2, b_router_group_2, w_router_expert_2, b_router_expert_2,
    w_gate_2, w_up_2, w_down_2,
):
    x = first_block(
        x, c, w_ada, b_ada, ffn1_gate, ffn1_up, ffn1_down, ffn2_gate, ffn2_up, ffn2_down, w_in,
        cmpk_w1, cmpk_w2, cmpk_pe, cmpv_w1, cmpv_w2, cmpv_pe, mla_q_norm, mla_w_uq, mla_kv_norm,
        mla_w_uk, mla_w_uv, w_branch_a, w_branch_b, w_out, final_norm,
    )
    return second_block(
        x, c_2, w_ada_2, b_ada_2, norm1_w_2, w_in_2, b_forget_2, conv_w_2, q_norm_w_2,
        k_norm_w_2, w_out_conv_2, w_out_attn_2, w_o_2, norm2_w_2, w_router_group_2,
        b_router_group_2, w_router_expert_2, b_router_expert_2, w_gate_2, w_up_2, w_down_2,
    )


_drawn_inputs = setup_inputs


def setup_inputs(seed=0):
    import zlib

    import numpy as np

    out = dict(_drawn_inputs(seed))
    spreads = {}
    factors = {'cmpk_pe': 4.185,
     'mla_q_norm': 8.0,
     'mla_kv_norm': 8.0,
     'norm1_w_2': 5.949,
     'b_forget_2': 35.576,
     'q_norm_w_2': 56.18,
     'k_norm_w_2': 54.486,
     'norm2_w_2': 26.826,
     'b_router_group_2': 39.31,
     'b_router_expert_2': 52.04}
    for name, (base, spread) in spreads.items():
        noise = np.random.default_rng([zlib.crc32(name.encode()), seed]).standard_normal(out[name].shape)
        drawn = base * np.exp(spread * noise) if base else spread * noise
        out[name] = __import__('jax').numpy.asarray(drawn.astype(out[name].dtype))
    for name, factor in factors.items():
        out[name] = (out[name] * factor).astype(out[name].dtype)
    return out
```

```python
import numpy as np
from contextlib import ExitStack

import concourse.bass as bass
from concourse import mybir

F32 = mybir.dt.float32
F32R = mybir.dt.float32r
BF16 = mybir.dt.bfloat16
ALU = mybir.AluOpType
ACT = mybir.ActivationFunctionType
AX = mybir.AxisListType

P = 128
S = 256
T = S // P
D = 1024
KD = D // P
DEPTH = 2
HEADS = 8
DH = 64
GROUPS = 2
F_UNIT = 256
D_FF = 2816
FFN_UNITS = D_FF // F_UNIT
EXPERTS = 32
EXPERT_GROUPS = 4
PER_GROUP = EXPERTS // EXPERT_GROUPS
CMP_BLOCK, CMP_STRIDE = 32, 16
N_CMP = S // CMP_STRIDE - 1
Q_RANK, KV_RANK, ROPE, NOPE = 384, 256, 32, 64
QK = NOPE + ROPE
EPS = 1e-6
MASKED = -1e30

BLK = 2048
UNIT = 3 * BLK
MIX_IN_UNITS, MERGE_UNITS = 6, 3
LAYER_UNITS = 2 * FFN_UNITS + MIX_IN_UNITS + MERGE_UNITS
HYB_IN_UNITS = 7
HYB_U0 = DEPTH * LAYER_UNITS
MOE_U0 = HYB_U0 + HYB_IN_UNITS + MERGE_UNITS
ALL_UNITS = MOE_U0 + EXPERTS

ADA_COLS = 256
ADA_STEPS = 3 * D // ADA_COLS
STAGES = 3 * DEPTH + 2

C_CQ, C_CKV, C_KR, C_GN, C_KC, C_KS, C_KW, C_Q, C_V = 0, 384, 640, 672, 696, 952, 1080, 1208, 1720
PROJ = C_V
MIX_COLS = 1976
U2_COLS = MIX_COLS - 2 * 768
UQ_OFF = 3520
HYB_QKV = 1536

K_ID, K_ONE, K_DIST, K_MASK, K_CMPB, K_COS, K_SIN, K_VALID, K_TRI, K_TIE8, K_TIE4 = np.cumsum(
    [0, 128, 128, 384, 384, 256, 64, 64, 2, 256, 64]).tolist()
K_ALL = K_TIE4 + 16
V_C, V_BADA, V_N1, V_N2, V_CONV, V_QN, V_KN, V_BF, V_BR = np.cumsum(
    [0, 16, STAGES * 24, 8, 8, 12, 1, 1, 8]).tolist()
V_ALL = V_BR + 36
L_PE, L_W2, L_QN, L_KVN = 0, 64, 192, 195
L_ALL = 197

SLOPES = [2.0 ** (-8.0 * (h + 1) / HEADS) for h in range(HEADS)]
CHAIN_PER_LAYER = 64


def program(nc, stream, ada, consts, vecs, layer_vecs, cmp_w1, fnorm, x_in, out):
    ctx = ExitStack()
    with ctx:
        def sb(name, shape, dt=F32):
            return ctx.enter_context(nc.sbuf_tensor(name, shape, dt))

        def sem(name):
            return ctx.enter_context(nc.semaphore(name))

        raw = sb("raw", [P, UNIT])
        w_hi = sb("w_hi", [P, UNIT], F32R)
        w_lo = sb("w_lo", [P, UNIT], F32R)
        x = sb("x", [P, T, D])
        uT_hi = sb("uT_hi", [P, KD, S], F32R)
        uT_lo = sb("uT_lo", [P, KD, S], F32R)
        gate_bc = sb("gate_bc", [P, D])
        ada_w = sb("ada_w", [P, 2, KD, ADA_COLS])
        ada_sum = sb("ada_sum", [P, ADA_COLS])
        cst = sb("cst", [P, K_ALL])
        vec = sb("vec", [P, V_ALL])
        c_act = sb("c_act", [P, 16])
        lvec = sb("lvec", [P, L_ALL])
        modf = sb("modf", [P, 24])
        stat = sb("stat", [P, 112])
        zeros = sb("zeros", [P, 512], BF16)
        cmpw = sb("cmpw", [P, 2, 2048])
        r_arena = sb("r_arena", [P, 4096], F32R)
        arena = sb("arena", [P, 11520])

        def at(off, *shape, parts=P):
            n = int(np.prod(shape))
            v = arena[0:parts, off:off + n]
            if len(shape) == 2:
                return v.rearrange("p (a b) -> p a b", a=shape[0])
            if len(shape) == 3:
                return v.rearrange("p (a b c) -> p a b c", a=shape[0], b=shape[1])
            if len(shape) == 4:
                return v.rearrange("p (a b c d) -> p a b c d", a=shape[0], b=shape[1], c=shape[2])
            return v

        def rat(off, a, b):
            return r_arena[:, off:off + a * b].rearrange("p (a b) -> p a b", a=a)

        ident = cst[:, K_ID:K_ID + 128]
        ones = cst[:, K_ONE:K_ONE + 128]
        dist = [cst[:, K_DIST:K_DIST + 128], cst[:, K_DIST + 128:K_DIST + 384]]
        mask = [cst[:, K_MASK:K_MASK + 128], cst[:, K_MASK + 128:K_MASK + 384]]
        cmp_bias = cst[:, K_CMPB:K_CMPB + 256].rearrange("p (a q i n) -> p a q i n", a=2, q=2, i=4)
        cos2 = cst[:, K_COS:K_COS + 64].rearrange("p (t r) -> p t r", t=T)
        sin2 = cst[:, K_SIN:K_SIN + 64].rearrange("p (t r) -> p t r", t=T)
        cmp_valid = cst[:, K_VALID:K_VALID + 2]
        tri = cst[:, K_TRI:K_TRI + 256]
        tie8 = cst[:, K_TIE8:K_TIE8 + 64].rearrange("p (a b) -> p a b", a=8)
        tie4 = cst[:, K_TIE4:K_TIE4 + 16].rearrange("p (a b) -> p a b", a=4)

        ss, ms, sq, rstd = stat[:, 0:2], stat[:, 2:4], stat[:, 4:6], stat[:, 6:8]
        lss, lms, lsq, lrs = stat[:, 8:12], stat[:, 12:16], stat[:, 16:20], stat[:, 20:24]
        nmax = [stat[:, 24:28], stat[:, 28:32]]
        psum_row = [stat[:, 96 + 4 * i:100 + 4 * i] for i in range(4)]
        pad = stat[:, 32:33]
        rsum, coef = stat[:, 40:44], stat[:, 44:48]
        cmax, csum, crec, ccoef = (at(11136, 16), at(11152, 16), at(11168, 16), at(11184, 16))
        nsa_gate = stat[:, 48:96].rearrange("p (t h k) -> p t h k", t=T, h=HEADS)

        xn, uTf, diag = at(0, T, D), at(2048, KD, S), at(4096, KD, P)
        act_g, hid = at(6144, T, F_UNIT), at(6656, T, F_UNIT)
        hT_hi, hT_lo = rat(0, 2, S), rat(512, 2, S)
        upd = at(2048, T, 2, 512)
        proj = at(0, T, PROJ)
        vsw = at(4096, T, 256)
        qT = at(4608, 4, S)
        kT = [at(5632, 2, S), at(6144, 2, S)]
        cT = at(6656, 2, S)
        blocks = at(7168, 2, CMP_BLOCK, N_CMP)
        p_cmp = at(7168, 16, 32)
        pT_cmp = at(7680, 4, P)
        hid_cmp, kT_cmp, v_cmp = at(8128, 2, 16), at(8192 + 96, 2, 16), at(8192 + 128, 2, DH)
        vm = at(8448, T, HEADS * DH)
        o_a, o_b = at(9472, T, 512), at(10496, T, 512)
        o_tmp = at(10496, 4, DH)
        lat_squares = at(9472, T, Q_RANK + KV_RANK)
        q_tok, k_tok = at(0, T, HEADS, QK), at(1536, T, HEADS, QK)
        rope_a, rope_b = at(9472, T, HEADS, ROPE), at(9472 + 512, T, HEADS, ROPE)
        kr_a, kr_b = at(10496, T, ROPE), at(10560, T, ROPE)
        qkT_m = cmpw[:, :, :].rearrange("p k (h s) -> p k h s", h=HEADS)
        scores = [at(0, 2, 2, S), at(1024, 2, 2, S)]
        pT = [at(2048, 2, 4, P), at(3072, 2, 4, P)]
        gates_m = at(4096, T, 2 * D)
        y, ytmp = at(0, T, D), at(2048, T, 2, 512)
        cqT_hi, cqT_lo = rat(0, 5, S), rat(1280, 5, S)
        oT_hi = [rat(0, 4, S), rat(2048, 4, S)]
        oT_lo = [rat(1024, 4, S), rat(3072, 4, S)]
        yT_hi, yT_lo = rat(0, 8, S), rat(2048, 8, S)
        fn_bc = at(4096, D)
        xcb = at(0, T, 1536)
        qkv = at(4096, T, HYB_QKV)
        gates_h = at(7168, T, 2 * D)
        f_row = at(11264, T, 8)
        f_e, f_l, f_cum = at(11280, T, 8), at(11296, T, 8), at(11312, T, 8)
        nlogf = at(11328, T, 8)
        qk_ss, qk_gain = at(11344, 32), at(11376, 4)
        qT_h = cmpw[:, 0, 0:1024].rearrange("p (c s) -> p c s", c=4)
        kT_h = cmpw[:, 0, 1024:2048].rearrange("p (c s) -> p c s", c=4)
        u_tok = cmpw[:, 1, 0:1024].rearrange("p (t s) -> p t s", t=T)
        squares = cmpw[:, 1, 1024:2048].rearrange("p (t s) -> p t s", t=T)
        bT = cmpw[:, 1, 1024:2048].rearrange("p (c s) -> p c s", c=4)
        uTc = at(0, 4, S + 2)
        conv = at(1056, 4, S)
        o_h = qkv[:, :, 0:512]
        r0 = 8192
        logits = at(r0, T, 36)
        g_gt, g_eq = at(r0 + 128, T, 4, 4), at(r0 + 160, T, 4, 4)
        g_rank, g_sel = at(r0 + 192, T, 4), at(r0 + 200, T, 4)
        g_max, g_exp, g_sum, p_sel = at(r0 + 208, T), at(r0 + 212, T, 4), at(r0 + 220, T), at(r0 + 224, T)
        le_m, le_g = at(r0 + 256, T, 4, 8), at(r0 + 320, T, 8)
        e_gt, e_eq = at(r0 + 384, T, 8, 8), at(r0 + 512, T, 8, 8)
        e_rank, e_max, e_exp, e_sum, e_w = (at(r0 + 640, T, 8), at(r0 + 656, T), at(r0 + 660, T, 8),
                                            at(r0 + 676, T), at(r0 + 680, T, 8))
        comb = at(r0 + 704, T, EXPERTS)

        bank = [ctx.enter_context(nc.psum_tensor(f"bank{i}", [P, 512], F32)) for i in range(8)]
        ACC, GU, HT, MOD = bank[0:4], bank[4:6], bank[6], bank[7]

        landed = [sem(f"block_landed{j}") for j in range(3)]
        hi_ready = [sem(f"block_hi{j}") for j in range(3)]
        lo_ready = [sem(f"block_lo{j}") for j in range(3)]
        used = [sem(f"block_used{j}") for j in range(3)]
        x_landed, cst_landed, fn_landed = sem("x_landed"), sem("cst_landed"), sem("fn_landed")
        lvec_landed, out_landed = sem("lvec_landed"), sem("out_landed")
        ada_landed = [sem("ada_landed0"), sem("ada_landed1")]
        c_ready, ada_chain, ada_ready = sem("c_ready"), sem("ada_chain"), sem("ada_ready")
        mod_step, mod_ready = sem("mod_step"), sem("mod_ready")
        x_ready, ss_done, ms_done, sq_done = sem("x_ready"), sem("ss_done"), sem("ms_done"), sem("sq_done")
        rstd_done, xn_done = sem("rstd_done"), sem("xn_done")
        diag_done, gate_psum, gate_ready = sem("diag_done"), sem("gate_psum"), sem("gate_ready")
        uT_psum, uTf_done, uT_hi_done, uT_ready = sem("uT_psum"), sem("uTf_done"), sem("uT_hi_done"), sem("uT_ready")
        gu0_done, silu_done, h_done = sem("gu0_done"), sem("silu_done"), sem("h_done")
        hT_psum, hT_hi_done, hT_ready = sem("hT_psum"), sem("hT_hi_done"), sem("hT_ready")
        chain = sem("vector_chain")
        w_done, w_evac_a, w_evac_v = sem("w_done"), sem("w_evac_a"), sem("w_evac_v")
        lat_ss, lat_ms, lat_sq, lat_ready = sem("lat_ss"), sem("lat_ms"), sem("lat_sq"), sem("lat_ready")
        nsa_gate_ready = sem("nsa_gate_ready")
        cqT_psum, cqT_hi_done, cqT_ready = sem("cqT_psum"), sem("cqT_hi_done"), sem("cqT_ready")
        q_psum, ks_psum, kw_psum, c_psum = sem("q_psum"), sem("ks_psum"), sem("kw_psum"), sem("c_psum")
        q_ready, ks_ready, kw_ready, blocks_ready = sem("q_ready"), sem("ks_ready"), sem("kw_ready"), sem("blocks_ready")
        hidc_psum, hidc_ready, kvc_psum, kvc_ready = sem("hidc_psum"), sem("hidc_ready"), sem("kvc_psum"), sem("kvc_ready")
        uq_psum, uk_psum, uv_psum = sem("uq_psum"), sem("uk_psum"), sem("uv_psum")
        uq_copied, uk_copied, uv_ready, rope_done = sem("uq_copied"), sem("uk_copied"), sem("uv_ready"), sem("rope_done")
        qm_psum, km_psum, qm_ready, km_ready = sem("qm_psum"), sem("km_psum"), sem("qm_ready"), sem("km_ready")
        cs_psum, cs_ready, cp_exp, cp_psum, cp_ready, co_psum, co_done = (
            sem("cs_psum"), sem("cs_ready"), sem("cp_exp"), sem("cp_psum"), sem("cp_ready"), sem("co_psum"), sem("co_done"))
        sc_done, bias_done, nmax_done, exp_done = sem("sc_done"), sem("bias_done"), sem("nmax_done"), sem("exp_done")
        pt_psum, pt_copied_a, pt_copied_v, pv_done, o_done = (
            sem("pt_psum"), sem("pt_copied_a"), sem("pt_copied_v"), sem("pv_done"), sem("o_done"))
        oT_psum, oT_hi_done, oT_ready = sem("oT_psum"), sem("oT_hi_done"), sem("oT_ready")
        pa_psum, ya_done, pb_psum, y_ready = sem("pa_psum"), sem("ya_done"), sem("pb_psum"), sem("y_ready")
        yT_psum, yT_hi_done, yT_ready = sem("yT_psum"), sem("yT_hi_done"), sem("yT_ready")
        u_ready, uc_psum, uc_ready, b_psum, ya_f32, ya_hi_done = (
            sem("u_ready"), sem("uc_psum"), sem("uc_ready"), sem("b_psum"), sem("ya_f32"), sem("ya_hi_done"))
        f_exp, f_exp_in, f_ln, f_ln_in, logf_ready, fcum_psum, fcum_ready = (
            sem("f_exp"), sem("f_exp_in"), sem("f_ln"), sem("f_ln_in"), sem("logf_ready"), sem("fcum_psum"), sem("fcum_ready"))
        qkn_ms, qkn_sq, qkn_ready, kh_psum, kh_ready = (
            sem("qkn_ms"), sem("qkn_sq"), sem("qkn_ready"), sem("kh_psum"), sem("kh_ready"))
        r_psum, r_exp_in, r_exp, comb_ready = sem("r_psum"), sem("r_exp_in"), sem("r_exp"), sem("comb_ready")
        first_ready = sem("first_ready")

        NSA_JOBS = [(k, qt, g) for k in (0, 1) for qt in (1, 0) for g in (0, 1)]
        MLA_JOBS = [(2, qt, g) for qt in (1, 0) for g in (0, 1)]
        JOBS = NSA_JOBS + MLA_JOBS
        HYB_JOBS = [(3, qt, g) for qt in (1, 0) for g in (0, 1)]
        NJ = len(JOBS)

        def f32(ap):
            return ap.bitcast(F32)

        block = ctx.enter_context(nc.Block())

        @block.sync
        def _(sp):
            sp.dma_start(cst[:, :], consts).then_inc(cst_landed, 16)
            sp.dma_start(vec[:, :], vecs).then_inc(cst_landed, 16)
            sp.dma_start(x[:, :, :], x_in.rearrange("(t p) d -> p t d", p=P)).then_inc(x_landed, 16)
            for j in range(3):
                sp.dma_start(raw[:, j * BLK:(j + 1) * BLK], stream[0, j]).then_inc(landed[j], 16)
            with sp.Fori(1, ALL_UNITS) as u:
                for j in range(3):
                    sp.wait_ge(lo_ready[j], u)
                    sp.dma_start(raw[:, j * BLK:(j + 1) * BLK], stream[u, j]).then_inc(landed[j], 16)
            sp.wait_ge(x_ready, 2 * (3 * DEPTH + 4))
            sp.dma_start(out.rearrange("(t p) d -> p t d", p=P), x[:, :, :]).then_inc(out_landed, 16)
            sp.wait_ge(out_landed, 16)

        @block.gpsimd
        def _(pool):
            def load(n, slot):
                pool.dma_start(ada_w[:, slot], ada[n]).then_inc(ada_landed[slot], 16)

            def step(pair, slot, c0, ahead):
                n = pair * 2 + slot
                w = ada_w[:, slot]
                pool.wait_ge(ada_landed[slot], pair * 16 + 16)
                nc.gpsimd.tensor_tensor(w, w, c_act[:, c0:c0 + 8].unsqueeze(2).to_broadcast([P, KD, ADA_COLS]),
                                        ALU.mult).then_inc(ada_chain, 1)
                pool.wait_ge(ada_chain, n * 3 + 1)
                nc.gpsimd.tensor_tensor(w[:, 0:4], w[:, 0:4], w[:, 4:8], ALU.add).then_inc(ada_chain, 1)
                pool.wait_ge(ada_chain, n * 3 + 2)
                nc.gpsimd.tensor_tensor(w[:, 0:2], w[:, 0:2], w[:, 2:4], ALU.add).then_inc(ada_chain, 1)
                pool.wait_ge(ada_chain, n * 3 + 3)
                pool.wait_ge(mod_step, n + 1)
                nc.gpsimd.tensor_tensor(ada_sum[:, :], w[:, 0], w[:, 1], ALU.add).then_inc(ada_ready, 1)
                if ahead:
                    pool.wait_ge(ada_ready, n + 1)
                    load(n + 2, slot)

            load(0, 0)
            load(1, 1)
            pool.wait_ge(c_ready, 1)
            c2_pair, end_pair = DEPTH * 3 * ADA_STEPS // 2, STAGES * ADA_STEPS // 2
            with pool.Fori(0, c2_pair) as pair:
                for slot in range(2):
                    step(pair, slot, 0, True)
            with pool.Fori(c2_pair, end_pair - 1) as pair:
                for slot in range(2):
                    step(pair, slot, 8, True)
            for slot in range(2):
                step(end_pair - 1, slot, 8, False)

        @block.scalar
        def _(act):
            def split(u, js):
                for j in js:
                    act.wait_ge(landed[j], 16 * u + 16)
                    act.wait_ge(used[j], u + 1)
                    act.activation(w_hi[:, j * BLK:(j + 1) * BLK], raw[:, j * BLK:(j + 1) * BLK],
                                   ACT.Copy).then_inc(hi_ready[j], 1)

            def rms_squares(q):
                for t in range(T):
                    act.wait_ge(x_ready, 2 * q + t + 1)
                    act.activation(xn[:, t], x[:, t], ACT.Square, accum_out=ss[:, t:t + 1]).then_inc(ss_done, 1)
                act.wait_ge(ms_done, q + 1)
                act.activation(sq, ms, ACT.Sqrt).then_inc(sq_done, 1)

            def norm(q, n):
                rms_squares(q)
                act.wait_ge(gate_psum, 2 * n + 1)
                act.activation(gate_bc[:, 0:512], HT[:, :], ACT.Copy).then_inc(gate_ready, 1)
                act.wait_ge(gate_psum, 2 * n + 2)
                act.activation(gate_bc[:, 512:1024], GU[1][:, :], ACT.Copy).then_inc(gate_ready, 1)
                for b in range(4):
                    act.wait_ge(uTf_done, 4 * n + b + 1)
                    act.activation(uT_hi[:, 2 * b:2 * b + 2], uTf[:, 2 * b:2 * b + 2], ACT.Copy).then_inc(uT_hi_done, 1)

            def silu(u, f):
                act.wait_ge(gu0_done, f + 1)
                act.activation(act_g[:, 0], GU[0][:, 0:F_UNIT], ACT.Silu).then_inc(silu_done, 1)
                act.wait_ge(used[1], u + 2)
                act.activation(act_g[:, 1], GU[1][:, 0:F_UNIT], ACT.Silu).then_inc(silu_done, 1)

            def h_split(f):
                act.wait_ge(hT_psum, f + 1)
                act.activation(hT_hi[:, :, :], HT[:, :].rearrange("p (f s) -> p f s", f=2), ACT.Copy).then_inc(hT_hi_done, 1)

            def ffn(u0, f0, n, more):
                split(u0 + 1, (0, 1))
                silu(u0, f0)
                split(u0, (2,))
                with act.Fori(1, n if more else n - 1) as i:
                    h_split(f0 + i - 1)
                    split(u0 + i + 1, (0, 1))
                    silu(u0 + i, f0 + i)
                    split(u0 + i, (2,))
                if not more:
                    h_split(f0 + n - 2)
                    silu(u0 + n - 1, f0 + n - 1)
                    split(u0 + n - 1, (2,))
                h_split(f0 + n - 1)

            def merge(u0, m, gates):
                split(u0, (2,))
                split(u0 + 1, (0,))
                split(u0 + 1, (1, 2))
                split(u0 + 2, (0,))
                for b in range(4):
                    act.wait_ge(yT_psum, 4 * m + b + 1)
                    act.activation(yT_hi[:, 2 * b:2 * b + 2], bank[4 + b if b < 3 else 0][:, :].rearrange("p (k s) -> p k s", k=2),
                                   ACT.Copy).then_inc(yT_hi_done, 1)
                split(u0 + 2, (1,))
                split(u0 + 2, (2,))
                split(u0 + 3, (0, 1))

            def job_exp(j0, jobs, j):
                kind, qt, g = jobs[j]
                nk = (qt + 1) * P
                sc = scores[j % 2]
                act.wait_ge(nmax_done, j0 + j + 1)
                for h in range(4):
                    v = sc[:, h // 2, h % 2, 0:nk]
                    e = act.activation(v, v, ACT.Exp, bias=nmax[j % 2][:, h:h + 1], accum_out=psum_row[j % 4][:, h:h + 1])
                e.then_inc(exp_done, 1)

            def jobs_run(j0, jobs):
                job_exp(j0, jobs, 0)
                job_exp(j0, jobs, 1)
                for j, (kind, qt, g) in enumerate(jobs):
                    act.wait_ge(pt_psum, j0 + j + 1)
                    if j >= 2:
                        act.wait_ge(pv_done, j0 + j - 1)
                    act.activation(pT[j % 2][:, 0], bank[4][:, :].rearrange("p (h q) -> p h q", h=4), ACT.Copy).then_inc(pt_copied_a, 1)
                    if j + 2 < len(jobs):
                        job_exp(j0, jobs, j + 2)

            act.wait_ge(cst_landed, 32)
            act.activation(c_act[:, :], vec[:, V_C:V_C + 16], ACT.Silu).then_inc(c_ready, 1)
            for j in range(2):
                act.wait_ge(landed[j], 16)
                act.activation(w_hi[:, j * BLK:(j + 1) * BLK], raw[:, j * BLK:(j + 1) * BLK], ACT.Copy).then_inc(hi_ready[j], 1)

            with act.Fori(0, DEPTH) as l:
                u_mix = l * LAYER_UNITS + FFN_UNITS
                act.wait_ge(x_ready, l * 6 + 2)
                act.dma_start(lvec[:, :], layer_vecs[l]).then_inc(lvec_landed, 16)
                act.dma_start(cmpw[:, :, :], cmp_w1[l].rearrange("p (k w) -> p k w", k=2)).then_inc(lvec_landed, 16)
                norm(l * 3, l * 3)
                ffn(l * LAYER_UNITS, l * 2 * FFN_UNITS, FFN_UNITS, True)

                norm(l * 3 + 1, l * 3 + 1)
                split(u_mix, (2,))
                split(u_mix + 1, (0, 1))
                act.wait_ge(w_done, l * 6 + 1)
                act.activation(proj[:, 0, 0:512], bank[0][:, :], ACT.Copy).then_inc(w_evac_a, 1)
                act.activation(proj[:, :, 512:768], bank[2][:, :].rearrange("p (t c) -> p t c", t=T), ACT.Copy).then_inc(w_evac_a, 1)
                split(u_mix + 1, (2,))
                act.wait_ge(w_evac_a, l * 8 + 2)
                act.wait_ge(w_evac_v, l * 3 + 1)
                for t in range(T):
                    act.activation(lat_squares[:, t, 0:Q_RANK], proj[:, t, C_CQ:C_CKV], ACT.Square, accum_out=lss[:, t:t + 1]).then_inc(lat_ss, 1)
                    act.activation(lat_squares[:, t, Q_RANK:], proj[:, t, C_CKV:C_KR], ACT.Square, accum_out=lss[:, 2 + t:3 + t]).then_inc(lat_ss, 1)
                act.wait_ge(lat_ms, l + 1)
                act.activation(lsq, lms, ACT.Sqrt).then_inc(lat_sq, 1)
                act.activation(nsa_gate.rearrange("p t h k -> p t (h k)"), proj[:, :, C_GN:C_KC], ACT.Sigmoid).then_inc(nsa_gate_ready, 1)
                split(u_mix + 2, (0, 1))
                act.wait_ge(w_done, l * 6 + 2)
                act.activation(proj[:, 0, 768:1280], bank[3][:, :], ACT.Copy).then_inc(w_evac_a, 1)
                act.activation(proj[:, :, 1280:1536], bank[5][:, :].rearrange("p (t c) -> p t c", t=T), ACT.Copy).then_inc(w_evac_a, 1)
                split(u_mix + 2, (2,))
                act.wait_ge(w_done, l * 6 + 3)
                act.activation(proj[:, 0, 1536:PROJ], bank[0][:, 0:184], ACT.Copy)
                act.activation(vsw[:, 0], bank[0][:, 184:440], ACT.Copy).then_inc(w_evac_a, 1)
                act.wait_ge(lvec_landed, l * 32 + 32)
                for b, cs in enumerate(((0, 1), (2, 3), (4,))):
                    act.wait_ge(cqT_psum, l * 3 + b + 1)
                    for i, c in enumerate(cs):
                        e = act.activation(cqT_hi[:, c], bank[2 + b][:, i * S:(i + 1) * S], ACT.Copy,
                                           scale=lvec[:, L_QN + c:L_QN + c + 1])
                    e.then_inc(cqT_hi_done, 1)
                for b in range(2):
                    act.wait_ge(q_psum, l * 2 + b + 1)
                    act.activation(qT[:, 2 * b:2 * b + 2], bank[5 + b][:, :].rearrange("p (c s) -> p c s", c=2), ACT.Copy,
                                   scale=DH ** -0.5).then_inc(q_ready, 1)
                act.wait_ge(ks_psum, l + 1)
                act.activation(kT[0][:, :, :], bank[0][:, :].rearrange("p (g s) -> p g s", g=2), ACT.Copy).then_inc(ks_ready, 1)
                act.wait_ge(hidc_psum, l + 1)
                for g in range(GROUPS):
                    rows = slice(DH * g, DH * g + DH)
                    e = act.activation(hid_cmp[rows, :, 0:N_CMP],
                                       bank[3 - g][rows, 0:32].rearrange("p (k n) -> p k n", k=2)[:, :, 0:N_CMP], ACT.Gelu_apprx_tanh)
                e.then_inc(hidc_ready, 1)
                split(u_mix + 3, (0,))
                for b in range(4):
                    act.wait_ge(uq_psum, l * 4 + b + 1)
                    act.activation(q_tok[:, b // 2, 4 * (b % 2):4 * (b % 2) + 4].rearrange("p h c -> p (h c)"), bank[b][:, 0:384],
                                   ACT.Copy).then_inc(uq_copied, 1)
                for b in range(4):
                    act.wait_ge(qm_psum, l * 4 + b + 1)
                    act.activation(qkT_m[0:QK, 0, 2 * b:2 * b + 2], bank[b][0:QK, :].rearrange("p (h s) -> p h s", h=2),
                                   ACT.Copy).then_inc(qm_ready, 1)
                act.wait_ge(cs_ready, l + 1)
                act.activation(p_cmp[:, :, 0:N_CMP], p_cmp[:, :, 0:N_CMP], ACT.Exp).then_inc(cp_exp, 1)
                act.wait_ge(cp_psum, l + 1)
                act.activation(pT_cmp[:, :, :], bank[2][:, :].rearrange("p (a q) -> p a q", a=4), ACT.Copy).then_inc(cp_ready, 1)
                jobs_run(l * NJ, JOBS)
                split(u_mix + 3, (1, 2))
                act.wait_ge(w_done, l * 6 + 4)
                act.activation(gates_m[:, 0, 0:512], bank[0][:, :], ACT.Sigmoid)
                act.activation(gates_m[:, 1, 0:512], bank[1][:, :], ACT.Sigmoid).then_inc(w_evac_a, 1)
                for m in (4, 5):
                    split(u_mix + m, (0, 1, 2))
                    b0, c0 = (3, 512) if m == 4 else (0, 1280)
                    act.wait_ge(w_done, l * 6 + m + 1)
                    for t in range(T):
                        act.activation(gates_m[:, t, c0:c0 + 512], bank[b0 + t][:, :], ACT.Sigmoid)
                    act.activation(gates_m[:, :, c0 + 512:c0 + 768], bank[b0 + 2][:, :].rearrange("p (t c) -> p t c", t=T),
                                   ACT.Sigmoid).then_inc(w_evac_a, 1)
                split(u_mix + 6, (0, 1))
                for b in range(4):
                    act.wait_ge(oT_psum, l * 4 + b + 1)
                    act.activation(oT_hi[b // 2][:, 2 * (b % 2):2 * (b % 2) + 2], bank[3 + b][:, :].rearrange("p (c s) -> p c s", c=2),
                                   ACT.Copy).then_inc(oT_hi_done, 1)
                merge(u_mix + MIX_IN_UNITS, l, None)

                norm(l * 3 + 2, l * 3 + 2)
                ffn(l * LAYER_UNITS + FFN_UNITS + MIX_IN_UNITS + MERGE_UNITS, l * 2 * FFN_UNITS + FFN_UNITS, FFN_UNITS, True)

            q6, n6 = 3 * DEPTH, 3 * DEPTH
            act.wait_ge(x_ready, 2 * q6 + 2)
            act.dma_start(fn_bc, fnorm).then_inc(fn_landed, 16)
            rms_squares(q6)
            norm(q6 + 1, n6)
            u = HYB_U0
            split(u, (2,))
            for m in range(HYB_IN_UNITS):
                if m + 1 < HYB_IN_UNITS:
                    split(u + m + 1, (0, 1))
                act.wait_ge(w_done, DEPTH * 6 + m + 1)
                b0, n2 = 3 * (m % 2), 256 if m < 6 else 8
                if m < 4:
                    dst, c0 = (xcb, 768 * m) if m < 2 else (qkv, 768 * (m - 2))
                    act.activation(dst[:, 0, c0:c0 + 512], bank[b0][:, :], ACT.Copy).then_inc(w_evac_a, 1)
                    act.activation(dst[:, :, c0 + 512:c0 + 768], bank[b0 + 2][:, :].rearrange("p (t c) -> p t c", t=T),
                                   ACT.Copy).then_inc(w_evac_a, 1)
                elif m == 4:
                    for t in range(T):
                        act.activation(f_row[:, t], bank[b0 + t][:, 0:8], ACT.Copy)
                        act.activation(gates_h[:, t, 0:504], bank[b0 + t][:, 8:512], ACT.Sigmoid)
                    act.activation(gates_h[:, :, 504:760], bank[b0 + 2][:, :].rearrange("p (t c) -> p t c", t=T),
                                   ACT.Sigmoid).then_inc(w_evac_a, 1)
                else:
                    c0 = 760 + 768 * (m - 5)
                    for t in range(T):
                        act.activation(gates_h[:, t, c0:c0 + 512], bank[b0 + t][:, :], ACT.Sigmoid)
                    act.activation(gates_h[:, :, c0 + 512:c0 + 512 + n2],
                                   bank[b0 + 2][:, 0:2 * n2].rearrange("p (t c) -> p t c", t=T), ACT.Sigmoid).then_inc(w_evac_a, 1)
                if m + 1 < HYB_IN_UNITS:
                    split(u + m + 1, (2,))
            act.wait_ge(qkn_ms, 1)
            act.activation(qk_ss, qk_ss, ACT.Sqrt).then_inc(qkn_sq, 1)
            act.wait_ge(f_exp_in, 1)
            act.activation(f_e[:, :, :], f_e[:, :, :], ACT.Exp).then_inc(f_exp, 1)
            act.wait_ge(f_ln_in, 1)
            act.activation(f_l[:, :, :], f_l[:, :, :], ACT.Ln).then_inc(f_ln, 1)
            for b in range(2):
                act.wait_ge(ya_f32, b + 1)
                act.activation(oT_hi[0][:, 2 * b:2 * b + 2], conv[:, 2 * b:2 * b + 2], ACT.Copy).then_inc(ya_hi_done, 1)
            for b in range(2):
                act.wait_ge(q_psum, DEPTH * 2 + b + 1)
                act.activation(qT_h[:, 2 * b:2 * b + 2], bank[b][:, :].rearrange("p (c s) -> p c s", c=2), ACT.Copy,
                               scale=qk_gain[:, 0:1]).then_inc(q_ready, 1)
            for b in range(2):
                act.wait_ge(kh_psum, b + 1)
                act.activation(kT_h[:, 2 * b:2 * b + 2], bank[2 + 2 * b][:, :].rearrange("p (c s) -> p c s", c=2), ACT.Copy,
                               scale=vec[:, V_KN:V_KN + 1]).then_inc(kh_ready, 1)
            jobs_run(DEPTH * NJ, HYB_JOBS)
            um = u + HYB_IN_UNITS
            split(um, (0, 1))
            for b in range(2):
                act.wait_ge(oT_psum, DEPTH * 4 + b + 1)
                act.activation(oT_hi[1][:, 2 * b:2 * b + 2], bank[5 + b][:, :].rearrange("p (c s) -> p c s", c=2),
                               ACT.Copy).then_inc(oT_hi_done, 1)
            merge(um, DEPTH, None)
            norm(q6 + 2, n6 + 1)
            act.wait_ge(r_exp_in, 1)
            act.activation(g_exp[:, :, :], g_exp[:, :, :], ACT.Exp)
            act.activation(e_exp[:, :, :], e_exp[:, :, :], ACT.Exp).then_inc(r_exp, 1)
            ffn(MOE_U0, DEPTH * 2 * FFN_UNITS, EXPERTS, False)

        @block.vector
        def _(dve):
            V = nc.vector
            links = [0, 0]

            def link(ins, layer=None):
                links[0] += 1
                ins.then_inc(chain, 1)
                dve.wait_ge(chain, links[1] + links[0])

            def split(u, js):
                for j in js:
                    b = slice(j * BLK, (j + 1) * BLK)
                    dve.wait_ge(hi_ready[j], u + 1)
                    V.tensor_tensor(w_lo[:, b], raw[:, b], f32(w_hi[:, b]), ALU.subtract).then_inc(lo_ready[j], 1)

            def rms(q):
                dve.wait_ge(ss_done, 2 * q + 2)
                V.tensor_scalar(ms, ss, 1.0 / D, EPS, ALU.mult, ALU.add).then_inc(ms_done, 1)
                dve.wait_ge(sq_done, q + 1)
                V.reciprocal(rstd, sq).then_inc(rstd_done, 1)
                dve.wait_ge(rstd_done, q + 1)

            def norm(q, n, gain=None, half=1.0):
                dve.wait_ge(mod_step, n * ADA_STEPS + ADA_STEPS + 1)
                link(V.tensor_tensor(modf[:, :], MOD[:, 0:24], vec[:, bass.ds(V_BADA + n * 24, 24)], ALU.add))
                V.tensor_scalar(modf[:, 8:16], modf[:, 8:16], 1.0, None, ALU.add).then_inc(mod_ready, 1)
                for k in range(KD):
                    d = V.tensor_scalar(diag[:, k], ident, modf[:, 16 + k:17 + k], half, ALU.mult, ALU.mult)
                d.then_inc(diag_done, 1)
                dve.wait_ge(mod_ready, n + 1)
                if gain is not None:
                    link(V.tensor_tensor(modf[:, 8:16], modf[:, 8:16], gain, ALU.mult))
                rms(q)
                for t in range(T):
                    V.tensor_scalar(xn[:, t], x[:, t], rstd[:, t:t + 1], None, ALU.mult).then_inc(xn_done, 1)
                for b in range(4):
                    dve.wait_ge(uT_psum, 4 * n + b + 1)
                    for i in range(2):
                        k = 2 * b + i
                        e = V.tensor_scalar(uTf[:, k], ACC[b][:, i * S:(i + 1) * S], modf[:, 8 + k:9 + k], modf[:, k:k + 1],
                                            ALU.mult, ALU.add)
                    e.then_inc(uTf_done, 1)
                for b in range(4):
                    dve.wait_ge(uT_hi_done, 4 * n + b + 1)
                    V.tensor_tensor(uT_lo[:, 2 * b:2 * b + 2], uTf[:, 2 * b:2 * b + 2], f32(uT_hi[:, 2 * b:2 * b + 2]),
                                    ALU.subtract).then_inc(uT_ready, 1)

            def hidden(f, weight):
                for t in range(T):
                    dve.wait_ge(silu_done, f * 2 + t + 1)
                    up = GU[t][:, F_UNIT:2 * F_UNIT]
                    if weight is None:
                        h = V.tensor_tensor(hid[:, t], act_g[:, t], up, ALU.mult)
                    else:
                        h = V.scalar_tensor_tensor(hid[:, t], act_g[:, t], comb[:, t, bass.ds(weight, 1)], up, ALU.mult, ALU.mult)
                    h.then_inc(h_done, 1)

            def h_split(f):
                dve.wait_ge(hT_hi_done, f + 1)
                V.tensor_tensor(hT_lo[:, :, :], HT[:, :].rearrange("p (f s) -> p f s", f=2), f32(hT_hi[:, :, :]),
                                ALU.subtract).then_inc(hT_ready, 1)

            def x_update(done):
                dve.wait_ge(*done)
                for t in range(T):
                    for h in range(2):
                        m = V.tensor_tensor(upd[:, t, h], ACC[2 * t + h][:, :], gate_bc[:, h * 512:(h + 1) * 512], ALU.mult)
                    link(m)
                    xt = x[:, t].rearrange("p (h c) -> p h c", h=2)
                    V.tensor_tensor(xt, xt, upd[:, t], ALU.add).then_inc(x_ready, 1)

            def ffn(u0, f0, n, more, moe=False):
                split(u0 + 1, (0, 1))
                hidden(f0, 0 if moe else None)
                split(u0, (2,))
                with dve.Fori(1, n if more else n - 1) as i:
                    h_split(f0 + i - 1)
                    split(u0 + i + 1, (0, 1))
                    hidden(f0 + i, i if moe else None)
                    split(u0 + i, (2,))
                if not more:
                    h_split(f0 + n - 2)
                    hidden(f0 + n - 1, n - 1)
                    split(u0 + n - 1, (2,))
                h_split(f0 + n - 1)
                x_update((used[2], u0 + n + 1))

            def merge(u0, m, gates):
                split(u0, (2,))
                split(u0 + 1, (0,))
                dve.wait_ge(pa_psum, m + 1)
                for t in range(T):
                    for h in range(2):
                        e = V.tensor_tensor(y[:, t, h * 512:(h + 1) * 512], gates[:, t, h * 512:(h + 1) * 512], ACC[2 * t + h][:, :], ALU.mult)
                e.then_inc(ya_done, 1)
                split(u0 + 1, (1, 2))
                split(u0 + 2, (0,))
                dve.wait_ge(pb_psum, m + 1)
                for t in range(T):
                    for h in range(2):
                        e = V.tensor_tensor(ytmp[:, t, h], gates[:, t, D + h * 512:D + (h + 1) * 512], ACC[2 * t + h][:, :], ALU.mult)
                    link(e)
                    yt = y[:, t].rearrange("p (h c) -> p h c", h=2)
                    V.tensor_tensor(yt, yt, ytmp[:, t], ALU.add).then_inc(y_ready, 1)
                for b in range(4):
                    dve.wait_ge(yT_hi_done, 4 * m + b + 1)
                    V.tensor_tensor(yT_lo[:, 2 * b:2 * b + 2], bank[4 + b if b < 3 else 0][:, :].rearrange("p (k s) -> p k s", k=2),
                                    f32(yT_hi[:, 2 * b:2 * b + 2]), ALU.subtract).then_inc(yT_ready, 1)
                split(u0 + 2, (1,))
                split(u0 + 2, (2,))
                split(u0 + 3, (0, 1))
                x_update((used[1], u0 + 4))

            def job_bias(j0, jobs, j):
                kind, qt, g = jobs[j]
                nk = (qt + 1) * P
                sc, sp = scores[j % 2], bank[0 + 2 * (j % 2):2 + 2 * (j % 2)]
                dve.wait_ge(sc_done, j0 + j + 1)
                for p in range(2):
                    ps = sp[p][:, :].rearrange("p (i s) -> p i s", i=2)
                    if kind == 2:
                        e = V.scalar_tensor_tensor(sc[:, p, :, 0:nk], ps[:, :, 0:nk], QK ** -0.5,
                                                   mask[qt].unsqueeze(1).to_broadcast([P, 2, nk]), ALU.mult, ALU.add)
                        continue
                    for i in range(2):
                        h = 4 * g + 2 * i + p
                        if kind == 3:
                            e = V.scalar_tensor_tensor(sc[:, p, i, 0:nk], ps[:, i, 0:nk], f_cum[:, qt, h:h + 1], mask[qt], ALU.add, ALU.add)
                        else:
                            e = V.scalar_tensor_tensor(sc[:, p, i, 0:nk], dist[qt], SLOPES[h], ps[:, i, 0:nk], ALU.mult, ALU.add)
                e.then_inc(bias_done, 1)
                dve.wait_ge(bias_done, j0 + j + 1)
                V.tensor_reduce(nmax[j % 2].rearrange("p (a i) -> p a i", a=2), sc[:, :, :, 0:nk], AX.X, ALU.max,
                                negate=True).then_inc(nmax_done, 1)

            def job_out(j0, jobs, j):
                kind, qt, g = jobs[j]
                dve.wait_ge(pv_done, j0 + j + 1)
                o_ps = HT[:, 0:4 * DH].rearrange("p (a i d) -> p a i d", a=2, i=2)
                link(V.reciprocal(rsum, psum_row[j % 4]))
                r = rsum.rearrange("p (a i) -> p a i", a=2)
                if kind < 2:
                    gate = nsa_gate[:, qt, 4 * g:4 * g + 4, 1 + kind].rearrange("p (i a) -> p a i", a=2)
                    link(V.tensor_tensor(coef.rearrange("p (a i) -> p a i", a=2), r, gate, ALU.mult))
                    r = coef.rearrange("p (a i) -> p a i", a=2)
                dst = o_h if kind == 3 else o_a if kind < 2 else o_b
                ov = dst[:, qt, 256 * g:256 * g + 256].rearrange("p (i a d) -> p a i d", i=2, a=2)
                if kind >= 2:
                    for a in range(2):
                        e = V.tensor_tensor(ov[:, a], o_ps[:, a], r[:, a].unsqueeze(2).to_broadcast([P, 2, DH]), ALU.mult)
                    e.then_inc(o_done, 1)
                else:
                    tv = o_tmp.rearrange("p (a i) d -> p a i d", a=2)
                    for a in range(2):
                        e = V.tensor_tensor(tv[:, a], o_ps[:, a], r[:, a].unsqueeze(2).to_broadcast([P, 2, DH]), ALU.mult)
                    e.then_inc(o_done, 1)
                    dve.wait_ge(o_done, j0 + j + 1)
                    for a in range(2):
                        e = V.tensor_tensor(ov[:, a], ov[:, a], tv[:, a], ALU.add)
                    link(e)

            def jobs_run(j0, jobs):
                job_bias(j0, jobs, 0)
                job_bias(j0, jobs, 1)
                for j, (kind, qt, g) in enumerate(jobs):
                    if qt:
                        dve.wait_ge(pt_psum, j0 + j + 1)
                        V.tensor_copy(pT[j % 2][:, 1], bank[5][:, :].rearrange("p (h q) -> p h q", h=4)).then_inc(pt_copied_v, 1)
                    if j + 2 < len(jobs):
                        job_bias(j0, jobs, j + 2)
                    job_out(j0, jobs, j)

            V.memset(zeros[:, :], 0.0).then_inc(first_ready, 1)
            for j in range(2):
                b = slice(j * BLK, (j + 1) * BLK)
                dve.wait_ge(hi_ready[j], 1)
                V.tensor_tensor(w_lo[:, b], raw[:, b], f32(w_hi[:, b]), ALU.subtract).then_inc(lo_ready[j], 1)
            dve.wait_ge(x_landed, 16)
            dve.wait_ge(cst_landed, 32)
            V.memset(stat[:, 0:2], 0.0).then_inc(x_ready, 2)

            with dve.Fori(0, DEPTH) as l:
                links[:] = [0, l * CHAIN_PER_LAYER]
                u_mix = l * LAYER_UNITS + FFN_UNITS
                norm(l * 3, l * 3, half=0.5)
                ffn(l * LAYER_UNITS, l * 2 * FFN_UNITS, FFN_UNITS, True)

                norm(l * 3 + 1, l * 3 + 1)
                split(u_mix, (2,))
                split(u_mix + 1, (0, 1))
                dve.wait_ge(w_done, l * 6 + 1)
                V.tensor_copy(proj[:, 1, 0:512], bank[1][:, :]).then_inc(w_evac_v, 1)
                split(u_mix + 1, (2,))
                dve.wait_ge(lat_ss, l * 4 + 4)
                V.tensor_scalar(lms[:, 0:2], lss[:, 0:2], 1.0 / Q_RANK, EPS, ALU.mult, ALU.add)
                V.tensor_scalar(lms[:, 2:4], lss[:, 2:4], 1.0 / KV_RANK, EPS, ALU.mult, ALU.add).then_inc(lat_ms, 1)
                dve.wait_ge(lat_sq, l + 1)
                link(V.reciprocal(lrs, lsq))
                for t in range(T):
                    V.tensor_scalar(proj[:, t, C_CQ:C_CKV], proj[:, t, C_CQ:C_CKV], lrs[:, t:t + 1], None, ALU.mult)
                    e = V.tensor_scalar(proj[:, t, C_CKV:C_KR], proj[:, t, C_CKV:C_KR], lrs[:, 2 + t:3 + t], None, ALU.mult)
                e.then_inc(lat_ready, 1)
                kr = proj[:, :, C_KR:C_GN]
                V.tensor_tensor(kr_a[:, :, :], kr, cos2, ALU.mult)
                link(V.tensor_tensor(kr_b[:, :, :], kr, sin2, ALU.mult))
                split(u_mix + 2, (0, 1))
                dve.wait_ge(w_done, l * 6 + 2)
                V.tensor_copy(proj[:, 1, 768:1280], bank[4][:, :]).then_inc(w_evac_v, 1)
                split(u_mix + 2, (2,))
                dve.wait_ge(w_done, l * 6 + 3)
                V.tensor_copy(proj[:, 1, 1536:PROJ], bank[1][:, 0:184])
                V.tensor_copy(vsw[:, 1], bank[1][:, 184:440]).then_inc(w_evac_v, 1)
                dve.wait_ge(lvec_landed, l * 32 + 32)
                for b, cs in enumerate(((0, 1), (2, 3), (4,))):
                    dve.wait_ge(cqT_hi_done, l * 3 + b + 1)
                    for i, c in enumerate(cs):
                        e = V.scalar_tensor_tensor(cqT_lo[:, c], bank[2 + b][:, i * S:(i + 1) * S], lvec[:, L_QN + c:L_QN + c + 1],
                                                   f32(cqT_hi[:, c]), ALU.mult, ALU.subtract)
                    e.then_inc(cqT_ready, 1)
                dve.wait_ge(kw_psum, l + 1)
                V.tensor_copy(kT[1][:, :, :], bank[1][:, :].rearrange("p (g s) -> p g s", g=2)).then_inc(kw_ready, 1)
                dve.wait_ge(c_psum, l + 1)
                link(V.tensor_copy(cT[:, :, :], bank[2][:, :].rearrange("p (k s) -> p k s", k=2)))
                for k in range(2):
                    tok = cT[:, k].rearrange("p (n j) -> p j n", j=CMP_STRIDE)
                    for a in range(2):
                        pe_b = lvec[:, L_PE + 32 * k + 16 * a:L_PE + 32 * k + 16 * a + 16].unsqueeze(2).to_broadcast([P, 16, N_CMP])
                        e = V.tensor_tensor(blocks[:, k, 16 * a:16 * a + 16], tok[:, :, a:a + N_CMP], pe_b, ALU.add)
                e.then_inc(blocks_ready, 1)
                split(u_mix + 3, (0,))
                dve.wait_ge(kvc_psum, l + 1)
                for g in range(GROUPS):
                    V.tensor_copy(kT_cmp[:, g, 0:N_CMP], bank[4 + g][:, 0:N_CMP])
                    for i in range(4):
                        e = V.tensor_copy(v_cmp[32 * i:32 * i + N_CMP, g], bank[4 + g][32 * i:32 * i + N_CMP, 64:128])
                e.then_inc(kvc_ready, 1)
                dve.wait_ge(uq_copied, l * 4 + 4)
                qr = q_tok[:, :, :, NOPE:QK]
                for t in range(T):
                    V.tensor_tensor(rope_a[:, t], qr[:, t], cos2[:, t].unsqueeze(1).to_broadcast([P, HEADS, ROPE]), ALU.mult)
                    e = V.tensor_tensor(rope_b[:, t], qr[:, t], sin2[:, t].unsqueeze(1).to_broadcast([P, HEADS, ROPE]), ALU.mult)
                link(e)
                H2 = ROPE // 2
                V.tensor_tensor(q_tok[:, :, :, NOPE:NOPE + H2], rope_a[:, :, :, 0:H2], rope_b[:, :, :, H2:ROPE], ALU.subtract)
                V.tensor_tensor(q_tok[:, :, :, NOPE + H2:QK], rope_b[:, :, :, 0:H2], rope_a[:, :, :, H2:ROPE], ALU.add).then_inc(rope_done, 1)
                bc = [P, HEADS, H2]
                for t in range(T):
                    V.tensor_tensor(k_tok[:, t, :, NOPE:NOPE + H2], kr_a[:, t, 0:H2].unsqueeze(1).to_broadcast(bc),
                                    kr_b[:, t, H2:ROPE].unsqueeze(1).to_broadcast(bc), ALU.subtract)
                    V.tensor_tensor(k_tok[:, t, :, NOPE + H2:QK], kr_b[:, t, 0:H2].unsqueeze(1).to_broadcast(bc),
                                    kr_a[:, t, H2:ROPE].unsqueeze(1).to_broadcast(bc), ALU.add)
                for t in range(T):
                    dve.wait_ge(uk_psum, l * 2 + t + 1)
                    V.tensor_copy(k_tok[:, t, :, 0:NOPE], bank[4 + t][:, :].rearrange("p (h c) -> p h c", h=HEADS)).then_inc(uk_copied, 1)
                for t in range(T):
                    dve.wait_ge(uv_psum, l * 2 + t + 1)
                    V.tensor_copy(vm[:, t], bank[6 if t == 0 else 3][:, :]).then_inc(uv_ready, 1)
                for b in range(4):
                    dve.wait_ge(km_psum, l * 4 + b + 1)
                    V.tensor_copy(qkT_m[0:QK, 1, 2 * b:2 * b + 2], bank[4 + b % 3][0:QK, :].rearrange("p (h s) -> p h s", h=2)).then_inc(km_ready, 1)
                link(V.memset(p_cmp[:, :, :], 0.0))
                dve.wait_ge(cs_psum, l + 1)
                pc = p_cmp.rearrange("p (a q i) n -> p a q i n", a=2, q=2)
                for p in range(2):
                    for qt in range(2):
                        e = V.tensor_tensor(pc[:, p, qt, :, 0:N_CMP], bank[p][:, 64 * qt:64 * qt + 64].rearrange("p (i n) -> p i n", i=4)[:, :, 0:N_CMP],
                                            cmp_bias[:, p, qt, :, 0:N_CMP], ALU.add)
                link(e)
                link(V.tensor_reduce(cmax, p_cmp[:, :, 0:N_CMP], AX.X, ALU.max))
                V.tensor_tensor(p_cmp[:, :, 0:N_CMP], p_cmp[:, :, 0:N_CMP], cmax.unsqueeze(2).to_broadcast([P, 16, N_CMP]),
                                ALU.subtract).then_inc(cs_ready, 1)
                dve.wait_ge(cp_exp, l + 1)
                link(V.tensor_reduce(csum, p_cmp[:, :, 0:N_CMP], AX.X, ALU.add))
                link(V.reciprocal(crec, csum))
                dve.wait_ge(nsa_gate_ready, l + 1)
                for qt in range(2):
                    g0 = nsa_gate[:, qt, :, 0].rearrange("p (i a) -> p a i", a=2)
                    cc = ccoef.rearrange("p (a q i) -> p a q i", a=2, q=2)[:, :, qt]
                    cr = crec.rearrange("p (a q i) -> p a q i", a=2, q=2)[:, :, qt]
                    e = V.scalar_tensor_tensor(cc, cr, cmp_valid[:, qt:qt + 1], g0, ALU.mult, ALU.mult)
                link(e)
                dve.wait_ge(co_psum, l + 1)
                oav = o_a.rearrange("p t (i a d) -> p t i a d", i=4, a=2)
                for i in range(4):
                    for qt in range(2):
                        cc = ccoef.rearrange("p (a q i) -> p a q i", a=2, q=2)[:, :, qt, i]
                        e = V.tensor_tensor(oav[:, qt, i], bank[3 + i][:, 128 * qt:128 * qt + 128].rearrange("p (a d) -> p a d", a=2),
                                            cc.unsqueeze(2).to_broadcast([P, 2, DH]), ALU.mult)
                e.then_inc(co_done, 1)
                dve.wait_ge(co_done, l + 1)
                jobs_run(l * NJ, JOBS)
                split(u_mix + 3, (1, 2))
                for m in (4, 5):
                    split(u_mix + m, (0, 1, 2))
                split(u_mix + 6, (0, 1))
                for b in range(4):
                    dve.wait_ge(oT_hi_done, l * 4 + b + 1)
                    V.tensor_tensor(oT_lo[b // 2][:, 2 * (b % 2):2 * (b % 2) + 2], bank[3 + b][:, :].rearrange("p (c s) -> p c s", c=2),
                                    f32(oT_hi[b // 2][:, 2 * (b % 2):2 * (b % 2) + 2]), ALU.subtract).then_inc(oT_ready, 1)
                dve.wait_ge(w_evac_a, l * 8 + 8)
                merge(u_mix + MIX_IN_UNITS, l, gates_m)

                norm(l * 3 + 2, l * 3 + 2, half=0.5)
                ffn(l * LAYER_UNITS + FFN_UNITS + MIX_IN_UNITS + MERGE_UNITS, l * 2 * FFN_UNITS + FFN_UNITS, FFN_UNITS, True)
                assert links[0] <= CHAIN_PER_LAYER
                if links[0] < CHAIN_PER_LAYER:
                    V.memset(pad, 0.0).then_inc(chain, CHAIN_PER_LAYER - links[0])

            links[:] = [0, DEPTH * CHAIN_PER_LAYER]
            q6, n6 = 3 * DEPTH, 3 * DEPTH
            rms(q6)
            dve.wait_ge(fn_landed, 16)
            for t in range(T):
                V.scalar_tensor_tensor(x[:, t], x[:, t], rstd[:, t:t + 1], fn_bc, ALU.mult, ALU.mult).then_inc(x_ready, 1)
            dve.wait_ge(x_ready, 2 * (q6 + 2))
            norm(q6 + 1, n6, gain=vec[:, V_N1:V_N1 + 8])
            u = HYB_U0
            split(u, (2,))
            for m in range(HYB_IN_UNITS):
                if m + 1 < HYB_IN_UNITS:
                    split(u + m + 1, (0, 1))
                if m < 4:
                    dve.wait_ge(w_done, DEPTH * 6 + m + 1)
                    dst, c0 = (xcb, 768 * m) if m < 2 else (qkv, 768 * (m - 2))
                    V.tensor_copy(dst[:, 1, c0:c0 + 512], bank[3 * (m % 2) + 1][:, :]).then_inc(w_evac_v, 1)
                if m + 1 < HYB_IN_UNITS:
                    split(u + m + 1, (2,))
            dve.wait_ge(w_evac_a, DEPTH * 8 + 4)
            dve.wait_ge(w_evac_v, DEPTH * 3 + 2)
            V.tensor_tensor(u_tok[:, :, :], xcb[:, :, 0:512], xcb[:, :, 512:1024], ALU.mult).then_inc(u_ready, 1)
            dve.wait_ge(w_evac_a, DEPTH * 8 + 8)
            dve.wait_ge(w_evac_v, DEPTH * 3 + 4)
            qk_s = qk_ss.rearrange("p (i t h) -> p i t h", i=2, t=T)
            for i in range(2):
                v = qkv[:, :, 512 * i:512 * i + 512]
                link(V.tensor_tensor(squares[:, :, :], v, v, ALU.mult))
                link(V.tensor_reduce(qk_s[:, i], squares.rearrange("p t (h d) -> p t h d", h=HEADS), AX.X, ALU.add))
            V.tensor_scalar(qk_gain[:, 0:1], vec[:, V_QN:V_QN + 1], DH ** -0.5, None, ALU.mult)
            V.tensor_scalar(qk_ss, qk_ss, 1.0 / DH, EPS, ALU.mult, ALU.add).then_inc(qkn_ms, 1)
            dve.wait_ge(w_evac_a, DEPTH * 8 + 9)
            bf = vec[:, V_BF:V_BF + 8].unsqueeze(1).to_broadcast([P, T, 8])
            link(V.tensor_tensor(f_row[:, :, :], f_row[:, :, :], bf, ALU.add))
            V.tensor_scalar(f_cum[:, :, :], f_row[:, :, :], 0.0, None, ALU.min)
            V.scalar_tensor_tensor(f_e[:, :, :], f_row[:, :, :], -1.0, f_row[:, :, :], ALU.mult, ALU.min).then_inc(f_exp_in, 1)
            dve.wait_ge(qkn_sq, 1)
            link(V.reciprocal(qk_ss, qk_ss))
            for i in range(2):
                for t in range(T):
                    v = qkv[:, t, 512 * i:512 * i + 512].rearrange("p (h d) -> p h d", h=HEADS)
                    e = V.tensor_tensor(v, v, qk_s[:, i, t].unsqueeze(2).to_broadcast([P, HEADS, DH]), ALU.mult)
            e.then_inc(qkn_ready, 1)
            dve.wait_ge(f_exp, 1)
            V.tensor_scalar(f_l[:, :, :], f_e[:, :, :], 1.0, None, ALU.add).then_inc(f_ln_in, 1)
            dve.wait_ge(f_ln, 1)
            V.tensor_tensor(nlogf[:, :, :], f_l[:, :, :], f_cum[:, :, :], ALU.subtract).then_inc(logf_ready, 1)
            dve.wait_ge(uc_psum, 2)
            dve.wait_ge(b_psum, 1)
            V.memset(uTc[:, :, 0:2], 0.0)
            for b in range(2):
                e = V.tensor_copy(uTc[:, 2 * b:2 * b + 2, 2:S + 2], bank[4 + b][:, :].rearrange("p (c s) -> p c s", c=2))
            e.then_inc(uc_ready, 1)
            dve.wait_ge(uc_ready, 1)
            for j in range(3):
                for c in range(4):
                    w = vec[:, V_CONV + 3 * c + j:V_CONV + 3 * c + j + 1]
                    if j == 0:
                        e = V.tensor_scalar(conv[:, c], uTc[:, c, 0:S], w, None, ALU.mult)
                    else:
                        e = V.scalar_tensor_tensor(conv[:, c], uTc[:, c, j:j + S], w, conv[:, c], ALU.mult, ALU.add)
                link(e)
            for b in range(2):
                V.tensor_tensor(conv[:, 2 * b:2 * b + 2], conv[:, 2 * b:2 * b + 2],
                                bank[6 - 3 * b][:, :].rearrange("p (c s) -> p c s", c=2), ALU.mult).then_inc(ya_f32, 1)
            for b in range(2):
                dve.wait_ge(ya_hi_done, b + 1)
                V.tensor_tensor(oT_lo[0][:, 2 * b:2 * b + 2], conv[:, 2 * b:2 * b + 2], f32(oT_hi[0][:, 2 * b:2 * b + 2]),
                                ALU.subtract).then_inc(oT_ready, 1)
            dve.wait_ge(fcum_psum, 1)
            V.tensor_scalar(f_cum[:, :, :], bank[5][:, 0:16].rearrange("p (t h) -> p t h", t=T), -1.0, None, ALU.mult).then_inc(fcum_ready, 1)
            dve.wait_ge(fcum_ready, 1)
            jobs_run(DEPTH * NJ, HYB_JOBS)
            um = u + HYB_IN_UNITS
            split(um, (0, 1))
            for b in range(2):
                dve.wait_ge(oT_hi_done, DEPTH * 4 + b + 1)
                V.tensor_tensor(oT_lo[1][:, 2 * b:2 * b + 2], bank[5 + b][:, :].rearrange("p (c s) -> p c s", c=2),
                                f32(oT_hi[1][:, 2 * b:2 * b + 2]), ALU.subtract).then_inc(oT_ready, 1)
            dve.wait_ge(w_evac_a, DEPTH * 8 + 11)
            merge(um, DEPTH, gates_h)
            norm(q6 + 2, n6 + 1, gain=vec[:, V_N2:V_N2 + 8])
            dve.wait_ge(r_psum, 1)
            br = vec[:, V_BR:V_BR + 36].unsqueeze(1).to_broadcast([P, T, 36])
            link(V.tensor_tensor(logits[:, :, :], HT[:, 0:128].rearrange("p (t c) -> p t c", t=T)[:, :, 0:36], br, ALU.add))
            lg = logits[:, :, 0:4]

            def ranks(v, n, gt, eq, tie, rank):
                for t in range(T):
                    mine = v[:, t].unsqueeze(2).to_broadcast([P, n, n])
                    other = v[:, t].unsqueeze(1).to_broadcast([P, n, n])
                    V.tensor_tensor(gt[:, t], other, mine, ALU.is_gt)
                    e = V.tensor_tensor(eq[:, t], other, mine, ALU.is_equal)
                link(e)
                for t in range(T):
                    e = V.tensor_tensor(eq[:, t], eq[:, t], tie, ALU.mult)
                link(e)
                link(V.tensor_tensor(gt[:, :], gt[:, :], eq[:, :], ALU.add))
                link(V.tensor_reduce(rank[:, :, :], gt[:, :], AX.X, ALU.add))

            ranks(lg, 4, g_gt, g_eq, tie4, g_rank)
            V.tensor_scalar(g_sel[:, :, :], g_rank[:, :, :], 0.0, None, ALU.is_equal)
            link(V.tensor_reduce(g_max, lg, AX.X, ALU.max))
            V.tensor_tensor(g_exp[:, :, :], lg, g_max.unsqueeze(2).to_broadcast([P, T, 4]), ALU.subtract)
            for t in range(T):
                e = V.tensor_tensor(le_m[:, t], logits[:, t, 4:36].rearrange("p (g e) -> p g e", g=4),
                                    g_sel[:, t].unsqueeze(2).to_broadcast([P, 4, 8]), ALU.mult)
            link(e)
            link(V.tensor_reduce(le_g[:, :, :], le_m.rearrange("p t g e -> p t e g"), AX.X, ALU.add))
            link(V.tensor_reduce(e_max, le_g[:, :, :], AX.X, ALU.max))
            V.tensor_tensor(e_exp[:, :, :], le_g[:, :, :], e_max.unsqueeze(2).to_broadcast([P, T, 8]), ALU.subtract).then_inc(r_exp_in, 1)
            ranks(le_g, 8, e_gt, e_eq, tie8, e_rank)
            link(V.tensor_scalar(e_rank[:, :, :], e_rank[:, :, :], 2.0, None, ALU.is_lt))
            dve.wait_ge(r_exp, 1)
            V.tensor_reduce(g_sum, g_exp[:, :, :], AX.X, ALU.add)
            link(V.tensor_tensor(e_exp[:, :, :], e_exp[:, :, :], e_rank[:, :, :], ALU.mult))
            link(V.tensor_reduce(e_sum, e_exp[:, :, :], AX.X, ALU.add))
            V.reciprocal(p_sel, g_sum)
            link(V.reciprocal(e_sum, e_sum))
            link(V.tensor_tensor(e_sum, e_sum, p_sel, ALU.mult))
            link(V.tensor_tensor(e_w[:, :, :], e_exp[:, :, :], e_sum.unsqueeze(2).to_broadcast([P, T, 8]), ALU.mult))
            for t in range(T):
                e = V.tensor_tensor(comb[:, t].rearrange("p (g e) -> p g e", g=4), g_sel[:, t].unsqueeze(2).to_broadcast([P, 4, 8]),
                                    e_w[:, t].unsqueeze(1).to_broadcast([P, 4, 8]), ALU.mult)
            e.then_inc(comb_ready, 1)
            dve.wait_ge(comb_ready, 1)
            ffn(MOE_U0, DEPTH * 2 * FFN_UNITS, EXPERTS, False, moe=True)

        @block.tensor
        def _(pe):
            def release(s_):
                pe.matmul(MOD[:, 64:65], zeros[:, 0:P], zeros[:, 0:1], start=True, stop=True, skip_group_check=True).then_inc(s_, 1)

            def carry_waits():
                pe.matmul(MOD[:, 64:65], zeros[:, 0:P], zeros[:, 0:1], start=True, stop=True, skip_group_check=True)

            def need(u, seen, off, n):
                for j in range(off // BLK, (off + n - 1) // BLK + 1):
                    if j not in seen:
                        pe.wait_ge(lo_ready[j], u + 1)
                        seen.add(j)

            def mm3(dst, xh, xl, off, n, first, last):
                pe.matmul(dst, xh, w_hi[:, off:off + n], start=first, stop=False, skip_group_check=True)
                pe.matmul(dst, xh, w_lo[:, off:off + n], start=False, stop=False, skip_group_check=True)
                return pe.matmul(dst, xl, w_hi[:, off:off + n], start=False, stop=last, skip_group_check=True)

            def tok(t):
                return slice(t * P, (t + 1) * P)

            def ada_step(n, col, first=None):
                if first is not None:
                    pe.wait_ge(mod_ready, first)
                pe.wait_ge(ada_ready, n + 1)
                for h in range(2):
                    m = pe.matmul(MOD[:, bass.ds(col + h, 1)], ada_sum[:, h * P:(h + 1) * P], ones[:, 0:1],
                                  start=True, stop=True, skip_group_check=True)
                m.then_inc(mod_step, 1)

            def columns(u, ncol, b0, ada_n=None, ada_c=0, stage=None, off0=0, ks=range(KD), close=(0, 1, 2)):
                seen, n2 = set(), ncol - 512
                m = None
                for k in ks:
                    off = off0 + k * ncol
                    need(u, seen, off, ncol)
                    for t in range(T):
                        m = mm3(bank[b0 + t][:, 0:min(512, ncol)], uT_hi[:, k, tok(t)], uT_lo[:, k, tok(t)], off, min(512, ncol),
                                k == 0, k == KD - 1)
                        if n2 > 0:
                            dst = bank[b0 + 2][:, t * n2:(t + 1) * n2]
                            m = mm3(dst, uT_hi[:, k, tok(t)], uT_lo[:, k, tok(t)], off + 512, n2, k == 0 and t == 0, k == KD - 1)
                    for j in close:
                        if k < KD - 1 and off < (j + 1) * BLK <= off + ncol:
                            m.then_inc(used[j], 1)
                    if ada_n is not None and k == 3:
                        ada_step(ada_n, ada_c, stage)
                m.then_inc(w_done, 1)
                for j in close:
                    if (j + 1) * BLK > off0 + (len(ks) - 1) * ncol:
                        release(used[j])
                if ada_n is not None:
                    ada_step(ada_n + 1, ada_c + 2)

            def norm(n):
                pe.wait_ge(diag_done, n + 1)
                for h, b in enumerate((HT, GU[1])):
                    pe.matmul(b[:, :], ones, diag[:, 4 * h:4 * h + 4], start=True, stop=True).then_inc(gate_psum, 1)
                pe.wait_ge(xn_done, 2 * n + 2)
                for b in range(4):
                    for i in range(2):
                        for t in range(T):
                            m = pe.transpose(ACC[b][:, i * S + t * P:i * S + (t + 1) * P], xn[:, t, (2 * b + i) * P:(2 * b + i + 1) * P], ident)
                    m.then_inc(uT_psum, 1)

            def gate_up(u):
                seen = set()
                for k in range(KD):
                    need(u, seen, k * 512, 512)
                    for t in range(T):
                        m = mm3(GU[t][:, :], uT_hi[:, k, tok(t)], uT_lo[:, k, tok(t)], k * 512, 512, k == 0, k == KD - 1)
                        if k == KD - 1 and t == 0:
                            m.then_inc(gu0_done, 1)
                    if k in (3, 7):
                        m.then_inc(used[k // 4], 1)

            def turn(f):
                pe.wait_ge(h_done, f * 2 + 2)
                for t in range(T):
                    for c in range(2):
                        m = pe.transpose(HT[:, c * S + t * P:c * S + (t + 1) * P], hid[:, t, c * P:(c + 1) * P], ident)
                m.then_inc(hT_psum, 1)

            def down(u, f, last=False):
                pe.wait_ge(hT_ready, f + 1)
                pe.wait_ge(lo_ready[2], u + 1)
                for c in range(2):
                    for t in range(T):
                        for h in range(2):
                            m = mm3(ACC[2 * t + h][:, :], hT_hi[:, c, tok(t)], hT_lo[:, c, tok(t)], 2 * BLK + c * D + h * 512, 512,
                                    False, last and c == 1)
                m.then_inc(used[2], 1)

            def ffn(u0, f0, n, nn, stage):
                pe.wait_ge(uT_ready, 4 * nn + 4)
                pe.wait_ge(gate_ready, 2 * nn + 2)
                gate_up(u0)
                if stage is not None:
                    ada_step(stage * ADA_STEPS, 0, stage)
                    ada_step(stage * ADA_STEPS + 1, 2)
                for b in range(4):
                    pe.matmul(ACC[b][:, :], zeros[:, 0:P], zeros[:, :], start=True, stop=False, skip_group_check=True)
                with pe.Fori(1, n) as i:
                    turn(f0 + i - 1)
                    gate_up(u0 + i)
                    if stage is not None:
                        ada_step(stage * ADA_STEPS + i + 1, i * 2 + 2)
                    down(u0 + i - 1, f0 + i - 1)
                turn(f0 + n - 1)
                down(u0 + n - 1, f0 + n - 1, last=True)

            def half_product(lhs, chunks, blocks_, sem_, first_wait):
                seen = {}
                pe.wait_ge(*first_wait)
                for k in range(4):
                    u, off = chunks[k]
                    need(u, seen.setdefault(str(u), set()), off, D)
                    for t in range(T):
                        for h in range(2):
                            m = mm3(ACC[2 * t + h][:, :], lhs[0][:, k, tok(t)], lhs[1][:, k, tok(t)], off + h * 512, 512, k == 0, k == 3)
                    if k in blocks_:
                        m.then_inc(used[blocks_[k]], 1)
                release(sem_)

            def merge(u0, m, close2):
                u1, u2 = u0 + 1, u0 + 2
                half_product((oT_hi[0], oT_lo[0]), [(u0, k * D) for k in range(4)], {1: 0, 3: 1}, pa_psum, (oT_ready, 4 * m + 2))
                pe.wait_ge(oT_ready, 4 * m + 4)
                half_product((oT_hi[1], oT_lo[1]), [(u0, 4 * D), (u0, 5 * D), (u1, 0), (u1, D)], {1: 2, 3: 0}, pb_psum, (ya_done, m + 1))
                pe.wait_ge(y_ready, 2 * m + 2)
                for b in range(4):
                    if b == 3:
                        pe.wait_ge(y_ready, 2 * m + 2)
                    dst = bank[4 + b if b < 3 else 0]
                    for i in range(2):
                        for t in range(T):
                            e = pe.transpose(dst[:, i * S + t * P:i * S + (t + 1) * P], y[:, t, (2 * b + i) * P:(2 * b + i + 1) * P], ident)
                    e.then_inc(yT_psum, 1)
                for k in range(KD):
                    u, off = (u1, BLK + k * D) if k < 4 else (u2, (k - 4) * D)
                    if k % 2 == 0:
                        pe.wait_ge(lo_ready[off // BLK], u + 1)
                    if k == 0:
                        pe.wait_ge(yT_ready, 4 * m + 4)
                    for t in range(T):
                        for h in range(2):
                            e = mm3(ACC[2 * t + h][:, :], yT_hi[:, k, tok(t)], yT_lo[:, k, tok(t)], off + h * 512, 512, k == 0, k == KD - 1)
                    if k % 2 == 1:
                        e.then_inc(used[off // BLK], 1)
                    elif k == 6 and close2:
                        e.then_inc(used[2], 1)

            def sc_job(j0, jobs, j):
                kind, qt, g = jobs[j]
                nk = (qt + 1) * P
                if j >= 2:
                    pe.wait_ge(bias_done, j0 + j - 1)
                for p in range(2):
                    half = slice(DH * p, DH * p + DH)
                    for i in range(2):
                        h, c = 4 * g + 2 * i + p, 2 * g + i
                        dst = bank[2 * (j % 2) + p][:, i * S:i * S + nk]
                        if kind == 2:
                            m = pe.matmul(dst, qkT_m[0:QK, 0, h, tok(qt)], qkT_m[0:QK, 1, h, 0:nk], start=True, stop=True, skip_group_check=True)
                        elif kind == 3:
                            pe.matmul(dst, nlogf[:, 0, h:h + 1].to_broadcast([P, P]), tri[:, 0:nk], start=True, stop=False, skip_group_check=True)
                            if qt:
                                pe.matmul(bank[2 * (j % 2) + p][:, i * S + P:i * S + nk], nlogf[:, 1, h:h + 1].to_broadcast([P, P]), tri[:, 0:P],
                                          start=False, stop=False, skip_group_check=True)
                            m = pe.matmul(dst, qT_h[half, c, tok(qt)], kT_h[half, c, 0:nk], start=False, stop=True, skip_group_check=True)
                        else:
                            m = pe.matmul(dst, qT[half, c, tok(qt)], kT[kind][half, g, 0:nk], start=True, stop=True, skip_group_check=True)
                m.then_inc(sc_done, 1)

            def jobs_run(j0, v0, jobs):
                nv = 0
                sc_job(j0, jobs, 0)
                if jobs is JOBS:
                    pe.wait_ge(cp_ready, j0_layer[0] + 1)
                    pe.wait_ge(co_done, j0_layer[0] + 1)
                sc_job(j0, jobs, 1)
                for j, (kind, qt, g) in enumerate(jobs):
                    pe.wait_ge(exp_done, j0 + j + 1)
                    if j >= 1:
                        pe.wait_ge(pt_copied_a, j0 + j)
                    if nv:
                        pe.wait_ge(pt_copied_v, v0 + nv)
                    for kt in range(qt + 1):
                        for h in range(4):
                            m = pe.transpose(bank[4 + kt][:, h * P:(h + 1) * P], scores[j % 2][:, h // 2, h % 2, tok(kt)], ident)
                    m.then_inc(pt_psum, 1)
                    if j + 2 < len(jobs):
                        sc_job(j0, jobs, j + 2)
                    nv += qt
                    pe.wait_ge(pt_copied_a, j0 + j + 1)
                    if qt:
                        pe.wait_ge(pt_copied_v, v0 + nv)
                    if j >= 1:
                        pe.wait_ge(o_done, j0 + j)
                    for a in range(4):
                        h = 4 * g + 2 * (a % 2) + a // 2
                        for kt in range(qt + 1):
                            if kind < 2:
                                v = vsw[:, kt, P * kind + DH * g:P * kind + DH * g + DH]
                            elif kind == 2:
                                v = vm[:, kt, DH * h:DH * h + DH]
                            else:
                                v = qkv[:, kt, 1024 + DH * h:1024 + DH * h + DH]
                            m = pe.matmul(HT[:, a * DH:(a + 1) * DH], pT[j % 2][:, kt, a], v, start=kt == 0, stop=kt == qt, skip_group_check=True)
                    m.then_inc(pv_done, 1)

            def turn_rows(dst, src, cols, parts=P):
                for t in range(T):
                    m = pe.transpose(dst[0:parts, t * P:(t + 1) * P], src(t, cols), ident)
                return m

            j0_layer = [0]
            pe.wait_ge(first_ready, 1)
            pe.wait_ge(cst_landed, 32)
            for s_ in used + [mod_step]:
                release(s_)
            for st in range(ADA_STEPS):
                ada_step(st, 2 * st)

            with pe.Fori(0, DEPTH) as l:
                j0_layer[0] = l
                u_mix = l * LAYER_UNITS + FFN_UNITS
                norm(l * 3)
                ffn(l * LAYER_UNITS, l * 2 * FFN_UNITS, FFN_UNITS, l * 3, l * 3 + 1)

                norm(l * 3 + 1)
                pe.wait_ge(uT_ready, l * 12 + 8)
                pe.wait_ge(gate_ready, l * 6 + 4)
                stage = l * 3 + 2
                for m in range(2):
                    columns(u_mix + m, 768, 3 * m, stage * ADA_STEPS + 2 * m, 4 * m, stage if m == 0 else None)
                pe.wait_ge(w_evac_a, l * 8 + 2)
                pe.wait_ge(w_evac_v, l * 3 + 1)
                columns(u_mix + 2, U2_COLS, 0, stage * ADA_STEPS + 4, 8, close=(0,))
                src = lambda t, cols: proj[:, t, cols]
                pe.wait_ge(lat_ready, l + 1)
                pe.wait_ge(w_evac_a, l * 8 + 4)
                pe.wait_ge(w_evac_v, l * 3 + 2)
                for c in range(5):
                    m = turn_rows(bank[2 + c // 2][:, (c % 2) * S:(c % 2) * S + S], src, slice(C_CQ + c * P, C_CQ + c * P + P))
                    if c in (1, 3, 4):
                        m.then_inc(cqT_psum, 1)
                pe.wait_ge(w_evac_a, l * 8 + 5)
                pe.wait_ge(w_evac_v, l * 3 + 3)
                for c in range(4):
                    m = turn_rows(bank[5 + c // 2][:, (c % 2) * S:(c % 2) * S + S], src, slice(C_Q + c * P, C_Q + c * P + P))
                    if c % 2:
                        m.then_inc(q_psum, 1)
                for kind, (c0, s_) in enumerate(((C_KS, ks_psum), (C_KW, kw_psum))):
                    for g in range(GROUPS):
                        for t in range(T):
                            for p in range(2):
                                m = pe.matmul(bank[kind][DH * p:DH * p + DH, g * S + t * P:g * S + (t + 1) * P],
                                              proj[:, t, c0 + g * DH:c0 + g * DH + DH], ident, start=True, stop=True,
                                              skip_group_check=True)
                    m.then_inc(s_, 1)
                pe.wait_ge(cqT_ready, l * 3 + 1)
                for k in range(2):
                    m = turn_rows(bank[2][:, k * S:k * S + S], src, slice(C_KC + k * P, C_KC + k * P + P))
                m.then_inc(c_psum, 1)
                pe.wait_ge(blocks_ready, l + 1)
                pe.wait_ge(cqT_ready, l * 3 + 3)
                carry_waits()
                for k in range(2):
                    for g in range(GROUPS):
                        rows = slice(DH * g, DH * g + DH)
                        for j in range(CMP_BLOCK):
                            m = pe.matmul(bank[3 - g][rows, 16 * k:16 * k + N_CMP], cmpw[rows, k, j * DH:(j + 1) * DH], blocks[rows, k, j],
                                          start=j == 0, stop=j == CMP_BLOCK - 1, skip_group_check=True)
                m.then_inc(hidc_psum, 1)
                pe.wait_ge(hidc_ready, l + 1)
                pe.wait_ge(q_ready, l * 2 + 2)
                carry_waits()
                for g in range(GROUPS):
                    rows = slice(DH * g, DH * g + DH)
                    for p in range(2):
                        pe.matmul(bank[4 + g][DH * p:DH * p + DH, 0:N_CMP], lvec[rows, L_W2:L_W2 + DH], hid_cmp[rows, 0, 0:N_CMP],
                                  start=True, stop=True, skip_group_check=True)
                    for i in range(4):
                        m = pe.matmul(bank[4 + g][32 * i:32 * i + N_CMP, 64:128], hid_cmp[rows, 1, 0:N_CMP], lvec[rows, L_W2 + DH:L_W2 + 2 * DH],
                                      start=True, stop=True, skip_group_check=True)
                m.then_inc(kvc_psum, 1)
                pe.wait_ge(ks_ready, l + 1)
                pe.wait_ge(kw_ready, l + 1)
                seen = set()
                for b in range(4):
                    for k in range(3):
                        off = UQ_OFF + k * 768 + (b % 2) * 384
                        need(u_mix + 2, seen, off, 384)
                        m = mm3(bank[b][:, 0:384], cqT_hi[:, k, tok(b // 2)], cqT_lo[:, k, tok(b // 2)], off, 384, k == 0, k == 2)
                    m.then_inc(uq_psum, 1)
                for j in (1, 2):
                    release(used[j])
                pe.wait_ge(kvc_ready, l + 1)
                pe.wait_ge(lo_ready[0], u_mix + 4)
                for t in range(T):
                    for k in range(2):
                        m = mm3(bank[4 + t][:, :], cqT_hi[:, 3 + k, tok(t)], cqT_lo[:, 3 + k, tok(t)], k * 512, 512, k == 0, k == 1)
                    m.then_inc(uk_psum, 1)
                pe.wait_ge(uq_copied, l * 4 + 4)
                for t in range(T):
                    for k in range(2):
                        m = mm3(bank[6 if t == 0 else 3][:, :], cqT_hi[:, 3 + k, tok(t)], cqT_lo[:, 3 + k, tok(t)], 1024 + k * 512, 512, k == 0, k == 1)
                    m.then_inc(uv_psum, 1)
                release(used[0])
                pe.wait_ge(rope_done, l + 1)
                for b in range(4):
                    if b == 3:
                        pe.wait_ge(uv_ready, l * 2 + 2)
                    for i in range(2):
                        m = turn_rows(bank[b][:, i * S:i * S + S], lambda t, h: q_tok[:, t, h], 2 * b + i, QK)
                    m.then_inc(qm_psum, 1)
                pe.wait_ge(uk_copied, l * 2 + 2)
                for b in range(4):
                    if b == 3:
                        pe.wait_ge(km_ready, l * 4 + 1)
                    for i in range(2):
                        m = turn_rows(bank[4 + b % 3][:, i * S:i * S + S], lambda t, h: k_tok[:, t, h], 2 * b + i, QK)
                    m.then_inc(km_psum, 1)
                pe.wait_ge(qm_ready, l * 4 + 4)
                for p in range(2):
                    half = slice(DH * p, DH * p + DH)
                    for qt in range(2):
                        for i in range(4):
                            m = pe.matmul(bank[p][:, 64 * qt + 16 * i:64 * qt + 16 * i + N_CMP], qT[half, i, tok(qt)], kT_cmp[half, i // 2, 0:N_CMP],
                                          start=True, stop=True, skip_group_check=True)
                m.then_inc(cs_psum, 1)
                pe.wait_ge(cp_exp, l + 1)
                for a in range(4):
                    m = pe.transpose(bank[2][:, a * P:(a + 1) * P], p_cmp[:, 4 * a:4 * a + 4, :], ident)
                m.then_inc(cp_psum, 1)
                pe.wait_ge(cp_ready, l + 1)
                pe.wait_ge(km_ready, l * 4 + 4)
                for i in range(4):
                    rows = slice(32 * i, 32 * i + N_CMP)
                    for qt in range(2):
                        for p in range(2):
                            m = pe.matmul(bank[3 + i][:, 128 * qt + 64 * p:128 * qt + 64 * p + 64], pT_cmp[rows, 2 * p + qt], v_cmp[rows, i // 2],
                                          start=True, stop=True, skip_group_check=True)
                m.then_inc(co_psum, 1)
                pe.wait_ge(cs_ready, l + 1)
                jobs_run(l * NJ, l * 6, JOBS)
                pe.wait_ge(bias_done, l * NJ + NJ)
                columns(u_mix + 3, 512, 0, stage * ADA_STEPS + 6, 12, off0=BLK, close=(1,))
                release(used[2])
                for m in (4, 5):
                    if m == 5:
                        pe.wait_ge(w_evac_a, l * 8 + 6)
                    columns(u_mix + m, 768, 3 if m == 4 else 0, stage * ADA_STEPS + 2 * m, 4 * m)
                pe.wait_ge(w_evac_a, l * 8 + 7)
                pe.wait_ge(o_done, l * NJ + NJ)
                for b in range(4):
                    o = o_a if b < 2 else o_b
                    for i in range(2):
                        c = 2 * (b % 2) + i
                        m = turn_rows(bank[3 + b][:, i * S:i * S + S], lambda t, c_: o[:, t, c_], slice(c * P, c * P + P))
                    m.then_inc(oT_psum, 1)
                pe.wait_ge(w_evac_a, l * 8 + 8)
                merge(u_mix + MIX_IN_UNITS, l, True)

                norm(l * 3 + 2)
                ffn(l * LAYER_UNITS + FFN_UNITS + MIX_IN_UNITS + MERGE_UNITS, l * 2 * FFN_UNITS + FFN_UNITS, FFN_UNITS, l * 3 + 2, l * 3 + 3)

            n6, u = 3 * DEPTH, HYB_U0
            norm(n6)
            pe.wait_ge(uT_ready, 4 * n6 + 4)
            pe.wait_ge(gate_ready, 2 * n6 + 2)
            evac_a = [2, 4, 6, 8, 9, 10, 11]
            for m in range(HYB_IN_UNITS):
                if m >= 2:
                    pe.wait_ge(w_evac_a, DEPTH * 8 + evac_a[m - 2])
                    pe.wait_ge(w_evac_v, DEPTH * 3 + min(m - 1, 4))
                columns(u + m, 768 if m < 6 else 520, 3 * (m % 2), (n6 + 1) * ADA_STEPS + 2 * m if m < 6 else None, 4 * m,
                        n6 + 1 if m == 0 else None)
            pe.wait_ge(w_evac_a, DEPTH * 8 + 11)
            pe.wait_ge(u_ready, 1)
            for c in range(4):
                m = turn_rows(bank[4 + c // 2][:, (c % 2) * S:(c % 2) * S + S], lambda t, c_: u_tok[:, t, c_], slice(c * P, c * P + P))
                if c % 2:
                    m.then_inc(uc_psum, 1)
            for c in range(4):
                m = turn_rows(bank[6 - 3 * (c // 2)][:, (c % 2) * S:(c % 2) * S + S], lambda t, c_: xcb[:, t, c_],
                              slice(1024 + c * P, 1024 + c * P + P))
            m.then_inc(b_psum, 1)
            pe.wait_ge(qkn_ready, 1)
            for c in range(4):
                m = turn_rows(bank[c // 2][:, (c % 2) * S:(c % 2) * S + S], lambda t, c_: qkv[:, t, c_], slice(c * P, c * P + P))
                if c % 2:
                    m.then_inc(q_psum, 1)
            pe.wait_ge(uc_ready, 1)
            for c in range(4):
                m = turn_rows(bank[2 + 2 * (c // 2)][:, (c % 2) * S:(c % 2) * S + S], lambda t, c_: qkv[:, t, c_],
                              slice(512 + c * P, 512 + c * P + P))
                if c % 2:
                    m.then_inc(kh_psum, 1)
            pe.wait_ge(logf_ready, 1)
            pe.matmul(bank[5][:, 0:8], tri[:, 0:P], nlogf[:, 0], start=True, stop=True, skip_group_check=True)
            pe.matmul(bank[5][:, 8:16], ones, nlogf[:, 0], start=True, stop=False, skip_group_check=True)
            pe.matmul(bank[5][:, 8:16], tri[:, 0:P], nlogf[:, 1], start=False, stop=True, skip_group_check=True).then_inc(fcum_psum, 1)
            pe.wait_ge(q_ready, DEPTH * 2 + 2)
            pe.wait_ge(kh_ready, 2)
            pe.wait_ge(ya_hi_done, 2)
            pe.wait_ge(oT_ready, DEPTH * 4 + 2)
            pe.wait_ge(fcum_ready, 1)
            jobs_run(DEPTH * NJ, DEPTH * 6, HYB_JOBS)
            um = u + HYB_IN_UNITS
            pe.wait_ge(o_done, DEPTH * NJ + len(HYB_JOBS))
            for b in range(2):
                for i in range(2):
                    c = 2 * b + i
                    m = turn_rows(bank[5 + b][:, i * S:i * S + S], lambda t, c_: o_h[:, t, c_], slice(c * P, c * P + P))
                m.then_inc(oT_psum, 1)
            merge(um, DEPTH, False)
            norm(n6 + 1)
            pe.wait_ge(uT_ready, 4 * n6 + 8)
            pe.wait_ge(gate_ready, 2 * n6 + 4)
            pe.wait_ge(lo_ready[2], um + 3)
            for t in range(T):
                for k in range(KD):
                    m = mm3(HT[:, 64 * t:64 * t + 36], uT_hi[:, k, tok(t)], uT_lo[:, k, tok(t)], 2 * BLK + 36 * k, 36, k == 0, k == KD - 1)
            m.then_inc(r_psum, 1)
            release(used[2])
            ffn(MOE_U0, DEPTH * 2 * FFN_UNITS, EXPERTS, n6 + 1, None)


def shape_constants():
    c = np.zeros((P, K_ALL), np.float32)
    q, k = np.arange(P)[:, None], np.arange(S)[None, :]
    c[:, K_ID:K_ID + 128] = np.eye(P)
    c[:, K_ONE:K_ONE + 128] = 1
    for t, (o, n) in enumerate(((0, P), (P, S))):
        d = (t * P + q) - k[:, :n]
        c[:, K_DIST + o:K_DIST + o + n] = np.where(d >= 0, -d, MASKED)
        c[:, K_MASK + o:K_MASK + o + n] = np.where(d >= 0, 0, MASKED)
    ends = np.arange(N_CMP) * CMP_STRIDE + CMP_BLOCK - 1
    b = np.zeros((P, 2, T, 4, 16), np.float32)
    for p in range(2):
        for t in range(T):
            for i in range(4):
                d = (t * P + q) - ends[None, :]
                b[:, p, t, i, :N_CMP] = np.where(d >= 0, -np.float32(SLOPES[2 * i + p]) * d.astype(np.float32), MASKED)
            c[:, K_VALID + t] = (t * P + np.arange(P)) >= CMP_BLOCK - 1
    c[:, K_CMPB:K_CMPB + 256] = b.reshape(P, 256)
    half = ROPE // 2
    inv = np.float32(10000.0) ** (-np.arange(half, dtype=np.float32) / half)
    ang = np.arange(S, dtype=np.float32)[:, None] * inv[None, :].astype(np.float32)
    for off, f in ((K_COS, np.cos), (K_SIN, np.sin)):
        v = np.tile(f(ang).astype(np.float32), (1, 2)).reshape(T, P, ROPE)
        c[:, off:off + 64] = v.transpose(1, 0, 2).reshape(P, 64)
    c[:, K_TRI:K_TRI + S] = (k >= q)
    c[:, K_TIE8:K_TIE8 + 64] = np.tril(np.ones((8, 8)), -1).reshape(1, 64)
    c[:, K_TIE4:K_TIE4 + 16] = np.tril(np.ones((4, 4)), -1).reshape(1, 16)
    return c


def kernel(**inputs):
    import concourse.bacc as bacc
    from concourse.bass_utils import run_bass_kernel_spmd

    a = {n: np.asarray(v) for n, v in inputs.items()}

    def rows(w):
        return w.reshape(w.shape[0] // P, P, w.shape[1]).transpose(1, 0, 2)

    units = np.zeros((ALL_UNITS, P, UNIT), np.float32)
    at = [0]

    def put(*parts):
        o = 0
        for p_ in parts:
            flat = p_.reshape(P, -1)
            units[at[0], :, o:o + flat.shape[1]] = flat
            o += flat.shape[1]
        at[0] += 1

    def put_ffn(gate, up, down):
        gu = np.concatenate([rows(gate), rows(up)], axis=2)
        put(gu, rows(down))

    def put_merge(wa, wb, wo, tail=None):
        ra, rb, ro = rows(wa), rows(wb), rows(wo)
        put(ra, rb[:, 0:2])
        put(rb[:, 2:4], ro[:, 0:4])
        put(ro[:, 4:8], *([] if tail is None else [rows(tail)]))

    splits = np.cumsum([512, 128, 128, 128, 128, 128, 128, 24, 384, 256, 32])
    for l in range(DEPTH):
        for f in range(FFN_UNITS):
            s_ = slice(f * F_UNIT, (f + 1) * F_UNIT)
            put_ffn(a["ffn1_gate"][l][:, s_], a["ffn1_up"][l][:, s_], a["ffn1_down"][l][s_])
        q, kc, vc, ks, vs, kw, vw, gn, cq, ckv, kr, gm = np.split(a["w_in"][l], splits, axis=1)
        w = rows(np.concatenate([cq, ckv, kr, gn, kc, vc, ks, kw, q, vs, vw], axis=1))
        g = rows(gm)
        put(w[:, :, 0:768])
        put(w[:, :, 768:1536])
        put(w[:, :, 1536:], rows(a["mla_w_uq"][l]))
        put(rows(a["mla_w_uk"][l]), rows(a["mla_w_uv"][l]), g[:, :, 0:512])
        put(g[:, :, 512:1280])
        put(g[:, :, 1280:2048])
        put_merge(a["w_branch_a"][l], a["w_branch_b"][l], a["w_out"][l])
        for f in range(FFN_UNITS):
            s_ = slice(f * F_UNIT, (f + 1) * F_UNIT)
            put_ffn(a["ffn2_gate"][l][:, s_], a["ffn2_up"][l][:, s_], a["ffn2_down"][l][s_])
    xi, cb, cc, q, k, v, fl, ga, gb = np.split(a["w_in_2"][0], np.cumsum([512] * 6 + [8, D]), axis=1)
    w = rows(np.concatenate([xi, cc, cb, q, k, v, fl, ga, gb], axis=1))
    for m in range(HYB_IN_UNITS):
        put(w[:, :, 768 * m:768 * (m + 1)])
    put_merge(a["w_out_conv_2"][0], a["w_out_attn_2"][0], a["w_o_2"][0],
              np.concatenate([a["w_router_group_2"][0], a["w_router_expert_2"][0]], axis=1))
    for e in range(EXPERTS):
        put_ffn(a["w_gate_2"][0, e], a["w_up_2"][0, e], a["w_down_2"][0, e])
    assert at[0] == ALL_UNITS
    stream = np.ascontiguousarray(units.reshape(ALL_UNITS, P, 3, BLK).transpose(0, 2, 1, 3))

    w_ada = np.concatenate([a["w_ada"].reshape(DEPTH, D, 3, 3 * D).transpose(0, 2, 1, 3).reshape(-1, D, 3 * D),
                            a["w_ada_2"][0].reshape(D, 2, 3 * D).transpose(1, 0, 2)], axis=0)
    ada = np.ascontiguousarray(w_ada.reshape(STAGES, P, KD, ADA_STEPS, ADA_COLS).transpose(0, 3, 1, 2, 4)
                               .reshape(STAGES * ADA_STEPS, P, KD, ADA_COLS))

    def cols(v):
        return v.reshape(-1, P).T

    vecs = np.zeros((P, V_ALL), np.float32)
    vecs[:, V_C:V_C + 8] = a["c"][0].reshape(P, KD)
    vecs[:, V_C + 8:V_C + 16] = a["c_2"][0].reshape(P, KD)
    vecs[:, V_BADA:V_BADA + STAGES * 24] = cols(np.concatenate([a["b_ada"].reshape(-1), a["b_ada_2"].reshape(-1)]))
    vecs[:, V_N1:V_N1 + 8] = cols(a["norm1_w_2"][0])
    vecs[:, V_N2:V_N2 + 8] = cols(a["norm2_w_2"][0])
    vecs[:, V_CONV:V_CONV + 12] = a["conv_w_2"][0].reshape(3, 4, P).transpose(2, 1, 0).reshape(P, 12)
    vecs[:, V_QN] = np.tile(a["q_norm_w_2"][0], 2)
    vecs[:, V_KN] = np.tile(a["k_norm_w_2"][0], 2)
    vecs[:, V_BF:V_BF + 8] = a["b_forget_2"][0][None, :]
    vecs[:, V_BR:V_BR + 36] = np.concatenate([a["b_router_group_2"][0], a["b_router_expert_2"][0]])[None, :]
    layer_vecs = np.zeros((DEPTH, P, L_ALL), np.float32)
    cmp_w1 = np.zeros((DEPTH, P, 2 * 2048), np.float32)
    for l in range(DEPTH):
        for k_, n in enumerate(("cmpk", "cmpv")):
            layer_vecs[l, :, L_PE + 32 * k_:L_PE + 32 * k_ + 32] = np.tile(a[n + "_pe"][l].T, (2, 1))
            layer_vecs[l, :, L_W2 + DH * k_:L_W2 + DH * k_ + DH] = np.tile(a[n + "_w2"][l], (2, 1))
            w1 = a[n + "_w1"][l].reshape(CMP_BLOCK, DH, DH).transpose(1, 0, 2).reshape(DH, 2048)
            cmp_w1[l, :, 2048 * k_:2048 * k_ + 2048] = np.tile(w1, (2, 1))
        layer_vecs[l, :, L_QN:L_QN + 3] = cols(a["mla_q_norm"][l])
        layer_vecs[l, :, L_KVN:L_KVN + 2] = cols(a["mla_kv_norm"][l])
    arrays = {
        "weight_stream": stream, "ada_steps": ada, "shape_constants": shape_constants(), "vectors": vecs,
        "layer_vectors": layer_vecs, "compress_w1": cmp_w1,
        "final_norm_rows": np.ascontiguousarray(np.broadcast_to(a["final_norm"], (P, D))),
        "tokens": np.ascontiguousarray(a["x"][0]),
    }
    nc = bacc.Bacc("TRN2", target_bir_lowering=False, num_devices=1)
    args = [nc.dram_tensor(n, v_.shape, mybir.dt.from_np(v_.dtype), kind="ExternalInput").ap() for n, v_ in arrays.items()]
    out = nc.dram_tensor("out", (S, D), F32, kind="ExternalOutput").ap()
    program(nc, *args, out)
    r = run_bass_kernel_spmd(nc, [arrays], core_ids=[0])
    return r.results[0]["out"].reshape(1, S, D)
```

```python
import numpy as np
from contextlib import ExitStack

import concourse.bass as bass
from concourse import mybir

F32 = mybir.dt.float32
F32R = mybir.dt.float32r
BF16 = mybir.dt.bfloat16
ALU = mybir.AluOpType
ACT = mybir.ActivationFunctionType
AX = mybir.AxisListType

P = 128
S = 256
T = S // P
D = 1024
KD = D // P
DEPTH = 2
HEADS = 8
DH = 64
GROUPS = 2
F_UNIT = 256
D_FF = 2816
FFN_UNITS = D_FF // F_UNIT
EXPERTS = 32
EXPERT_GROUPS = 4
PER_GROUP = EXPERTS // EXPERT_GROUPS
CMP_BLOCK, CMP_STRIDE = 32, 16
N_CMP = S // CMP_STRIDE - 1
Q_RANK, KV_RANK, ROPE, NOPE = 384, 256, 32, 64
QK = NOPE + ROPE
EPS = 1e-6
MASKED = -1e30

BLK = 2048
UNIT = 3 * BLK
MIX_IN_UNITS, MERGE_UNITS = 6, 3
LAYER_UNITS = 2 * FFN_UNITS + MIX_IN_UNITS + MERGE_UNITS
HYB_IN_UNITS = 7
HYB_U0 = DEPTH * LAYER_UNITS
MOE_U0 = HYB_U0 + HYB_IN_UNITS + MERGE_UNITS
MOE_F0 = DEPTH * 2 * FFN_UNITS
SPARSE = range(1, EXPERT_GROUPS)

IN_LINE, LAST_BEHIND = (0, 1, 2), (-1, 0, 4)

ADA_COLS = 256
ADA_STEPS = 3 * D // ADA_COLS
STAGES = 3 * DEPTH + 2

C_CQ, C_CKV, C_KR, C_GN, C_KC, C_KS, C_KW, C_Q, C_V = 0, 384, 640, 672, 696, 952, 1080, 1208, 1720
PROJ = C_V
MIX_COLS = 1976
U2_COLS = MIX_COLS - 2 * 768
UQ_OFF = 3520
HYB_QKV = 1536

K_ID, K_ONE, K_DIST, K_MASK, K_CMPB, K_COS, K_SIN, K_VALID, K_TRI, K_TIE8, K_TIE4, K_PLACE, K_BASE = np.cumsum(
    [0, 128, 128, 384, 384, 256, 64, 64, 2, 256, 64, 16, 128]).tolist()
K_ALL = K_BASE + EXPERT_GROUPS
V_C, V_BADA, V_N1, V_N2, V_CONV, V_QN, V_KN, V_BF, V_BR = np.cumsum(
    [0, 16, STAGES * 24, 8, 8, 12, 1, 1, 8]).tolist()
V_ALL = V_BR + 36
L_PE, L_W2, L_QN, L_KVN = 0, 32, 160, 163
L_ALL = 165

SLOPES = [2.0 ** (-8.0 * (h + 1) / HEADS) for h in range(HEADS)]
CHAIN_PER_LAYER = 64


def program(nc, stream, experts, ada, consts, vecs, layer_vecs, cmp_w1, fnorm, x_in, out):
    ctx = ExitStack()
    with ctx:
        def sb(name, shape, dt=F32):
            return ctx.enter_context(nc.sbuf_tensor(name, shape, dt))

        def sem(name):
            return ctx.enter_context(nc.semaphore(name))

        raw = sb("raw", [P, UNIT])
        w_hi = sb("w_hi", [P, UNIT], F32R)
        w_lo = sb("w_lo", [P, UNIT], F32R)
        x = sb("x", [P, T, D])
        uT_hi = sb("uT_hi", [P, KD, S], F32R)
        uT_lo = sb("uT_lo", [P, KD, S], F32R)
        gate_bc = sb("gate_bc", [P, D])
        ada_w = sb("ada_w", [P, 2, KD, ADA_COLS])
        ada_sum = sb("ada_sum", [P, ADA_COLS])
        cst = sb("cst", [P, K_ALL])
        vec = sb("vec", [P, V_ALL])
        c_act = sb("c_act", [P, 16])
        lvec = sb("lvec", [P, L_ALL])
        modf = sb("modf", [P, 24])
        stat = sb("stat", [P, 112])
        zeros = sb("zeros", [P, 512], BF16)
        cmpw = sb("cmpw", [P, 2, 2048])
        expert_base = sb("expert_base", [P, EXPERT_GROUPS], mybir.dt.int32)
        r_arena = sb("r_arena", [P, 4096], F32R)
        arena = sb("arena", [P, 11776])

        def at(off, *shape, parts=P):
            n = int(np.prod(shape))
            v = arena[0:parts, off:off + n]
            if len(shape) == 2:
                return v.rearrange("p (a b) -> p a b", a=shape[0])
            if len(shape) == 3:
                return v.rearrange("p (a b c) -> p a b c", a=shape[0], b=shape[1])
            if len(shape) == 4:
                return v.rearrange("p (a b c d) -> p a b c d", a=shape[0], b=shape[1], c=shape[2])
            return v

        def rat(off, a, b):
            return r_arena[:, off:off + a * b].rearrange("p (a b) -> p a b", a=a)

        ident = cst[:, K_ID:K_ID + 128]
        ones = cst[:, K_ONE:K_ONE + 128]
        dist = [cst[:, K_DIST:K_DIST + 128], cst[:, K_DIST + 128:K_DIST + 384]]
        mask = [cst[:, K_MASK:K_MASK + 128], cst[:, K_MASK + 128:K_MASK + 384]]
        cmp_bias = cst[:, K_CMPB:K_CMPB + 256].rearrange("p (a q i n) -> p a q i n", a=2, q=2, i=4)
        cos2 = cst[:, K_COS:K_COS + 64].rearrange("p (t r) -> p t r", t=T)
        sin2 = cst[:, K_SIN:K_SIN + 64].rearrange("p (t r) -> p t r", t=T)
        cmp_valid = cst[:, K_VALID:K_VALID + 2]
        tri = cst[:, K_TRI:K_TRI + 256]
        tie8 = cst[:, K_TIE8:K_TIE8 + 64].rearrange("p (a b) -> p a b", a=8)
        tie4 = cst[:, K_TIE4:K_TIE4 + 16].rearrange("p (a b) -> p a b", a=4)

        ss, ms, sq, rstd = stat[:, 0:2], stat[:, 2:4], stat[:, 4:6], stat[:, 6:8]
        lss, lms, lsq, lrs = stat[:, 8:12], stat[:, 12:16], stat[:, 16:20], stat[:, 20:24]
        nmax = [stat[:, 24:28], stat[:, 28:32]]
        psum_row = [stat[:, 96 + 4 * i:100 + 4 * i] for i in range(4)]
        pad = stat[:, 32:33]
        rsum, coef = stat[:, 40:44], stat[:, 44:48]
        cmax, csum, crec, ccoef = (at(11136, 16), at(11152, 16), at(11168, 16), at(11184, 16))
        nsa_gate = stat[:, 48:96].rearrange("p (t h k) -> p t h k", t=T, h=HEADS)

        xn, uTf, diag = at(0, T, D), at(2048, KD, S), at(4096, KD, P)
        first_w = [ada_w[:, 0], ada_w[:, 1]] + [at(5120 + i * KD * ADA_COLS, KD, ADA_COLS) for i in range(3)]
        act_g, hid = at(6144, T, F_UNIT), at(6656, T, F_UNIT)
        hT_hi, hT_lo = rat(0, 2, S), rat(512, 2, S)
        upd = at(2048, T, 2, 512)
        proj = at(0, T, PROJ)
        vsw = at(4096, T, 256)
        qT = at(4608, 4, S)
        kT = [at(5632, 2, S), at(6144, 2, S)]
        cT = at(9728, 2 * GROUPS, S)
        blocks = at(7168, 2 * GROUPS, CMP_STRIDE, N_CMP)
        p_cmp = at(7168, 16, 32)
        pT_cmp = at(7680, 4, P)
        hid_cmp, kT_cmp, v_cmp = at(8128, 2, 16), at(8192 + 96, 2, 16), at(8192 + 128, 2, DH)
        vm = at(8704, T, HEADS * DH)
        o_a, o_b = at(9728, T, 512), at(10752, T, 512)
        o_tmp = at(10752, 4, DH)
        lat_squares = at(9728, T, Q_RANK + KV_RANK)
        q_tok, k_tok = at(0, T, HEADS, QK), at(1536, T, HEADS, QK)
        rope_a, rope_b = at(9728, T, HEADS, ROPE), at(9728 + 512, T, HEADS, ROPE)
        kr_a, kr_b = at(10752, T, ROPE), at(10816, T, ROPE)
        qkT_m = cmpw[:, :, :].rearrange("p k (h s) -> p k h s", h=HEADS)
        scores = [at(0, 2, 2, S), at(1024, 2, 2, S)]
        pT = [at(2048, 2, 4, P), at(3072, 2, 4, P)]
        gates_m = [at(6656, T, 512), at(7680, T, 512), at(4096, T, 512), at(5120, T, 512)]
        y, ytmp = at(0, T, D), at(2048, T, 2, 512)
        cqT_hi, cqT_lo = rat(0, 5, S), rat(1280, 5, S)
        oT_hi = [rat(0, 4, S), rat(2048, 4, S)]
        oT_lo = [rat(1024, 4, S), rat(3072, 4, S)]
        yT_hi, yT_lo = rat(0, 8, S), rat(2048, 8, S)
        fn_bc = at(8192, D)
        xcb = at(0, T, 1536)
        qkv = at(4096, T, HYB_QKV)
        gates_h = at(7168, T, 2 * D)
        gate_sets_h = [gates_h[:, :, i * 512:(i + 1) * 512] for i in range(4)]
        f_row = at(11264, T, 8)
        f_e, f_l, f_cum = at(11280, T, 8), at(11296, T, 8), at(11312, T, 8)
        nlogf = at(11328, T, 8)
        qk_ss, qk_gain = at(11344, 32), at(11376, 4)
        qT_h = cmpw[:, 0, 0:1024].rearrange("p (c s) -> p c s", c=4)
        kT_h = cmpw[:, 0, 1024:2048].rearrange("p (c s) -> p c s", c=4)
        u_tok = cmpw[:, 1, 0:1024].rearrange("p (t s) -> p t s", t=T)
        squares = cmpw[:, 1, 1024:2048].rearrange("p (t s) -> p t s", t=T)
        uTc = at(0, 4, S + 2)
        conv = at(1056, 4, S)
        o_h = qkv[:, :, 0:512]
        r0 = 8192
        logits = at(r0, T, 36)
        g_gt, g_eq = at(r0 + 128, T, 4, 4), at(r0 + 160, T, 4, 4)
        g_rank, g_sel = at(r0 + 192, T, 4), at(r0 + 200, T, 4)
        g_max, g_exp, g_sum, p_sel = at(r0 + 208, T), at(r0 + 212, T, 4), at(r0 + 220, T), at(r0 + 224, T)
        le_m, le_g = at(r0 + 256, T, 4, 8), at(r0 + 320, T, 8)
        e_gt, e_eq = at(r0 + 384, T, 8, 8), at(r0 + 512, T, 8, 8)
        e_rank, e_max, e_exp, e_sum, e_w = (at(r0 + 640, T, 8), at(r0 + 656, T), at(r0 + 660, T, 8),
                                            at(r0 + 676, T), at(r0 + 680, T, 8))
        g_cum, g_total, g_place = at(r0 + 720, T, 4), at(r0 + 728, T, 4), at(r0 + 736, T, 4)
        own_cum, by_rank, g_base_in, g_base = at(r0 + 744, T), at(r0 + 748, 4, 4), at(r0 + 764, 4, 4), at(r0 + 780, 4)
        member_in, member, place = at(r0 + 784, T, 4, 4), at(r0 + 816, T, 4), at(r0 + 824, T, 4)
        dense_w, sparse_w = at(r0 + 832, T, PER_GROUP), at(r0 + 848, 3, PER_GROUP)
        pick, pick_T = at(9216, T, 3, P), at(9984, 3, S)
        usf = [at(2048, KD, P), at(4096, KD, P), at(5120, KD, P)]
        us_hi = [rat(1024, KD, P)] + [uT_hi[:, :, i * P:(i + 1) * P] for i in range(T)]
        us_lo = [rat(2048, KD, P)] + [uT_lo[:, :, i * P:(i + 1) * P] for i in range(T)]
        hTs_hi, hTs_lo = rat(0, 2, P), rat(512, 2, P)
        y_s = [at(0, D), at(1024, D), at(4096, D)]
        group_iota = cst[:, K_BASE:K_BASE + EXPERT_GROUPS]
        place_iota = cst[:, K_PLACE:K_PLACE + P]

        bank = [ctx.enter_context(nc.psum_tensor(f"bank{i}", [P, 512], F32)) for i in range(8)]
        ACC, GU, HT, MOD = bank[0:4], bank[4:6], bank[6], bank[7]
        YT = [bank[4], bank[5], bank[6], bank[3]]
        SPREAD = [bank[2], bank[3], bank[5], bank[7]]

        landed = [sem(f"block_landed{r}") for r in range(3)]
        hi_done, split_done = sem("blocks_hi"), sem("blocks_split")
        used = [sem(f"block_used{j}") for j in range(3)]
        x_landed, cst_landed, fn_landed = sem("x_landed"), sem("cst_landed"), sem("fn_landed")
        lvec_landed, out_landed = sem("lvec_landed"), sem("out_landed")
        ada_landed = [sem("ada_landed0"), sem("ada_landed1")]
        first_landed = [sem(f"first_landed{i}") for i in range(5)]
        c_ready, ada_chain, ada_ready = sem("c_ready"), sem("ada_chain"), sem("ada_ready")
        mod_step, mod_ready = sem("mod_step"), sem("mod_ready")
        x_ready, ss_done, ms_done, sq_done = sem("x_ready"), sem("ss_done"), sem("ms_done"), sem("sq_done")
        rstd_done, xn_done = sem("rstd_done"), sem("xn_done")
        diag_done, gate_psum, gate_ready = sem("diag_done"), sem("gate_psum"), sem("gate_ready")
        uT_psum, uTf_done_a, uTf_done_v = sem("uT_psum"), sem("uTf_done_a"), sem("uTf_done_v")
        uT_hi_done, uT_ready = sem("uT_hi_done"), sem("uT_ready")
        gu0_done, silu_done, h_done = sem("gu0_done"), sem("silu_done"), sem("h_done")
        hT_psum, hT_hi_done, hT_ready = sem("hT_psum"), sem("hT_hi_done"), sem("hT_ready")
        chain = sem("vector_chain")
        w_done, w_evac_a, w_evac_v = sem("w_done"), sem("w_evac_a"), sem("w_evac_v")
        lat_ss, lat_ms, lat_sq, lat_ready = sem("lat_ss"), sem("lat_ms"), sem("lat_sq"), sem("lat_ready")
        nsa_gate_ready = sem("nsa_gate_ready")
        cqT_psum, cqT_hi_done, cqT_ready = sem("cqT_psum"), sem("cqT_hi_done"), sem("cqT_ready")
        q_psum, ks_psum, kw_psum, c_psum = sem("q_psum"), sem("ks_psum"), sem("kw_psum"), sem("c_psum")
        q_ready, ks_ready, kw_ready, blocks_ready = sem("q_ready"), sem("ks_ready"), sem("kw_ready"), sem("blocks_ready")
        hidc_psum, hidc_ready, kvc_psum, kvc_ready = sem("hidc_psum"), sem("hidc_ready"), sem("kvc_psum"), sem("kvc_ready")
        uq_psum, uk_psum, uv_psum = sem("uq_psum"), sem("uk_psum"), sem("uv_psum")
        uq_copied, uk_copied, uv_ready, rope_done = sem("uq_copied"), sem("uk_copied"), sem("uv_ready"), sem("rope_done")
        qm_psum, km_psum, qm_ready, km_ready = sem("qm_psum"), sem("km_psum"), sem("qm_ready"), sem("km_ready")
        cs_psum, cs_ready, cp_exp, cp_psum, cp_ready, co_psum, co_done = (
            sem("cs_psum"), sem("cs_ready"), sem("cp_exp"), sem("cp_psum"), sem("cp_ready"), sem("co_psum"), sem("co_done"))
        sc_done, bias_done, nmax_done, exp_done = sem("sc_done"), sem("bias_done"), sem("nmax_done"), sem("exp_done")
        pt_psum, pt_copied_a, pt_copied_v, pv_done, o_done = (
            sem("pt_psum"), sem("pt_copied_a"), sem("pt_copied_v"), sem("pv_done"), sem("o_done"))
        oT_psum, oT_hi_done, oT_ready = sem("oT_psum"), sem("oT_hi_done"), sem("oT_ready")
        pa_psum, ya_done, pb_psum, y_ready = sem("pa_psum"), sem("ya_done"), sem("pb_psum"), sem("y_ready")
        yT_psum, yT_hi_done, yT_ready = sem("yT_psum"), sem("yT_hi_done"), sem("yT_ready")
        u_ready, uc_psum, uc_ready, b_psum, ya_f32, ya_hi_done = (
            sem("u_ready"), sem("uc_psum"), sem("uc_ready"), sem("b_psum"), sem("ya_f32"), sem("ya_hi_done"))
        f_exp, f_exp_in, f_ln, f_ln_in, logf_ready, fcum_psum, fcum_ready = (
            sem("f_exp"), sem("f_exp_in"), sem("f_ln"), sem("f_ln_in"), sem("logf_ready"), sem("fcum_psum"), sem("fcum_ready"))
        qkn_ms, qkn_sq, qkn_ready, kh_psum, kh_ready = (
            sem("qkn_ms"), sem("qkn_sq"), sem("qkn_ready"), sem("kh_psum"), sem("kh_ready"))
        r_psum, r_exp_in, r_exp = sem("r_psum"), sem("r_exp_in"), sem("r_exp")
        sel_ready, count_psum, base_ready, pick_ready = sem("sel_ready"), sem("count_psum"), sem("base_ready"), sem("pick_ready")
        ew_ready, pick_T_psum, pick_T_ready = sem("ew_ready"), sem("pick_T_psum"), sem("pick_T_ready")
        us_psum, usf_done_a, usf_done_v, us_hi_done, us_ready = (
            sem("us_psum"), sem("usf_done_a"), sem("usf_done_v"), sem("us_hi_done"), sem("us_ready"))
        ys_psum, ys_ready, spread_done = sem("ys_psum"), sem("ys_ready"), sem("spread_done")
        first_ready = sem("first_ready")
        first_tile = sem("first_tile")

        NSA_JOBS = [(k, qt, g) for k in (0, 1) for qt in (1, 0) for g in (0, 1)]
        MLA_JOBS = [(2, qt, g) for qt in (1, 0) for g in (0, 1)]
        JOBS = NSA_JOBS + MLA_JOBS
        HYB_JOBS = [(3, qt, g) for qt in (1, 0) for g in (0, 1)]
        NJ = len(JOBS)
        K_BANKS = (5, 6, 4, 5)
        GATE_CHUNKS = [[(j // 3, k) for k in ((0, 1, 2), (3, 4, 5), (6, 7))[j % 3]] for j in range(NJ)]
        JOB_SPLITS = {0: (4, 0), 2: (4, 1), 3: (4, 2), 5: (5, 0), 6: (5, 1), 8: (5, 2), 9: (6, 0), 11: (6, 1)}

        def gate_place(i, k):
            at_ = 3 * UNIT + BLK + (i * KD + k) * 512
            return at_ // UNIT, at_ % UNIT
        GATHERS = [(2, 4), (0, 0), (1, 2)]

        def f32(ap):
            return ap.bitcast(F32)

        block = ctx.enter_context(nc.Block())

        @block.sync
        def _(sp):
            sp.dma_start(cst[:, :], consts).then_inc(cst_landed, 16)
            sp.dma_start(vec[:, :], vecs).then_inc(cst_landed, 16)
            for st in range(ADA_STEPS):
                slot = st % len(first_w)
                if st >= len(first_w):
                    sp.wait_ge(mod_step, st - len(first_w) + 2)
                sp.dma_start(first_w[slot], ada[st]).then_inc(first_landed[slot], 16)
                if st == 1:
                    sp.dma_start(x[:, :, :], x_in.rearrange("(t p) d -> p t d", p=P)).then_inc(x_landed, 16)
                if st >= ADA_STEPS - 3:
                    j = st - (ADA_STEPS - 3)
                    sp.dma_start(raw[:, j * BLK:(j + 1) * BLK], stream[j]).then_inc(landed[j], 16)
            with sp.Fori(1, MOE_U0) as i:
                for r in range(3):
                    sp.wait_ge(split_done, i * 3 + r - 2)
                    sp.dma_start(raw[:, r * BLK:(r + 1) * BLK], stream[i * 3 + r]).then_inc(landed[r], 16)
            sp.wait_ge(base_ready, 1)
            bases = [sp.value_load(expert_base[0:1, s:s + 1], min_val=0, max_val=3 * (EXPERTS - PER_GROUP)) for s in range(EXPERT_GROUPS)]

            def load(s, i, j, order=LAST_BEHIND):
                at_ = (s * PER_GROUP + i + MOE_U0) * 3 + order[j]
                r = (order[j] + 3) % 3
                sp.wait_ge(split_done, at_ - 2)
                sp.dma_start(raw[:, r * BLK:(r + 1) * BLK], experts[bases[s] + (i * 3 + j)]).then_inc(landed[r], 16)

            for s in range(EXPERT_GROUPS):
                load(s, 0, 0, LAST_BEHIND if s else IN_LINE)
                load(s, 0, 1, LAST_BEHIND if s else IN_LINE)
                if s:
                    load(s - 1, PER_GROUP - 1, 2)
                with sp.Fori(1, PER_GROUP) as i:
                    load(s, i, 0)
                    load(s, i, 1)
                    load(s, i - 1, 2)
            load(EXPERT_GROUPS - 1, PER_GROUP - 1, 2, IN_LINE)
            sp.wait_ge(x_ready, 2 * (3 * DEPTH + 5))
            sp.dma_start(out.rearrange("(t p) d -> p t d", p=P), x[:, :, :]).then_inc(out_landed, 16)
            sp.wait_ge(out_landed, 16)

        @block.gpsimd
        def _(pool):
            first_pair = ADA_STEPS // 2

            def load(n, slot):
                pool.dma_start(ada_w[:, slot], ada[n]).then_inc(ada_landed[slot], 16)

            def step(pair, slot, c0, ahead):
                n = pair * 2 + slot
                w = ada_w[:, slot]
                done = (pair - first_pair) * 2 + slot
                pool.wait_ge(ada_landed[slot], (pair - first_pair) * 16 + 16)
                nc.gpsimd.tensor_tensor(w, w, c_act[:, c0:c0 + 8].unsqueeze(2).to_broadcast([P, KD, ADA_COLS]),
                                        ALU.mult).then_inc(ada_chain, 1)
                pool.wait_ge(ada_chain, done * 3 + 1)
                nc.gpsimd.tensor_tensor(w[:, 0:4], w[:, 0:4], w[:, 4:8], ALU.add).then_inc(ada_chain, 1)
                pool.wait_ge(ada_chain, done * 3 + 2)
                nc.gpsimd.tensor_tensor(w[:, 0:2], w[:, 0:2], w[:, 2:4], ALU.add).then_inc(ada_chain, 1)
                pool.wait_ge(ada_chain, done * 3 + 3)
                pool.wait_ge(mod_step, n + 1)
                nc.gpsimd.tensor_tensor(ada_sum[:, :], w[:, 0], w[:, 1], ALU.add).then_inc(ada_ready, 1)
                if ahead:
                    pool.wait_ge(ada_ready, done + 1)
                    load(n + 2, slot)

            pool.wait_ge(mod_step, ADA_STEPS + 1)
            load(ADA_STEPS, 0)
            load(ADA_STEPS + 1, 1)
            pool.wait_ge(c_ready, 1)
            c2_pair, end_pair = DEPTH * 3 * ADA_STEPS // 2, STAGES * ADA_STEPS // 2
            with pool.Fori(first_pair, c2_pair) as pair:
                for slot in range(2):
                    step(pair, slot, 0, True)
            with pool.Fori(c2_pair, end_pair - 1) as pair:
                for slot in range(2):
                    step(pair, slot, 8, True)
            for slot in range(2):
                step(end_pair - 1, slot, 8, False)

        @block.scalar
        def _(act):
            def split(u, js, order=IN_LINE):
                for j in js:
                    r = (order[j] + 3) % 3
                    act.wait_ge(landed[r], (u + (order[j] - r) // 3) * 16 + 16)
                    act.wait_ge(used[j], u + 1)
                    act.activation(w_hi[:, j * BLK:(j + 1) * BLK], raw[:, r * BLK:(r + 1) * BLK], ACT.Copy).then_inc(hi_done, 1)

            def rms_squares(q, late=None):
                for t in range(T):
                    act.wait_ge(x_ready, 2 * q + t + 1)
                    act.activation(xn[:, t], x[:, t], ACT.Square, accum_out=ss[:, t:t + 1]).then_inc(ss_done, 1)
                    act.wait_ge(ms_done, 2 * q + t + 1)
                    act.activation(sq[:, t:t + 1], ms[:, t:t + 1], ACT.Sqrt).then_inc(sq_done, 1)
                    if late is not None:
                        split(late, (t,))

            def norm(q, n, late=None):
                rms_squares(q, late)
                act.wait_ge(mod_ready, n + 1)
                for b in range(4):
                    if b % 2 == 0:
                        act.wait_ge(uT_psum, 4 * n + b + 2)
                        for k in (2 * b + 2, 2 * b + 3):
                            e = act.activation(uTf[:, k], ACC[b + 1][:, (k % 2) * S:(k % 2) * S + S], ACT.Identity,
                                               scale=modf[:, 8 + k:9 + k], bias=modf[:, k:k + 1])
                        e.then_inc(uTf_done_a, 1)
                        act.wait_ge(uTf_done_v, 2 * n + b // 2 + 1)
                    else:
                        act.wait_ge(uTf_done_a, 2 * n + b // 2 + 1)
                    act.activation(uT_hi[:, 2 * b:2 * b + 2], uTf[:, 2 * b:2 * b + 2], ACT.Copy).then_inc(uT_hi_done, 1)
                for h, g in enumerate((HT, GU[1])):
                    act.wait_ge(gate_psum, 2 * n + h + 1)
                    act.activation(gate_bc[:, h * 512:(h + 1) * 512], g[:, :], ACT.Copy).then_inc(gate_ready, 1)

            def silu(u, f):
                act.wait_ge(gu0_done, f + 1)
                act.activation(act_g[:, 0], GU[0][:, 0:F_UNIT], ACT.Silu).then_inc(silu_done, 1)
                act.wait_ge(used[1], u + 2)
                act.activation(act_g[:, 1], GU[1][:, 0:F_UNIT], ACT.Silu).then_inc(silu_done, 1)

            def h_split(f):
                act.wait_ge(hT_psum, f + 1)
                act.activation(hT_hi[:, :, :], HT[:, :].rearrange("p (f s) -> p f s", f=2), ACT.Copy).then_inc(hT_hi_done, 1)

            def ffn(u0, f0, n):
                split(u0 + 1, (0,), LAST_BEHIND)
                silu(u0, f0)
                split(u0 + 1, (1,), LAST_BEHIND)
                split(u0, (2,), LAST_BEHIND)
                with act.Fori(1, n) as i:
                    h_split(f0 + i - 1)
                    split(u0 + i + 1, (0,), LAST_BEHIND)
                    silu(u0 + i, f0 + i)
                    split(u0 + i + 1, (1,), LAST_BEHIND)
                    split(u0 + i, (2,), LAST_BEHIND)
                h_split(f0 + n - 1)

            def merge(u0, m):
                split(u0, (2,))
                split(u0 + 1, (0, 1, 2))
                split(u0 + 2, (0,))
                for b in range(4):
                    act.wait_ge(yT_psum, 4 * m + b + 1)
                    act.activation(yT_hi[:, 2 * b:2 * b + 2], YT[b][:, :].rearrange("p (k s) -> p k s", k=2), ACT.Copy).then_inc(yT_hi_done, 1)
                split(u0 + 2, (1, 2))

            def job_exp(j0, jobs, j):
                kind, qt, g = jobs[j]
                nk = (qt + 1) * P
                sc = scores[j % 2]
                act.wait_ge(nmax_done, j0 + j + 1)
                for h in range(4):
                    v = sc[:, h // 2, h % 2, 0:nk]
                    e = act.activation(v, v, ACT.Exp, bias=nmax[j % 2][:, h:h + 1], accum_out=psum_row[j % 4][:, h:h + 1])
                e.then_inc(exp_done, 1)

            def jobs_run(j0, jobs, beside=lambda j: None):
                job_exp(j0, jobs, 0)
                for j, (kind, qt, g) in enumerate(jobs):
                    beside(j)
                    act.wait_ge(pt_psum, j0 + j + 1)
                    if j >= 2:
                        act.wait_ge(pv_done, j0 + j - 1)
                    act.activation(pT[j % 2][:, 0], bank[4][:, :].rearrange("p (h q) -> p h q", h=4), ACT.Copy).then_inc(pt_copied_a, 1)
                    if j + 1 < len(jobs):
                        job_exp(j0, jobs, j + 1)

            act.wait_ge(cst_landed, 32)
            act.activation(c_act[:, :], vec[:, V_C:V_C + 16], ACT.Silu).then_inc(c_ready, 1)
            for j in range(2):
                act.wait_ge(landed[j], 16)
                act.activation(w_hi[:, j * BLK:(j + 1) * BLK], raw[:, j * BLK:(j + 1) * BLK], ACT.Copy).then_inc(hi_done, 1)

            with act.Fori(0, DEPTH) as l:
                u_mix = l * LAYER_UNITS + FFN_UNITS
                act.wait_ge(x_ready, l * 6 + 2)
                act.dma_start(lvec[:, :], layer_vecs[l]).then_inc(lvec_landed, 16)
                act.dma_start(cmpw[:, :, 0:CMP_STRIDE * DH], cmp_w1[l]).then_inc(lvec_landed, 16)
                norm(l * 3, l * 3)
                ffn(l * LAYER_UNITS, l * 2 * FFN_UNITS, FFN_UNITS)

                norm(l * 3 + 1, l * 3 + 1)
                split(u_mix, (2,))
                split(u_mix + 1, (0, 1))
                act.wait_ge(w_done, l * 7 + 1)
                act.activation(proj[:, 0, 0:512], bank[0][:, :], ACT.Copy).then_inc(w_evac_a, 1)
                act.activation(proj[:, :, 512:768], bank[2][:, :].rearrange("p (t c) -> p t c", t=T), ACT.Copy).then_inc(w_evac_a, 1)
                split(u_mix + 1, (2,))
                act.wait_ge(w_evac_a, l * 9 + 2)
                act.wait_ge(w_evac_v, l * 3 + 1)
                for t in range(T):
                    act.activation(lat_squares[:, t, 0:Q_RANK], proj[:, t, C_CQ:C_CKV], ACT.Square, accum_out=lss[:, t:t + 1]).then_inc(lat_ss, 1)
                    act.activation(lat_squares[:, t, Q_RANK:], proj[:, t, C_CKV:C_KR], ACT.Square, accum_out=lss[:, 2 + t:3 + t]).then_inc(lat_ss, 1)
                act.wait_ge(lat_ms, l + 1)
                act.activation(lsq, lms, ACT.Sqrt).then_inc(lat_sq, 1)
                act.activation(nsa_gate.rearrange("p t h k -> p t (h k)"), proj[:, :, C_GN:C_KC], ACT.Sigmoid).then_inc(nsa_gate_ready, 1)
                split(u_mix + 2, (0, 1))
                act.wait_ge(w_done, l * 7 + 2)
                act.activation(proj[:, 0, 768:1280], bank[3][:, :], ACT.Copy).then_inc(w_evac_a, 1)
                act.activation(proj[:, :, 1280:1536], bank[5][:, :].rearrange("p (t c) -> p t c", t=T), ACT.Copy).then_inc(w_evac_a, 1)
                split(u_mix + 2, (2,))
                act.wait_ge(w_done, l * 7 + 3)
                act.activation(proj[:, 0, 1536:PROJ], bank[0][:, 0:184], ACT.Copy)
                act.activation(vsw[:, 0], bank[0][:, 184:440], ACT.Copy).then_inc(w_evac_a, 1)
                split(u_mix + 3, (0,))
                act.wait_ge(lvec_landed, l * 32 + 32)
                for b, cs in enumerate(((0, 1), (2, 3), (4,))):
                    act.wait_ge(cqT_psum, l * 3 + b + 1)
                    for i, c in enumerate(cs):
                        e = act.activation(cqT_hi[:, c], bank[2 + b][:, i * S:(i + 1) * S], ACT.Copy,
                                           scale=lvec[:, L_QN + c:L_QN + c + 1])
                    e.then_inc(cqT_hi_done, 1)
                for b in range(2):
                    act.wait_ge(q_psum, l * 2 + b + 1)
                    act.activation(qT[:, 2 * b:2 * b + 2], bank[5 + b][:, :].rearrange("p (c s) -> p c s", c=2), ACT.Copy,
                                   scale=DH ** -0.5).then_inc(q_ready, 1)
                act.wait_ge(ks_psum, l + 1)
                act.activation(kT[0][:, :, :], bank[0][:, :].rearrange("p (g s) -> p g s", g=2), ACT.Copy).then_inc(ks_ready, 1)
                act.wait_ge(hidc_psum, l + 1)
                act.activation(hid_cmp[:, :, 0:N_CMP], bank[4][:, 0:32].rearrange("p (k n) -> p k n", k=2)[:, :, 0:N_CMP],
                               ACT.Gelu_apprx_tanh).then_inc(hidc_ready, 1)
                act.wait_ge(cs_ready, l + 1)
                act.activation(p_cmp[:, :, 0:N_CMP], p_cmp[:, :, 0:N_CMP], ACT.Exp).then_inc(cp_exp, 1)
                for b in range(4):
                    act.wait_ge(uq_psum, l * 4 + b + 1)
                    act.activation(q_tok[:, b // 2, 4 * (b % 2):4 * (b % 2) + 4].rearrange("p h c -> p (h c)"), bank[b][:, 0:384],
                                   ACT.Copy).then_inc(uq_copied, 1)
                act.wait_ge(cp_psum, l + 1)
                act.activation(pT_cmp[:, :, :], bank[6][:, :].rearrange("p (a q) -> p a q", a=4), ACT.Copy).then_inc(cp_ready, 1)
                split(u_mix + 3, (1, 2))
                for b in range(4):
                    act.wait_ge(qm_psum, l * 4 + b + 1)
                    act.activation(qkT_m[0:QK, 0, 2 * b:2 * b + 2], bank[b][0:QK, :].rearrange("p (h s) -> p h s", h=2),
                                   ACT.Copy).then_inc(qm_ready, 1)

                def beside(j):
                    if j in JOB_SPLITS:
                        m, b = JOB_SPLITS[j]
                        split(u_mix + m, (b,))
                    if j % 3 == 2:
                        act.wait_ge(w_done, l * 7 + 4 + j // 3)
                        if j // 3 == 2:
                            act.wait_ge(pv_done, l * NJ + len(NSA_JOBS))
                        for t in range(T):
                            e = act.activation(gates_m[j // 3][:, t], bank[2 + t][:, :], ACT.Sigmoid)
                        e.then_inc(w_evac_a, 1)

                jobs_run(l * NJ, JOBS, beside)
                for b in range(4):
                    act.wait_ge(oT_psum, l * 4 + b + 1)
                    act.activation(oT_hi[b // 2][:, 2 * (b % 2):2 * (b % 2) + 2], bank[3 + b][:, :].rearrange("p (c s) -> p c s", c=2),
                                   ACT.Copy).then_inc(oT_hi_done, 1)
                merge(u_mix + MIX_IN_UNITS, l)

                norm(l * 3 + 2, l * 3 + 2, late=u_mix + MIX_IN_UNITS + MERGE_UNITS)
                ffn(l * LAYER_UNITS + FFN_UNITS + MIX_IN_UNITS + MERGE_UNITS, l * 2 * FFN_UNITS + FFN_UNITS, FFN_UNITS)

            q6, n6 = 3 * DEPTH, 3 * DEPTH
            act.wait_ge(x_ready, 2 * q6 + 2)
            act.dma_start(fn_bc, fnorm).then_inc(fn_landed, 16)
            rms_squares(q6)
            norm(q6 + 1, n6)
            u = HYB_U0
            split(u, (2,))
            for m in range(HYB_IN_UNITS):
                if m + 1 < HYB_IN_UNITS:
                    split(u + m + 1, (0, 1))
                act.wait_ge(w_done, DEPTH * 7 + m + 1)
                b0, n2 = 3 * (m % 2), 256 if m < 6 else 8
                if m < 4:
                    dst, c0 = (xcb, 768 * m) if m < 2 else (qkv, 768 * (m - 2))
                    act.activation(dst[:, 0, c0:c0 + 512], bank[b0][:, :], ACT.Copy).then_inc(w_evac_a, 1)
                    act.activation(dst[:, :, c0 + 512:c0 + 768], bank[b0 + 2][:, :].rearrange("p (t c) -> p t c", t=T),
                                   ACT.Copy).then_inc(w_evac_a, 1)
                elif m == 4:
                    for t in range(T):
                        act.activation(f_row[:, t], bank[b0 + t][:, 0:8], ACT.Copy)
                        act.activation(gates_h[:, t, 0:504], bank[b0 + t][:, 8:512], ACT.Sigmoid)
                    act.activation(gates_h[:, :, 504:760], bank[b0 + 2][:, :].rearrange("p (t c) -> p t c", t=T),
                                   ACT.Sigmoid).then_inc(w_evac_a, 1)
                else:
                    c0 = 760 + 768 * (m - 5)
                    for t in range(T):
                        act.activation(gates_h[:, t, c0:c0 + 512], bank[b0 + t][:, :], ACT.Sigmoid)
                    act.activation(gates_h[:, :, c0 + 512:c0 + 512 + n2],
                                   bank[b0 + 2][:, 0:2 * n2].rearrange("p (t c) -> p t c", t=T), ACT.Sigmoid).then_inc(w_evac_a, 1)
                if m + 1 < HYB_IN_UNITS:
                    split(u + m + 1, (2,))
            act.wait_ge(qkn_ms, 1)
            act.activation(qk_ss, qk_ss, ACT.Sqrt).then_inc(qkn_sq, 1)
            act.wait_ge(f_exp_in, 1)
            act.activation(f_e[:, :, :], f_e[:, :, :], ACT.Exp).then_inc(f_exp, 1)
            act.wait_ge(f_ln_in, 1)
            act.activation(f_l[:, :, :], f_l[:, :, :], ACT.Ln).then_inc(f_ln, 1)
            for b in range(2):
                act.wait_ge(ya_f32, b + 1)
                act.activation(oT_hi[0][:, 2 * b:2 * b + 2], conv[:, 2 * b:2 * b + 2], ACT.Copy).then_inc(ya_hi_done, 1)
            for b in range(2):
                act.wait_ge(q_psum, DEPTH * 2 + b + 1)
                act.activation(qT_h[:, 2 * b:2 * b + 2], bank[b][:, :].rearrange("p (c s) -> p c s", c=2), ACT.Copy,
                               scale=qk_gain[:, 0:1]).then_inc(q_ready, 1)
            for b in range(2):
                act.wait_ge(kh_psum, b + 1)
                act.activation(kT_h[:, 2 * b:2 * b + 2], bank[2 + 2 * b][:, :].rearrange("p (c s) -> p c s", c=2), ACT.Copy,
                               scale=vec[:, V_KN:V_KN + 1]).then_inc(kh_ready, 1)
            jobs_run(DEPTH * NJ, HYB_JOBS)
            um = u + HYB_IN_UNITS
            split(um, (0, 1))
            for b in range(2):
                act.wait_ge(oT_psum, DEPTH * 4 + b + 1)
                act.activation(oT_hi[1][:, 2 * b:2 * b + 2], bank[5 + b][:, :].rearrange("p (c s) -> p c s", c=2),
                               ACT.Copy).then_inc(oT_hi_done, 1)
            merge(um, DEPTH)
            norm(q6 + 2, n6 + 1)
            act.wait_ge(r_exp_in, 1)
            act.activation(g_exp[:, :, :], g_exp[:, :, :], ACT.Exp)
            act.activation(e_exp[:, :, :], e_exp[:, :, :], ACT.Exp).then_inc(r_exp, 1)
            for n, (i, b) in enumerate(GATHERS):
                act.wait_ge(us_psum, 2 * n + 1)
                for k in range(4):
                    e = act.activation(usf[i][:, k], bank[b][:, k * P:(k + 1) * P], ACT.Identity, scale=modf[:, 8 + k:9 + k], bias=modf[:, k:k + 1])
                e.then_inc(usf_done_a, 1)
            act.wait_ge(usf_done_a, len(GATHERS))
            act.wait_ge(usf_done_v, len(GATHERS))
            act.activation(us_hi[0], usf[0], ACT.Copy).then_inc(us_hi_done, 1)
            split(MOE_U0, (0, 1))
            act.wait_ge(pick_T_psum, 1)
            act.activation(pick_T[:, 0:2], bank[6][:, :].rearrange("p (i s) -> p i s", i=2), ACT.Copy)
            act.activation(pick_T[:, 2], bank[7][:, 0:S], ACT.Copy)
            act.activation(sparse_w[:, :, :], bank[7][:, S:S + 3 * PER_GROUP].rearrange("p (i e) -> p i e", i=3), ACT.Copy).then_inc(pick_T_ready, 1)
            ffn(MOE_U0, MOE_F0, PER_GROUP)

            def sparse_h_split(f):
                act.wait_ge(hT_psum, f + 1)
                act.activation(hTs_hi, HT[:, 0:S].rearrange("p (c s) -> p c s", c=2), ACT.Copy).then_inc(hT_hi_done, 1)

            def sparse_unit(u, f, first=False, last=False):
                if not first:
                    sparse_h_split(f - 1)
                if not last:
                    split(u + 1, (0,), LAST_BEHIND)
                act.wait_ge(used[1], u + 2)
                act.activation(act_g[:, 0], GU[0][:, 0:F_UNIT], ACT.Silu).then_inc(silu_done, 2)
                if not last:
                    split(u + 1, (1,), LAST_BEHIND)
                split(u, (2,), IN_LINE if last else LAST_BEHIND)

            def sparse_out(i):
                act.wait_ge(ys_psum, i + 1)
                for h in range(2):
                    e = act.activation(y_s[i][:, h * 512:(h + 1) * 512], ACC[h][:, :], ACT.Copy)
                e.then_inc(ys_ready, 1)

            for s in SPARSE:
                u, f = MOE_U0 + s * PER_GROUP, MOE_F0 + s * PER_GROUP
                sparse_unit(u, f, first=s == 1)
                if s > 1:
                    sparse_out(s - 2)
                else:
                    act.wait_ge(used[1], MOE_U0 + PER_GROUP + 1)
                    for i in (1, 2):
                        act.activation(us_hi[i], usf[i], ACT.Copy).then_inc(us_hi_done, 1)
                with act.Fori(1, PER_GROUP - 1) as i:
                    sparse_unit(u + i, f + i)
                sparse_unit(u + PER_GROUP - 1, f + PER_GROUP - 1, last=s == SPARSE[-1])
            sparse_h_split(MOE_F0 + EXPERTS - 1)
            sparse_out(len(SPARSE) - 1)

        @block.vector
        def _(dve):
            V = nc.vector
            links = [0, 0]

            def link(ins, layer=None):
                links[0] += 1
                ins.then_inc(chain, 1)
                dve.wait_ge(chain, links[1] + links[0])

            def split(u, js, order=IN_LINE):
                for j in js:
                    b, r = slice(j * BLK, (j + 1) * BLK), (order[j] + 3) % 3
                    dve.wait_ge(hi_done, u * 3 + order[j] + 1)
                    V.tensor_tensor(w_lo[:, b], raw[:, r * BLK:(r + 1) * BLK], f32(w_hi[:, b]), ALU.subtract).then_inc(split_done, 1)

            def rms(q, t):
                c = slice(t, t + 1)
                dve.wait_ge(ss_done, 2 * q + t + 1)
                V.tensor_scalar(ms[:, c], ss[:, c], 1.0 / D, EPS, ALU.mult, ALU.add).then_inc(ms_done, 1)
                dve.wait_ge(sq_done, 2 * q + t + 1)
                V.reciprocal(rstd[:, c], sq[:, c]).then_inc(rstd_done, 1)
                dve.wait_ge(rstd_done, 2 * q + t + 1)

            def modulation(n, gain=None, half=1.0):
                dve.wait_ge(mod_step, n * ADA_STEPS + ADA_STEPS + 1)
                link(V.tensor_tensor(modf[:, :], MOD[:, 0:24], vec[:, bass.ds(V_BADA + n * 24, 24)], ALU.add))
                e = V.tensor_scalar(modf[:, 8:16], modf[:, 8:16], 1.0, None, ALU.add)
                if gain is not None:
                    link(e)
                    e = V.tensor_tensor(modf[:, 8:16], modf[:, 8:16], gain, ALU.mult)
                e.then_inc(mod_ready, 1)
                for k in range(KD):
                    d = V.tensor_scalar(diag[:, k], ident, modf[:, 16 + k:17 + k], half, ALU.mult, ALU.mult)
                d.then_inc(diag_done, 1)
                dve.wait_ge(mod_ready, n + 1)

            def norm_tile(q, t):
                rms(q, t)
                V.tensor_scalar(xn[:, t], x[:, t], rstd[:, t:t + 1], None, ALU.mult).then_inc(xn_done, 1)

            def norm(q, n, tiles=range(T), late=None):
                for t in tiles:
                    norm_tile(q, t)
                for b in (0, 2):
                    dve.wait_ge(uT_psum, 4 * n + b + 1)
                    for k in (2 * b, 2 * b + 1):
                        e = V.tensor_scalar(uTf[:, k], ACC[b][:, (k % 2) * S:(k % 2) * S + S], modf[:, 8 + k:9 + k], modf[:, k:k + 1],
                                            ALU.mult, ALU.add)
                    e.then_inc(uTf_done_v, 1)
                for b in range(4):
                    dve.wait_ge(uT_hi_done, 4 * n + b + 1)
                    V.tensor_tensor(uT_lo[:, 2 * b:2 * b + 2], uTf[:, 2 * b:2 * b + 2], f32(uT_hi[:, 2 * b:2 * b + 2]),
                                    ALU.subtract).then_inc(uT_ready, 1)
                if late is not None:
                    split(late, (1,))

            def hidden(f, weight):
                for t in range(T):
                    dve.wait_ge(silu_done, f * 2 + t + 1)
                    up = GU[t][:, F_UNIT:2 * F_UNIT]
                    if weight is None:
                        h = V.tensor_tensor(hid[:, t], act_g[:, t], up, ALU.mult)
                    else:
                        h = V.scalar_tensor_tensor(hid[:, t], act_g[:, t], dense_w[:, t, bass.ds(weight, 1)], up, ALU.mult, ALU.mult)
                    h.then_inc(h_done, 1)

            def h_split(f):
                dve.wait_ge(hT_hi_done, f + 1)
                V.tensor_tensor(hT_lo[:, :, :], HT[:, :].rearrange("p (f s) -> p f s", f=2), f32(hT_hi[:, :, :]),
                                ALU.subtract).then_inc(hT_ready, 1)

            def x_update(n, done, banks=ACC, between=lambda: None):
                for t in range(T):
                    if t == 0:
                        dve.wait_ge(first_tile, n + 1)
                    else:
                        between()
                        dve.wait_ge(*done)
                    for h in range(2):
                        m = V.tensor_tensor(upd[:, t, h], banks[2 * t + h][:, :], gate_bc[:, h * 512:(h + 1) * 512], ALU.mult)
                    link(m)
                    xt = x[:, t].rearrange("p (h c) -> p h c", h=2)
                    V.tensor_tensor(xt, xt, upd[:, t], ALU.add).then_inc(x_ready, 1)

            def ffn(u0, f0, n, stage, following, between=lambda: None, moe=False):
                split(u0 + 1, (0,), LAST_BEHIND)
                hidden(f0, 0 if moe else None)
                split(u0 + 1, (1,), LAST_BEHIND)
                split(u0, (2,), LAST_BEHIND)
                with dve.Fori(1, n) as i:
                    h_split(f0 + i - 1)
                    split(u0 + i + 1, (0,), LAST_BEHIND)
                    hidden(f0 + i, i if moe else None)
                    split(u0 + i + 1, (1,), LAST_BEHIND)
                    split(u0 + i, (2,), LAST_BEHIND)
                h_split(f0 + n - 1)
                following()
                x_update(stage, (used[2], u0 + n + 1), between=between)

            def merge(u0, m, stage, gates, following, between, more=True):
                split(u0, (2,))
                for t in range(T):
                    dve.wait_ge(pa_psum, 2 * m + t + 1)
                    for h in range(2):
                        e = V.tensor_tensor(y[:, t, h * 512:(h + 1) * 512], gates[h][:, t], ACC[2 * t + h][:, :], ALU.mult)
                    e.then_inc(ya_done, 1)
                    split(u0 + 1, (t,))
                for t in range(T):
                    dve.wait_ge(pb_psum, 2 * m + t + 1)
                    for h in range(2):
                        e = V.tensor_tensor(ytmp[:, t, h], gates[2 + h][:, t], ACC[2 * t + h][:, :], ALU.mult)
                    link(e)
                    yt = y[:, t].rearrange("p (h c) -> p h c", h=2)
                    V.tensor_tensor(yt, yt, ytmp[:, t], ALU.add).then_inc(y_ready, 1)
                    split(*((u0 + 1, (2,)) if t == 0 else (u0 + 2, (0,))))
                for b in range(4):
                    dve.wait_ge(yT_hi_done, 4 * m + b + 1)
                    V.tensor_tensor(yT_lo[:, 2 * b:2 * b + 2], YT[b][:, :].rearrange("p (k s) -> p k s", k=2),
                                    f32(yT_hi[:, 2 * b:2 * b + 2]), ALU.subtract).then_inc(yT_ready, 1)
                split(u0 + 2, (1,))
                following()
                split(u0 + 2, (2,))

                def rest():
                    between()
                    if more:
                        split(u0 + 3, (0,))

                x_update(stage, (used[1], u0 + 4), between=rest)

            def job_bias(j0, jobs, j):
                kind, qt, g = jobs[j]
                nk = (qt + 1) * P
                sc, sp = scores[j % 2], bank[0:2]
                dve.wait_ge(sc_done, j0 + j + 1)
                for p in range(2):
                    ps = sp[p][:, :].rearrange("p (i s) -> p i s", i=2)
                    if kind == 2:
                        e = V.scalar_tensor_tensor(sc[:, p, :, 0:nk], ps[:, :, 0:nk], QK ** -0.5,
                                                   mask[qt].unsqueeze(1).to_broadcast([P, 2, nk]), ALU.mult, ALU.add)
                        continue
                    for i in range(2):
                        h = 4 * g + 2 * i + p
                        if kind == 3:
                            e = V.scalar_tensor_tensor(sc[:, p, i, 0:nk], ps[:, i, 0:nk], f_cum[:, qt, h:h + 1], mask[qt], ALU.add, ALU.add)
                        else:
                            e = V.scalar_tensor_tensor(sc[:, p, i, 0:nk], dist[qt], SLOPES[h], ps[:, i, 0:nk], ALU.mult, ALU.add)
                e.then_inc(bias_done, 1)
                dve.wait_ge(bias_done, j0 + j + 1)
                V.tensor_reduce(nmax[j % 2].rearrange("p (a i) -> p a i", a=2), sc[:, :, :, 0:nk], AX.X, ALU.max,
                                negate=True).then_inc(nmax_done, 1)

            def job_out(j0, jobs, j):
                kind, qt, g = jobs[j]
                dve.wait_ge(pv_done, j0 + j + 1)
                o_ps = HT[:, 0:4 * DH].rearrange("p (a i d) -> p a i d", a=2, i=2)
                link(V.reciprocal(rsum, psum_row[j % 4]))
                r = rsum.rearrange("p (a i) -> p a i", a=2)
                if kind < 2:
                    gate = nsa_gate[:, qt, 4 * g:4 * g + 4, 1 + kind].rearrange("p (i a) -> p a i", a=2)
                    link(V.tensor_tensor(coef.rearrange("p (a i) -> p a i", a=2), r, gate, ALU.mult))
                    r = coef.rearrange("p (a i) -> p a i", a=2)
                dst = o_h if kind == 3 else o_a if kind < 2 else o_b
                ov = dst[:, qt, 256 * g:256 * g + 256].rearrange("p (i a d) -> p a i d", i=2, a=2)
                if kind >= 2:
                    for a in range(2):
                        e = V.tensor_tensor(ov[:, a], o_ps[:, a], r[:, a].unsqueeze(2).to_broadcast([P, 2, DH]), ALU.mult)
                    e.then_inc(o_done, 1)
                else:
                    tv = o_tmp.rearrange("p (a i) d -> p a i d", a=2)
                    for a in range(2):
                        e = V.tensor_tensor(tv[:, a], o_ps[:, a], r[:, a].unsqueeze(2).to_broadcast([P, 2, DH]), ALU.mult)
                    e.then_inc(o_done, 1)
                    dve.wait_ge(o_done, j0 + j + 1)
                    for a in range(2):
                        e = V.tensor_tensor(ov[:, a], ov[:, a], tv[:, a], ALU.add)
                    link(e)

            def jobs_run(j0, jobs, beside=lambda j: None):
                job_bias(j0, jobs, 0)
                for j, (kind, qt, g) in enumerate(jobs):
                    if j + 1 < len(jobs):
                        job_bias(j0, jobs, j + 1)
                    beside(j)
                    if qt:
                        dve.wait_ge(pt_psum, j0 + j + 1)
                        V.tensor_copy(pT[j % 2][:, 1], bank[5][:, :].rearrange("p (h q) -> p h q", h=4)).then_inc(pt_copied_v, 1)
                    if j:
                        job_out(j0, jobs, j - 1)
                job_out(j0, jobs, len(jobs) - 1)

            V.memset(zeros[:, :], 0.0).then_inc(first_ready, 1)
            for j in range(2):
                b = slice(j * BLK, (j + 1) * BLK)
                dve.wait_ge(hi_done, j + 1)
                V.tensor_tensor(w_lo[:, b], raw[:, b], f32(w_hi[:, b]), ALU.subtract).then_inc(split_done, 1)
            dve.wait_ge(x_landed, 16)
            dve.wait_ge(cst_landed, 32)
            V.memset(stat[:, 0:2], 0.0).then_inc(x_ready, 2)

            with dve.Fori(0, DEPTH) as l:
                links[:] = [0, l * CHAIN_PER_LAYER]
                u_mix = l * LAYER_UNITS + FFN_UNITS
                modulation(l * 3, half=0.5)
                norm(l * 3, l * 3)
                ffn(l * LAYER_UNITS, l * 2 * FFN_UNITS, FFN_UNITS, l * 3, lambda: modulation(l * 3 + 1),
                    lambda: norm_tile(l * 3 + 1, 0))

                norm(l * 3 + 1, l * 3 + 1, (1,))
                split(u_mix, (2,))
                split(u_mix + 1, (0, 1))
                dve.wait_ge(w_done, l * 7 + 1)
                V.tensor_copy(proj[:, 1, 0:512], bank[1][:, :]).then_inc(w_evac_v, 1)
                split(u_mix + 1, (2,))
                dve.wait_ge(lat_ss, l * 4 + 4)
                V.tensor_scalar(lms[:, 0:2], lss[:, 0:2], 1.0 / Q_RANK, EPS, ALU.mult, ALU.add)
                V.tensor_scalar(lms[:, 2:4], lss[:, 2:4], 1.0 / KV_RANK, EPS, ALU.mult, ALU.add).then_inc(lat_ms, 1)
                dve.wait_ge(lat_sq, l + 1)
                link(V.reciprocal(lrs, lsq))
                for t in range(T):
                    V.tensor_scalar(proj[:, t, C_CQ:C_CKV], proj[:, t, C_CQ:C_CKV], lrs[:, t:t + 1], None, ALU.mult)
                    e = V.tensor_scalar(proj[:, t, C_CKV:C_KR], proj[:, t, C_CKV:C_KR], lrs[:, 2 + t:3 + t], None, ALU.mult)
                e.then_inc(lat_ready, 1)
                kr = proj[:, :, C_KR:C_GN]
                V.tensor_tensor(kr_a[:, :, :], kr, cos2, ALU.mult)
                link(V.tensor_tensor(kr_b[:, :, :], kr, sin2, ALU.mult))
                split(u_mix + 2, (0, 1))
                dve.wait_ge(w_done, l * 7 + 2)
                V.tensor_copy(proj[:, 1, 768:1280], bank[4][:, :]).then_inc(w_evac_v, 1)
                split(u_mix + 2, (2,))
                dve.wait_ge(w_done, l * 7 + 3)
                V.tensor_copy(proj[:, 1, 1536:PROJ], bank[1][:, 0:184])
                V.tensor_copy(vsw[:, 1], bank[1][:, 184:440]).then_inc(w_evac_v, 1)
                split(u_mix + 3, (0,))
                dve.wait_ge(lvec_landed, l * 32 + 32)
                for b, cs in enumerate(((0, 1), (2, 3), (4,))):
                    dve.wait_ge(cqT_hi_done, l * 3 + b + 1)
                    for i, c in enumerate(cs):
                        e = V.scalar_tensor_tensor(cqT_lo[:, c], bank[2 + b][:, i * S:(i + 1) * S], lvec[:, L_QN + c:L_QN + c + 1],
                                                   f32(cqT_hi[:, c]), ALU.mult, ALU.subtract)
                    e.then_inc(cqT_ready, 1)
                dve.wait_ge(kw_psum, l + 1)
                V.tensor_copy(kT[1][:, :, :], bank[1][:, :].rearrange("p (g s) -> p g s", g=2)).then_inc(kw_ready, 1)
                dve.wait_ge(c_psum, l + 1)
                for k in range(2):
                    both = bank[2 + k][:, :].rearrange("p (g s) -> p g s", g=GROUPS)
                    V.tensor_copy(cT[0:DH, 2 * k:2 * k + 2], both[0:DH])
                    e = V.tensor_copy(cT[DH:P, 2 * k:2 * k + 2, 0:S - CMP_STRIDE], both[DH:P, :, CMP_STRIDE:S])
                link(e)
                for k in range(2):
                    place_k = lvec[:, L_PE + CMP_STRIDE * k:L_PE + CMP_STRIDE * (k + 1)].unsqueeze(2).to_broadcast([P, CMP_STRIDE, N_CMP])
                    for g in range(GROUPS):
                        tok = cT[:, 2 * k + g].rearrange("p (n j) -> p j n", j=CMP_STRIDE)
                        e = V.tensor_tensor(blocks[:, 2 * k + g], tok[:, :, 0:N_CMP], place_k, ALU.add)
                e.then_inc(blocks_ready, 1)
                dve.wait_ge(kvc_psum, l + 1)
                for g in range(GROUPS):
                    V.tensor_copy(kT_cmp[:, g, 0:N_CMP], bank[4 + g][:, 0:N_CMP])
                    for i in range(4):
                        e = V.tensor_copy(v_cmp[32 * i:32 * i + N_CMP, g], bank[4 + g][32 * i:32 * i + N_CMP, 64:128])
                e.then_inc(kvc_ready, 1)
                link(V.memset(p_cmp[:, :, :], 0.0))
                dve.wait_ge(cs_psum, l + 1)
                pc = p_cmp.rearrange("p (a q i) n -> p a q i n", a=2, q=2)
                for p in range(2):
                    for qt in range(2):
                        e = V.tensor_tensor(pc[:, p, qt, :, 0:N_CMP], bank[4 + p][:, 64 * qt:64 * qt + 64].rearrange("p (i n) -> p i n", i=4)[:, :, 0:N_CMP],
                                            cmp_bias[:, p, qt, :, 0:N_CMP], ALU.add)
                link(e)
                link(V.tensor_reduce(cmax, p_cmp[:, :, 0:N_CMP], AX.X, ALU.max))
                V.tensor_tensor(p_cmp[:, :, 0:N_CMP], p_cmp[:, :, 0:N_CMP], cmax.unsqueeze(2).to_broadcast([P, 16, N_CMP]),
                                ALU.subtract).then_inc(cs_ready, 1)
                H2 = ROPE // 2
                bc = [P, HEADS, H2]
                for t in range(T):
                    V.tensor_tensor(k_tok[:, t, :, NOPE:NOPE + H2], kr_a[:, t, 0:H2].unsqueeze(1).to_broadcast(bc),
                                    kr_b[:, t, H2:ROPE].unsqueeze(1).to_broadcast(bc), ALU.subtract)
                    V.tensor_tensor(k_tok[:, t, :, NOPE + H2:QK], kr_b[:, t, 0:H2].unsqueeze(1).to_broadcast(bc),
                                    kr_a[:, t, H2:ROPE].unsqueeze(1).to_broadcast(bc), ALU.add)
                dve.wait_ge(cp_exp, l + 1)
                link(V.tensor_reduce(csum, p_cmp[:, :, 0:N_CMP], AX.X, ALU.add))
                link(V.reciprocal(crec, csum))
                dve.wait_ge(nsa_gate_ready, l + 1)
                for qt in range(2):
                    g0 = nsa_gate[:, qt, :, 0].rearrange("p (i a) -> p a i", a=2)
                    cc = ccoef.rearrange("p (a q i) -> p a q i", a=2, q=2)[:, :, qt]
                    cr = crec.rearrange("p (a q i) -> p a q i", a=2, q=2)[:, :, qt]
                    e = V.scalar_tensor_tensor(cc, cr, cmp_valid[:, qt:qt + 1], g0, ALU.mult, ALU.mult)
                link(e)
                dve.wait_ge(uq_copied, l * 4 + 4)
                qr = q_tok[:, :, :, NOPE:QK]
                for t in range(T):
                    V.tensor_tensor(rope_a[:, t], qr[:, t], cos2[:, t].unsqueeze(1).to_broadcast([P, HEADS, ROPE]), ALU.mult)
                    e = V.tensor_tensor(rope_b[:, t], qr[:, t], sin2[:, t].unsqueeze(1).to_broadcast([P, HEADS, ROPE]), ALU.mult)
                link(e)
                V.tensor_tensor(q_tok[:, :, :, NOPE:NOPE + H2], rope_a[:, :, :, 0:H2], rope_b[:, :, :, H2:ROPE], ALU.subtract)
                V.tensor_tensor(q_tok[:, :, :, NOPE + H2:QK], rope_b[:, :, :, 0:H2], rope_a[:, :, :, H2:ROPE], ALU.add).then_inc(rope_done, 1)
                for t in range(T):
                    dve.wait_ge(uk_psum, l * 2 + t + 1)
                    V.tensor_copy(k_tok[:, t, :, 0:NOPE], bank[4 + t][:, :].rearrange("p (h c) -> p h c", h=HEADS)).then_inc(uk_copied, 1)
                split(u_mix + 3, (1,))
                dve.wait_ge(co_psum, l + 1)
                dve.wait_ge(rope_done, l + 1)
                oav = o_a.rearrange("p t (i a d) -> p t i a d", i=4, a=2)
                for i in range(4):
                    for qt in range(2):
                        cc = ccoef.rearrange("p (a q i) -> p a q i", a=2, q=2)[:, :, qt, i]
                        e = V.tensor_tensor(oav[:, qt, i], bank[i][:, 128 * qt:128 * qt + 128].rearrange("p (a d) -> p a d", a=2),
                                            cc.unsqueeze(2).to_broadcast([P, 2, DH]), ALU.mult)
                e.then_inc(co_done, 1)
                dve.wait_ge(co_done, l + 1)
                for t in range(T):
                    dve.wait_ge(uv_psum, l * 2 + t + 1)
                    V.tensor_copy(vm[:, t], bank[6 - 2 * t][:, :]).then_inc(uv_ready, 1)
                split(u_mix + 3, (2,))
                for b in range(4):
                    dve.wait_ge(km_psum, l * 4 + b + 1)
                    V.tensor_copy(qkT_m[0:QK, 1, 2 * b:2 * b + 2], bank[K_BANKS[b]][0:QK, :].rearrange("p (h s) -> p h s", h=2)).then_inc(km_ready, 1)

                def beside(j):
                    if j in JOB_SPLITS:
                        m, b = JOB_SPLITS[j]
                        split(u_mix + m, (b,))

                jobs_run(l * NJ, JOBS, beside)
                for b in range(4):
                    dve.wait_ge(oT_hi_done, l * 4 + b + 1)
                    V.tensor_tensor(oT_lo[b // 2][:, 2 * (b % 2):2 * (b % 2) + 2], bank[3 + b][:, :].rearrange("p (c s) -> p c s", c=2),
                                    f32(oT_hi[b // 2][:, 2 * (b % 2):2 * (b % 2) + 2]), ALU.subtract).then_inc(oT_ready, 1)
                dve.wait_ge(w_evac_a, l * 9 + 9)
                merge(u_mix + MIX_IN_UNITS, l, l * 3 + 1, gates_m, lambda: modulation(l * 3 + 2, half=0.5), lambda: norm_tile(l * 3 + 2, 0))

                norm(l * 3 + 2, l * 3 + 2, (1,), late=u_mix + MIX_IN_UNITS + MERGE_UNITS)
                ffn(l * LAYER_UNITS + FFN_UNITS + MIX_IN_UNITS + MERGE_UNITS, l * 2 * FFN_UNITS + FFN_UNITS, FFN_UNITS,
                    l * 3 + 2, lambda: None)
                assert links[0] <= CHAIN_PER_LAYER
                if links[0] < CHAIN_PER_LAYER:
                    V.memset(pad, 0.0).then_inc(chain, CHAIN_PER_LAYER - links[0])

            links[:] = [0, DEPTH * CHAIN_PER_LAYER]
            q6, n6 = 3 * DEPTH, 3 * DEPTH
            modulation(n6, gain=vec[:, V_N1:V_N1 + 8])
            dve.wait_ge(fn_landed, 16)
            for t in range(T):
                rms(q6, t)
                V.scalar_tensor_tensor(x[:, t], x[:, t], rstd[:, t:t + 1], fn_bc, ALU.mult, ALU.mult).then_inc(x_ready, 1)
            dve.wait_ge(x_ready, 2 * (q6 + 2))
            norm(q6 + 1, n6)
            u = HYB_U0
            split(u, (2,))
            for m in range(HYB_IN_UNITS):
                if m + 1 < HYB_IN_UNITS:
                    split(u + m + 1, (0, 1))
                if m < 4:
                    dve.wait_ge(w_done, DEPTH * 7 + m + 1)
                    dst, c0 = (xcb, 768 * m) if m < 2 else (qkv, 768 * (m - 2))
                    V.tensor_copy(dst[:, 1, c0:c0 + 512], bank[3 * (m % 2) + 1][:, :]).then_inc(w_evac_v, 1)
                if m + 1 < HYB_IN_UNITS:
                    split(u + m + 1, (2,))
            dve.wait_ge(w_evac_a, DEPTH * 9 + 4)
            dve.wait_ge(w_evac_v, DEPTH * 3 + 2)
            V.tensor_tensor(u_tok[:, :, :], xcb[:, :, 0:512], xcb[:, :, 512:1024], ALU.mult).then_inc(u_ready, 1)
            dve.wait_ge(w_evac_a, DEPTH * 9 + 8)
            dve.wait_ge(w_evac_v, DEPTH * 3 + 4)
            qk_s = qk_ss.rearrange("p (i t h) -> p i t h", i=2, t=T)
            for i in range(2):
                v = qkv[:, :, 512 * i:512 * i + 512]
                link(V.tensor_tensor(squares[:, :, :], v, v, ALU.mult))
                link(V.tensor_reduce(qk_s[:, i], squares.rearrange("p t (h d) -> p t h d", h=HEADS), AX.X, ALU.add))
            V.tensor_scalar(qk_gain[:, 0:1], vec[:, V_QN:V_QN + 1], DH ** -0.5, None, ALU.mult)
            V.tensor_scalar(qk_ss, qk_ss, 1.0 / DH, EPS, ALU.mult, ALU.add).then_inc(qkn_ms, 1)
            dve.wait_ge(w_evac_a, DEPTH * 9 + 9)
            bf = vec[:, V_BF:V_BF + 8].unsqueeze(1).to_broadcast([P, T, 8])
            link(V.tensor_tensor(f_row[:, :, :], f_row[:, :, :], bf, ALU.add))
            V.tensor_scalar(f_cum[:, :, :], f_row[:, :, :], 0.0, None, ALU.min)
            V.scalar_tensor_tensor(f_e[:, :, :], f_row[:, :, :], -1.0, f_row[:, :, :], ALU.mult, ALU.min).then_inc(f_exp_in, 1)
            dve.wait_ge(qkn_sq, 1)
            link(V.reciprocal(qk_ss, qk_ss))
            for i in range(2):
                for t in range(T):
                    v = qkv[:, t, 512 * i:512 * i + 512].rearrange("p (h d) -> p h d", h=HEADS)
                    e = V.tensor_tensor(v, v, qk_s[:, i, t].unsqueeze(2).to_broadcast([P, HEADS, DH]), ALU.mult)
            e.then_inc(qkn_ready, 1)
            dve.wait_ge(f_exp, 1)
            V.tensor_scalar(f_l[:, :, :], f_e[:, :, :], 1.0, None, ALU.add).then_inc(f_ln_in, 1)
            dve.wait_ge(f_ln, 1)
            V.tensor_tensor(nlogf[:, :, :], f_l[:, :, :], f_cum[:, :, :], ALU.subtract).then_inc(logf_ready, 1)
            dve.wait_ge(uc_psum, 2)
            dve.wait_ge(b_psum, 1)
            V.memset(uTc[:, :, 0:2], 0.0)
            for b in range(2):
                e = V.tensor_copy(uTc[:, 2 * b:2 * b + 2, 2:S + 2], bank[4 + b][:, :].rearrange("p (c s) -> p c s", c=2))
            e.then_inc(uc_ready, 1)
            dve.wait_ge(uc_ready, 1)
            for j in range(3):
                for c in range(4):
                    w = vec[:, V_CONV + 3 * c + j:V_CONV + 3 * c + j + 1]
                    if j == 0:
                        e = V.tensor_scalar(conv[:, c], uTc[:, c, 0:S], w, None, ALU.mult)
                    else:
                        e = V.scalar_tensor_tensor(conv[:, c], uTc[:, c, j:j + S], w, conv[:, c], ALU.mult, ALU.add)
                link(e)
            for b in range(2):
                V.tensor_tensor(conv[:, 2 * b:2 * b + 2], conv[:, 2 * b:2 * b + 2],
                                bank[6 - 3 * b][:, :].rearrange("p (c s) -> p c s", c=2), ALU.mult).then_inc(ya_f32, 1)
            for b in range(2):
                dve.wait_ge(ya_hi_done, b + 1)
                V.tensor_tensor(oT_lo[0][:, 2 * b:2 * b + 2], conv[:, 2 * b:2 * b + 2], f32(oT_hi[0][:, 2 * b:2 * b + 2]),
                                ALU.subtract).then_inc(oT_ready, 1)
            dve.wait_ge(fcum_psum, 1)
            V.tensor_scalar(f_cum[:, :, :], bank[5][:, 0:16].rearrange("p (t h) -> p t h", t=T), -1.0, None, ALU.mult).then_inc(fcum_ready, 1)
            dve.wait_ge(fcum_ready, 1)
            jobs_run(DEPTH * NJ, HYB_JOBS)
            um = u + HYB_IN_UNITS
            split(um, (0, 1))
            for b in range(2):
                dve.wait_ge(oT_hi_done, DEPTH * 4 + b + 1)
                V.tensor_tensor(oT_lo[1][:, 2 * b:2 * b + 2], bank[5 + b][:, :].rearrange("p (c s) -> p c s", c=2),
                                f32(oT_hi[1][:, 2 * b:2 * b + 2]), ALU.subtract).then_inc(oT_ready, 1)
            dve.wait_ge(w_evac_a, DEPTH * 9 + 11)
            merge(um, DEPTH, n6, gate_sets_h, lambda: modulation(n6 + 1, gain=vec[:, V_N2:V_N2 + 8]),
                  lambda: norm_tile(q6 + 2, 0), more=False)
            norm(q6 + 2, n6 + 1, (1,))
            dve.wait_ge(r_psum, 1)
            br = vec[:, V_BR:V_BR + 36].unsqueeze(1).to_broadcast([P, T, 36])
            link(V.tensor_tensor(logits[:, :, :], HT[:, 0:128].rearrange("p (t c) -> p t c", t=T)[:, :, 0:36], br, ALU.add))
            lg = logits[:, :, 0:4]

            def ranks(v, n, gt, eq, tie, rank):
                for t in range(T):
                    mine = v[:, t].unsqueeze(2).to_broadcast([P, n, n])
                    other = v[:, t].unsqueeze(1).to_broadcast([P, n, n])
                    V.tensor_tensor(gt[:, t], other, mine, ALU.is_gt)
                    e = V.tensor_tensor(eq[:, t], other, mine, ALU.is_equal)
                link(e)
                for t in range(T):
                    e = V.tensor_tensor(eq[:, t], eq[:, t], tie, ALU.mult)
                link(e)
                link(V.tensor_tensor(gt[:, :], gt[:, :], eq[:, :], ALU.add))
                link(V.tensor_reduce(rank[:, :, :], gt[:, :], AX.X, ALU.add))

            ranks(lg, 4, g_gt, g_eq, tie4, g_rank)
            V.tensor_scalar(g_sel[:, :, :], g_rank[:, :, :], 0.0, None, ALU.is_equal).then_inc(sel_ready, 1)
            link(V.tensor_reduce(g_max, lg, AX.X, ALU.max))
            V.tensor_tensor(g_exp[:, :, :], lg, g_max.unsqueeze(2).to_broadcast([P, T, 4]), ALU.subtract)
            dve.wait_ge(sel_ready, 1)
            for t in range(T):
                e = V.tensor_tensor(le_m[:, t], logits[:, t, 4:36].rearrange("p (g e) -> p g e", g=4),
                                    g_sel[:, t].unsqueeze(2).to_broadcast([P, 4, 8]), ALU.mult)
            link(e)
            dve.wait_ge(count_psum, 1)
            for t in range(T):
                V.tensor_copy(g_total[:, t], GU[1][:, 0:4])
            link(V.tensor_tensor(g_cum[:, :, :], GU[1][:, 4:12].rearrange("p (t g) -> p t g", t=T), g_sel[:, :, :], ALU.mult))
            V.tensor_reduce(own_cum, g_cum[:, :, :], AX.X, ALU.add)
            ranks(g_total, 4, g_gt, g_eq, tie4, g_place)
            for r in range(EXPERT_GROUPS):
                e = V.tensor_scalar(by_rank[:, r], g_place[:, 0], float(r), None, ALU.is_equal)
            link(e)
            link(V.tensor_tensor(g_base_in[:, :, :], by_rank[:, :, :], group_iota.unsqueeze(1).to_broadcast([P, 4, 4]), ALU.mult))
            link(V.tensor_reduce(g_base, g_base_in[:, :, :], AX.X, ALU.add))
            V.tensor_copy(expert_base[:, :], g_base).then_inc(base_ready, 1)
            for t in range(T):
                e = V.tensor_tensor(member_in[:, t], by_rank[:, :, :], g_sel[:, t].unsqueeze(1).to_broadcast([P, 4, 4]), ALU.mult)
            link(e)
            link(V.tensor_reduce(member[:, :, :], member_in[:, :], AX.X, ALU.add))
            link(V.tensor_tensor(place[:, :, :], member[:, :, :], own_cum.unsqueeze(2).to_broadcast([P, T, 4]), ALU.mult))
            link(V.tensor_scalar(place[:, :, :], place[:, :, :], 1.0, None, ALU.subtract))
            for t in range(T):
                for r in SPARSE:
                    e = V.tensor_scalar(pick[:, t, r - 1], place_iota, place[:, t, r:r + 1], None, ALU.is_equal)
            e.then_inc(pick_ready, 1)
            link(V.tensor_reduce(le_g[:, :, :], le_m.rearrange("p t g e -> p t e g"), AX.X, ALU.add))
            link(V.tensor_reduce(e_max, le_g[:, :, :], AX.X, ALU.max))
            V.tensor_tensor(e_exp[:, :, :], le_g[:, :, :], e_max.unsqueeze(2).to_broadcast([P, T, 8]), ALU.subtract).then_inc(r_exp_in, 1)
            ranks(le_g, 8, e_gt, e_eq, tie8, e_rank)
            link(V.tensor_scalar(e_rank[:, :, :], e_rank[:, :, :], 2.0, None, ALU.is_lt))
            dve.wait_ge(r_exp, 1)
            V.tensor_reduce(g_sum, g_exp[:, :, :], AX.X, ALU.add)
            link(V.tensor_tensor(e_exp[:, :, :], e_exp[:, :, :], e_rank[:, :, :], ALU.mult))
            link(V.tensor_reduce(e_sum, e_exp[:, :, :], AX.X, ALU.add))
            V.reciprocal(p_sel, g_sum)
            link(V.reciprocal(e_sum, e_sum))
            link(V.tensor_tensor(e_sum, e_sum, p_sel, ALU.mult))
            V.tensor_tensor(e_w[:, :, :], e_exp[:, :, :], e_sum.unsqueeze(2).to_broadcast([P, T, 8]), ALU.mult).then_inc(ew_ready, 1)
            dve.wait_ge(ew_ready, 1)
            link(V.tensor_tensor(dense_w[:, :, :], e_w[:, :, :], member[:, :, 0:1].to_broadcast([P, T, PER_GROUP]), ALU.mult))
            for n, (i, b) in enumerate(GATHERS):
                dve.wait_ge(us_psum, 2 * n + 2)
                for k in range(4, KD):
                    e = V.tensor_scalar(usf[i][:, k], bank[b + 1][:, (k - 4) * P:(k - 3) * P], modf[:, 8 + k:9 + k], modf[:, k:k + 1], ALU.mult, ALU.add)
                e.then_inc(usf_done_v, 1)
            dve.wait_ge(us_hi_done, 1)
            V.tensor_tensor(us_lo[0], usf[0], f32(us_hi[0]), ALU.subtract).then_inc(us_ready, 1)
            split(MOE_U0, (0, 1))
            ffn(MOE_U0, MOE_F0, PER_GROUP, n6 + 1, lambda: None, moe=True)

            dve.wait_ge(pick_T_ready, 1)

            def sparse_h_split(f):
                dve.wait_ge(hT_hi_done, f + 1)
                V.tensor_tensor(hTs_lo, HT[:, 0:S].rearrange("p (c s) -> p c s", c=2), f32(hTs_hi), ALU.subtract).then_inc(hT_ready, 1)

            def sparse_unit(u, f, r, e, first=False, last=False):
                if not first:
                    sparse_h_split(f - 1)
                if not last:
                    split(u + 1, (0,), LAST_BEHIND)
                dve.wait_ge(silu_done, f * 2 + 2)
                V.scalar_tensor_tensor(hid[:, 0], act_g[:, 0], sparse_w[:, r - 1, bass.ds(e, 1)], GU[0][:, F_UNIT:2 * F_UNIT],
                                       ALU.mult, ALU.mult).then_inc(h_done, 2)
                if not last:
                    split(u + 1, (1,), LAST_BEHIND)
                split(u, (2,), IN_LINE if last else LAST_BEHIND)

            for r in SPARSE:
                u, f = MOE_U0 + r * PER_GROUP, MOE_F0 + r * PER_GROUP
                sparse_unit(u, f, r, 0, first=r == 1)
                if r == 1:
                    for i in (1, 2):
                        dve.wait_ge(us_hi_done, i + 1)
                        V.tensor_tensor(us_lo[i], usf[i], f32(us_hi[i]), ALU.subtract).then_inc(us_ready, 1)
                with dve.Fori(1, PER_GROUP - 1) as i:
                    sparse_unit(u + i, f + i, r, i)
                sparse_unit(u + PER_GROUP - 1, f + PER_GROUP - 1, r, PER_GROUP - 1, last=r == SPARSE[-1])
            sparse_h_split(MOE_F0 + EXPERTS - 1)
            x_update(STAGES, (spread_done, 1), SPREAD)

        @block.tensor
        def _(pe):
            def release(s_):
                pe.matmul(MOD[:, 64:65], zeros[:, 0:P], zeros[:, 0:1], start=True, stop=True, skip_group_check=True).then_inc(s_, 1)

            def carry_waits():
                pe.matmul(MOD[:, 64:65], zeros[:, 0:P], zeros[:, 0:1], start=True, stop=True, skip_group_check=True)

            def need(u, seen, off, n, order=IN_LINE):
                for j in range(off // BLK, (off + n - 1) // BLK + 1):
                    if j not in seen:
                        pe.wait_ge(split_done, u * 3 + order[j] + 1)
                        seen.add(j)

            def mm3(dst, xh, xl, off, n, first, last):
                pe.matmul(dst, xh, w_hi[:, off:off + n], start=first, stop=False, skip_group_check=True)
                pe.matmul(dst, xh, w_lo[:, off:off + n], start=False, stop=False, skip_group_check=True)
                return pe.matmul(dst, xl, w_hi[:, off:off + n], start=False, stop=last, skip_group_check=True)

            def tok(t):
                return slice(t * P, (t + 1) * P)

            def ada_step(n, col, first=None):
                if first is not None:
                    pe.wait_ge(mod_ready, first)
                pe.wait_ge(ada_ready, n - ADA_STEPS + 1)
                for h in range(2):
                    m = pe.matmul(MOD[:, bass.ds(col + h, 1)], ada_sum[:, h * P:(h + 1) * P], ones[:, 0:1],
                                  start=True, stop=True, skip_group_check=True)
                m.then_inc(mod_step, 1)

            def columns(u, ncol, b0, ada_n=None, ada_c=0, stage=None, off0=0, close=(0, 1, 2), first_of=None):
                seen, n2 = set(), ncol - 512
                m = None
                for k in range(KD):
                    off = off0 + k * ncol
                    need(u, seen, off, ncol)
                    if first_of is not None and k % 2 == 0:
                        pe.wait_ge(uT_ready, 4 * first_of + k // 2 + 1)
                    for t in range(T):
                        m = mm3(bank[b0 + t][:, 0:min(512, ncol)], uT_hi[:, k, tok(t)], uT_lo[:, k, tok(t)], off, min(512, ncol),
                                k == 0, k == KD - 1)
                        if n2 > 0:
                            dst = bank[b0 + 2][:, t * n2:(t + 1) * n2]
                            m = mm3(dst, uT_hi[:, k, tok(t)], uT_lo[:, k, tok(t)], off + 512, n2, k == 0 and t == 0, k == KD - 1)
                    for j in close:
                        if k < KD - 1 and off < (j + 1) * BLK <= off + ncol:
                            m.then_inc(used[j], 1)
                    if ada_n is not None and k == 3:
                        ada_step(ada_n, ada_c, stage)
                m.then_inc(w_done, 1)
                for j in close:
                    if (j + 1) * BLK > off0 + (KD - 1) * ncol:
                        release(used[j])
                if ada_n is not None:
                    ada_step(ada_n + 1, ada_c + 2)

            def norm(n, q):
                pe.wait_ge(x_ready, 2 * q + 2)
                for t in range(T):
                    pe.wait_ge(xn_done, 2 * n + t + 1)
                    for b in range(4):
                        for k in (2 * b, 2 * b + 1):
                            m = pe.transpose(ACC[b][:, (k % 2) * S + t * P:(k % 2) * S + (t + 1) * P], xn[:, t, k * P:(k + 1) * P], ident)
                        if t == T - 1:
                            m.then_inc(uT_psum, 1)
                pe.wait_ge(diag_done, n + 1)
                for h, b in enumerate((HT, GU[1])):
                    pe.matmul(b[:, :], ones, diag[:, 4 * h:4 * h + 4], start=True, stop=True).then_inc(gate_psum, 1)

            def gate_up(u, first_of=None):
                seen = set()
                order = [(k, t) for k in range(KD) for t in range(T)] if first_of is None else [(k, t) for t in range(T) for k in range(KD)]
                for k, t in order:
                    need(u, seen, k * 512, 512, LAST_BEHIND if first_of is None else IN_LINE)
                    if first_of is not None and t == 0 and k % 2 == 0:
                        pe.wait_ge(uT_ready, 4 * first_of + k // 2 + 1)
                    if first_of is not None and t == 1 and k == 0:
                        pe.wait_ge(gate_ready, 2 * first_of + 2)
                    m = mm3(GU[t][:, :], uT_hi[:, k, tok(t)], uT_lo[:, k, tok(t)], k * 512, 512, k == 0, k == KD - 1)
                    if k == KD - 1 and t == 0:
                        m.then_inc(gu0_done, 1)
                    if t == T - 1 and k in (3, 7):
                        m.then_inc(used[k // 4], 1)

            def turn(f):
                pe.wait_ge(h_done, f * 2 + 2)
                for t in range(T):
                    for c in range(2):
                        m = pe.transpose(HT[:, c * S + t * P:c * S + (t + 1) * P], hid[:, t, c * P:(c + 1) * P], ident)
                m.then_inc(hT_psum, 1)

            def down(u, f, last=False):
                pe.wait_ge(hT_ready, f + 1)
                need(u, set(), 2 * BLK, BLK, LAST_BEHIND)
                for t, c in [(t, c) for t in range(T) for c in range(2)]:
                    for h in range(2):
                        m = mm3(ACC[2 * t + h][:, :], hT_hi[:, c, tok(t)], hT_lo[:, c, tok(t)], 2 * BLK + c * D + h * 512, 512,
                                False, last and c == 1)
                    if last and (t, c) == (0, 1):
                        m.then_inc(first_tile, 1)
                m.then_inc(used[2], 1)

            def ffn(u0, f0, n, nn, stage):
                gate_up(u0, nn)
                if stage is not None:
                    ada_step(stage * ADA_STEPS, 0, stage)
                    ada_step(stage * ADA_STEPS + 1, 2)
                for b in range(4):
                    pe.matmul(ACC[b][:, :], zeros[:, 0:P], zeros[:, :], start=True, stop=False, skip_group_check=True)
                with pe.Fori(1, n) as i:
                    turn(f0 + i - 1)
                    gate_up(u0 + i)
                    if stage is not None:
                        ada_step(stage * ADA_STEPS + i + 1, i * 2 + 2)
                    down(u0 + i - 1, f0 + i - 1)
                turn(f0 + n - 1)
                down(u0 + n - 1, f0 + n - 1, last=True)

            def half_product(lhs, chunks, closes, ready, done):
                seen = {}
                for t in range(T):
                    pe.wait_ge(*ready[t])
                    for k, (u, off) in enumerate(chunks):
                        need(u, seen.setdefault(str(u), set()), off, D)
                        for h in range(2):
                            e = mm3(ACC[2 * t + h][:, :], lhs[0][:, k, tok(t)], lhs[1][:, k, tok(t)], off + h * 512, 512, k == 0, k == 3)
                        if t == T - 1 and k in closes:
                            e.then_inc(used[closes[k]], 1)
                    release(done)

            def merge(u0, m, close2):
                u1, u2 = u0 + 1, u0 + 2
                half_product((oT_hi[0], oT_lo[0]), [(u0, k * D) for k in range(4)], {1: 0, 3: 1}, [(oT_ready, 4 * m + 2)] * T, pa_psum)
                pe.wait_ge(oT_ready, 4 * m + 4)
                half_product((oT_hi[1], oT_lo[1]), [(u0, 4 * D), (u0, 5 * D), (u1, 0), (u1, D)], {1: 2, 3: 0},
                             [(ya_done, 2 * m + t + 1) for t in range(T)], pb_psum)
                for b, t in [(b, t) for t in range(T) for b in range(3)] + [(3, t) for t in range(T)]:
                    if b != 3:
                        pe.wait_ge(y_ready, 2 * m + t + 1)
                    for k in (2 * b, 2 * b + 1):
                        e = pe.transpose(YT[b][:, (k % 2) * S + t * P:(k % 2) * S + (t + 1) * P], y[:, t, k * P:(k + 1) * P], ident)
                    if t == T - 1:
                        e.then_inc(yT_psum, 1)
                seen = {}
                for half in range(2):
                    for t in range(T):
                        for k in range(4 * half, 4 * half + 4):
                            u, off = (u1, BLK + k * D) if k < 4 else (u2, (k - 4) * D)
                            need(u, seen.setdefault(str(u), set()), off, D)
                            if t == 0 and k % 2 == 0:
                                pe.wait_ge(yT_ready, 4 * m + k // 2 + 1)
                            if (t, k) == (1, 0):
                                pe.wait_ge(yT_ready, 4 * m + 4)
                            for h in range(2):
                                e = mm3(ACC[2 * t + h][:, :], yT_hi[:, k, tok(t)], yT_lo[:, k, tok(t)], off + h * 512, 512, k == 0, k == KD - 1)
                            if (t, k) == (0, KD - 1):
                                e.then_inc(first_tile, 1)
                            elif t == T - 1 and k % 2 == 1:
                                e.then_inc(used[off // BLK], 1)
                            elif (t, k) == (T - 1, 6) and close2:
                                e.then_inc(used[2], 1)

            def sc_job(j0, jobs, j):
                kind, qt, g = jobs[j]
                nk = (qt + 1) * P
                if j >= 1:
                    pe.wait_ge(bias_done, j0 + j)
                for p in range(2):
                    half = slice(DH * p, DH * p + DH)
                    for i in range(2):
                        h, c = 4 * g + 2 * i + p, 2 * g + i
                        dst = bank[p][:, i * S:i * S + nk]
                        if kind == 2:
                            m = pe.matmul(dst, qkT_m[0:QK, 0, h, tok(qt)], qkT_m[0:QK, 1, h, 0:nk], start=True, stop=True, skip_group_check=True)
                        elif kind == 3:
                            pe.matmul(dst, nlogf[:, 0, h:h + 1].to_broadcast([P, P]), tri[:, 0:nk], start=True, stop=False, skip_group_check=True)
                            if qt:
                                pe.matmul(bank[p][:, i * S + P:i * S + nk], nlogf[:, 1, h:h + 1].to_broadcast([P, P]), tri[:, 0:P],
                                          start=False, stop=False, skip_group_check=True)
                            m = pe.matmul(dst, qT_h[half, c, tok(qt)], kT_h[half, c, 0:nk], start=False, stop=True, skip_group_check=True)
                        else:
                            m = pe.matmul(dst, qT[half, c, tok(qt)], kT[kind][half, g, 0:nk], start=True, stop=True, skip_group_check=True)
                m.then_inc(sc_done, 1)

            def pv_job(j0, jobs, j, v_copied):
                kind, qt, g = jobs[j]
                pe.wait_ge(pt_copied_a, j0 + j + 1)
                if v_copied is not None:
                    pe.wait_ge(pt_copied_v, v_copied)
                if j >= 1:
                    pe.wait_ge(o_done, j0 + j)
                for a in range(4):
                    h = 4 * g + 2 * (a % 2) + a // 2
                    for kt in range(qt + 1):
                        if kind < 2:
                            v = vsw[:, kt, P * kind + DH * g:P * kind + DH * g + DH]
                        elif kind == 2:
                            v = vm[:, kt, DH * h:DH * h + DH]
                        else:
                            v = qkv[:, kt, 1024 + DH * h:1024 + DH * h + DH]
                        m = pe.matmul(HT[:, a * DH:(a + 1) * DH], pT[j % 2][:, kt, a], v, start=kt == 0, stop=kt == qt, skip_group_check=True)
                m.then_inc(pv_done, 1)

            def jobs_run(j0, v0, jobs, beside=lambda j: None):
                nv = 0
                sc_job(j0, jobs, 0)
                for j, (kind, qt, g) in enumerate(jobs):
                    if j + 1 < len(jobs):
                        sc_job(j0, jobs, j + 1)
                    beside(j)
                    pe.wait_ge(exp_done, j0 + j + 1)
                    if j >= 1:
                        pe.wait_ge(pt_copied_a, j0 + j)
                    if nv:
                        pe.wait_ge(pt_copied_v, v0 + nv)
                    for kt in range(qt + 1):
                        for h in range(4):
                            m = pe.transpose(bank[4 + kt][:, h * P:(h + 1) * P], scores[j % 2][:, h // 2, h % 2, tok(kt)], ident)
                    m.then_inc(pt_psum, 1)
                    if j:
                        pv_job(j0, jobs, j - 1, v0 + nv if jobs[j - 1][1] else None)
                    nv += qt
                pv_job(j0, jobs, len(jobs) - 1, v0 + nv if jobs[-1][1] else None)

            def turn_rows(dst, src, cols, parts=P):
                for t in range(T):
                    m = pe.transpose(dst[0:parts, t * P:(t + 1) * P], src(t, cols), ident)
                return m

            pe.wait_ge(first_ready, 1)
            pe.wait_ge(cst_landed, 32)
            for s_ in used + [mod_step]:
                release(s_)
            pe.wait_ge(c_ready, 1)
            for st in range(ADA_STEPS):
                slot = st % len(first_w)
                pe.wait_ge(first_landed[slot], 16 * (st // len(first_w)) + 16)
                for h in range(2):
                    for k in range(KD):
                        m = pe.matmul(MOD[:, 2 * st + h:2 * st + h + 1], first_w[slot][:, k, h * P:(h + 1) * P], c_act[:, k:k + 1],
                                      start=k == 0, stop=k == KD - 1, skip_group_check=True)
                m.then_inc(mod_step, 1)

            with pe.Fori(0, DEPTH) as l:
                u_mix = l * LAYER_UNITS + FFN_UNITS
                norm(l * 3, l * 3)
                ffn(l * LAYER_UNITS, l * 2 * FFN_UNITS, FFN_UNITS, l * 3, l * 3 + 1)

                norm(l * 3 + 1, l * 3 + 1)
                stage = l * 3 + 2
                for m in range(2):
                    if m == 1:
                        pe.wait_ge(gate_ready, l * 6 + 4)
                    columns(u_mix + m, 768, 3 * m, stage * ADA_STEPS + 2 * m, 4 * m, stage if m == 0 else None,
                            first_of=l * 3 + 1 if m == 0 else None)
                pe.wait_ge(w_evac_a, l * 9 + 2)
                pe.wait_ge(w_evac_v, l * 3 + 1)
                columns(u_mix + 2, U2_COLS, 0, stage * ADA_STEPS + 4, 8, close=(0,))
                src = lambda t, cols: proj[:, t, cols]
                pe.wait_ge(lat_ready, l + 1)
                pe.wait_ge(w_evac_a, l * 9 + 4)
                pe.wait_ge(w_evac_v, l * 3 + 2)
                for c in range(5):
                    m = turn_rows(bank[2 + c // 2][:, (c % 2) * S:(c % 2) * S + S], src, slice(C_CQ + c * P, C_CQ + c * P + P))
                    if c in (1, 3, 4):
                        m.then_inc(cqT_psum, 1)
                pe.wait_ge(w_evac_a, l * 9 + 5)
                pe.wait_ge(w_evac_v, l * 3 + 3)
                for c in range(4):
                    m = turn_rows(bank[5 + c // 2][:, (c % 2) * S:(c % 2) * S + S], src, slice(C_Q + c * P, C_Q + c * P + P))
                    if c % 2:
                        m.then_inc(q_psum, 1)
                for kind, (c0, s_) in enumerate(((C_KS, ks_psum), (C_KW, kw_psum))):
                    for g in range(GROUPS):
                        for t in range(T):
                            for p in range(2):
                                m = pe.matmul(bank[kind][DH * p:DH * p + DH, g * S + t * P:g * S + (t + 1) * P],
                                              proj[:, t, c0 + g * DH:c0 + g * DH + DH], ident, start=True, stop=True,
                                              skip_group_check=True)
                    m.then_inc(s_, 1)
                pe.wait_ge(cqT_ready, l * 3 + 2)
                for k in range(2):
                    for g in range(GROUPS):
                        for t in range(T):
                            for p in range(2):
                                m = pe.matmul(bank[2 + k][DH * p:DH * p + DH, g * S + t * P:g * S + (t + 1) * P],
                                              proj[:, t, C_KC + (2 * k + g) * DH:C_KC + (2 * k + g + 1) * DH], ident,
                                              start=True, stop=True, skip_group_check=True)
                m.then_inc(c_psum, 1)
                pe.wait_ge(blocks_ready, l + 1)
                pe.wait_ge(cqT_ready, l * 3 + 3)
                carry_waits()
                for k in range(2):
                    for g in range(GROUPS):
                        for j in range(CMP_STRIDE):
                            m = pe.matmul(bank[4][DH * g:DH * g + DH, 16 * k:16 * k + N_CMP], cmpw[:, k, j * DH:(j + 1) * DH], blocks[:, 2 * k + g, j],
                                          start=j == 0, stop=j == CMP_STRIDE - 1, skip_group_check=True)
                m.then_inc(hidc_psum, 1)
                pe.wait_ge(hidc_ready, l + 1)
                pe.wait_ge(q_ready, l * 2 + 2)
                carry_waits()
                for g in range(GROUPS):
                    rows = slice(DH * g, DH * g + DH)
                    for p in range(2):
                        pe.matmul(bank[4 + g][DH * p:DH * p + DH, 0:N_CMP], lvec[rows, L_W2:L_W2 + DH], hid_cmp[rows, 0, 0:N_CMP],
                                  start=True, stop=True, skip_group_check=True)
                    for i in range(4):
                        m = pe.matmul(bank[4 + g][32 * i:32 * i + N_CMP, 64:128], hid_cmp[rows, 1, 0:N_CMP], lvec[rows, L_W2 + DH:L_W2 + 2 * DH],
                                      start=True, stop=True, skip_group_check=True)
                m.then_inc(kvc_psum, 1)
                pe.wait_ge(kvc_ready, l + 1)
                for p in range(2):
                    half = slice(DH * p, DH * p + DH)
                    for qt in range(2):
                        for i in range(4):
                            m = pe.matmul(bank[4 + p][:, 64 * qt + 16 * i:64 * qt + 16 * i + N_CMP], qT[half, i, tok(qt)], kT_cmp[half, i // 2, 0:N_CMP],
                                          start=True, stop=True, skip_group_check=True)
                m.then_inc(cs_psum, 1)
                pe.wait_ge(ks_ready, l + 1)
                pe.wait_ge(kw_ready, l + 1)
                seen = set()
                for b in range(4):
                    for k in range(3):
                        off = UQ_OFF + k * 768 + (b % 2) * 384
                        need(u_mix + 2, seen, off, 384)
                        m = mm3(bank[b][:, 0:384], cqT_hi[:, k, tok(b // 2)], cqT_lo[:, k, tok(b // 2)], off, 384, k == 0, k == 2)
                    m.then_inc(uq_psum, 1)
                for j in (1, 2):
                    release(used[j])
                pe.wait_ge(cp_exp, l + 1)
                for a in range(4):
                    m = pe.transpose(bank[6][:, a * P:(a + 1) * P], p_cmp[:, 4 * a:4 * a + 4, :], ident)
                m.then_inc(cp_psum, 1)
                need(u_mix + 3, set(), 0, BLK)
                for t in range(T):
                    for k in range(2):
                        m = mm3(bank[4 + t][:, :], cqT_hi[:, 3 + k, tok(t)], cqT_lo[:, 3 + k, tok(t)], k * 512, 512, k == 0, k == 1)
                    m.then_inc(uk_psum, 1)
                pe.wait_ge(cp_ready, l + 1)
                pe.wait_ge(uq_copied, l * 4 + 4)
                for i in range(4):
                    rows = slice(32 * i, 32 * i + N_CMP)
                    for qt in range(2):
                        for p in range(2):
                            m = pe.matmul(bank[i][:, 128 * qt + 64 * p:128 * qt + 64 * p + 64], pT_cmp[rows, 2 * p + qt], v_cmp[rows, i // 2],
                                          start=True, stop=True, skip_group_check=True)
                m.then_inc(co_psum, 1)
                for t in range(T):
                    if t == 1:
                        pe.wait_ge(uk_copied, l * 2 + 1)
                    for k in range(2):
                        m = mm3(bank[6 - 2 * t][:, :], cqT_hi[:, 3 + k, tok(t)], cqT_lo[:, 3 + k, tok(t)], 1024 + k * 512, 512, k == 0, k == 1)
                    m.then_inc(uv_psum, 1)
                release(used[0])
                pe.wait_ge(rope_done, l + 1)
                pe.wait_ge(co_done, l + 1)
                for b in range(4):
                    for i in range(2):
                        m = turn_rows(bank[b][:, i * S:i * S + S], lambda t, h: q_tok[:, t, h], 2 * b + i, QK)
                    m.then_inc(qm_psum, 1)
                pe.wait_ge(uk_copied, l * 2 + 2)
                for b in range(4):
                    if b == 1:
                        pe.wait_ge(uv_ready, l * 2 + 2)
                    if b == 3:
                        pe.wait_ge(km_ready, l * 4 + 1)
                    for i in range(2):
                        m = turn_rows(bank[K_BANKS[b]][:, i * S:i * S + S], lambda t, h: k_tok[:, t, h], 2 * b + i, QK)
                    m.then_inc(km_psum, 1)
                pe.wait_ge(qm_ready, l * 4 + 4)
                seen = {m: set() for m in (3, 4, 5)}

                def beside(j):
                    if j == 0:
                        pe.wait_ge(km_ready, l * 4 + 4)
                    if j % 3 == 0 and j:
                        pe.wait_ge(w_evac_a, l * 9 + 5 + j // 3)
                    for i, k in GATE_CHUNKS[j]:
                        m, off = gate_place(i, k)
                        need(u_mix + m, seen[m], off, 512)
                        for t in range(T):
                            e = mm3(bank[2 + t][:, :], uT_hi[:, k, tok(t)], uT_lo[:, k, tok(t)], off, 512, k == 0, k == KD - 1)
                        if k % 4 == 3:
                            e.then_inc(used[off // BLK], 1)
                        if k == KD - 1:
                            release(w_done)
                    if j % 2 == 1:
                        ada_step(stage * ADA_STEPS + 6 + j // 2, 12 + j - 1)

                jobs_run(l * NJ, l * 6, JOBS, beside)
                pe.wait_ge(w_evac_a, l * 9 + 9)
                pe.wait_ge(o_done, l * NJ + NJ)
                for b in range(4):
                    o = o_a if b < 2 else o_b
                    for i in range(2):
                        c = 2 * (b % 2) + i
                        m = turn_rows(bank[3 + b][:, i * S:i * S + S], lambda t, c_: o[:, t, c_], slice(c * P, c * P + P))
                    m.then_inc(oT_psum, 1)
                merge(u_mix + MIX_IN_UNITS, l, True)

                norm(l * 3 + 2, l * 3 + 2)
                ffn(l * LAYER_UNITS + FFN_UNITS + MIX_IN_UNITS + MERGE_UNITS, l * 2 * FFN_UNITS + FFN_UNITS, FFN_UNITS, l * 3 + 2, l * 3 + 3)

            n6, u = 3 * DEPTH, HYB_U0
            norm(n6, n6 + 1)
            evac_a = [2, 4, 6, 8, 9, 10, 11]
            for m in range(HYB_IN_UNITS):
                if m == 1:
                    pe.wait_ge(gate_ready, 2 * n6 + 2)
                if m >= 2:
                    pe.wait_ge(w_evac_a, DEPTH * 9 + evac_a[m - 2])
                    pe.wait_ge(w_evac_v, DEPTH * 3 + min(m - 1, 4))
                columns(u + m, 768 if m < 6 else 520, 3 * (m % 2), (n6 + 1) * ADA_STEPS + 2 * m if m < 6 else None, 4 * m,
                        n6 + 1 if m == 0 else None, first_of=n6 if m == 0 else None)
            pe.wait_ge(w_evac_a, DEPTH * 9 + 11)
            pe.wait_ge(u_ready, 1)
            for c in range(4):
                m = turn_rows(bank[4 + c // 2][:, (c % 2) * S:(c % 2) * S + S], lambda t, c_: u_tok[:, t, c_], slice(c * P, c * P + P))
                if c % 2:
                    m.then_inc(uc_psum, 1)
            for c in range(4):
                m = turn_rows(bank[6 - 3 * (c // 2)][:, (c % 2) * S:(c % 2) * S + S], lambda t, c_: xcb[:, t, c_],
                              slice(1024 + c * P, 1024 + c * P + P))
            m.then_inc(b_psum, 1)
            pe.wait_ge(qkn_ready, 1)
            for c in range(4):
                m = turn_rows(bank[c // 2][:, (c % 2) * S:(c % 2) * S + S], lambda t, c_: qkv[:, t, c_], slice(c * P, c * P + P))
                if c % 2:
                    m.then_inc(q_psum, 1)
            pe.wait_ge(uc_ready, 1)
            for c in range(4):
                m = turn_rows(bank[2 + 2 * (c // 2)][:, (c % 2) * S:(c % 2) * S + S], lambda t, c_: qkv[:, t, c_],
                              slice(512 + c * P, 512 + c * P + P))
                if c % 2:
                    m.then_inc(kh_psum, 1)
            pe.wait_ge(logf_ready, 1)
            pe.matmul(bank[5][:, 0:8], tri[:, 0:P], nlogf[:, 0], start=True, stop=True, skip_group_check=True)
            pe.matmul(bank[5][:, 8:16], ones, nlogf[:, 0], start=True, stop=False, skip_group_check=True)
            pe.matmul(bank[5][:, 8:16], tri[:, 0:P], nlogf[:, 1], start=False, stop=True, skip_group_check=True).then_inc(fcum_psum, 1)
            pe.wait_ge(q_ready, DEPTH * 2 + 2)
            pe.wait_ge(kh_ready, 2)
            pe.wait_ge(ya_hi_done, 2)
            pe.wait_ge(oT_ready, DEPTH * 4 + 2)
            pe.wait_ge(fcum_ready, 1)
            jobs_run(DEPTH * NJ, DEPTH * 6, HYB_JOBS)
            um = u + HYB_IN_UNITS
            pe.wait_ge(o_done, DEPTH * NJ + len(HYB_JOBS))
            for b in range(2):
                for i in range(2):
                    c = 2 * b + i
                    m = turn_rows(bank[5 + b][:, i * S:i * S + S], lambda t, c_: o_h[:, t, c_], slice(c * P, c * P + P))
                m.then_inc(oT_psum, 1)
            merge(um, DEPTH, False)
            norm(n6 + 1, n6 + 2)
            pe.wait_ge(uT_ready, 4 * n6 + 8)
            pe.wait_ge(gate_ready, 2 * n6 + 4)
            need(um + 2, set(), 2 * BLK, BLK)
            for t in range(T):
                for k in range(KD):
                    m = mm3(HT[:, 64 * t:64 * t + 36], uT_hi[:, k, tok(t)], uT_lo[:, k, tok(t)], 2 * BLK + 36 * k, 36, k == 0, k == KD - 1)
            m.then_inc(r_psum, 1)
            release(used[2])
            pe.wait_ge(sel_ready, 1)
            pe.matmul(GU[1][:, 0:4], ones, g_sel[:, 0], start=True, stop=False, skip_group_check=True)
            pe.matmul(GU[1][:, 0:4], ones, g_sel[:, 1], start=False, stop=True, skip_group_check=True)
            pe.matmul(GU[1][:, 4:8], tri[:, 0:P], g_sel[:, 0], start=True, stop=True, skip_group_check=True)
            pe.matmul(GU[1][:, 8:12], ones, g_sel[:, 0], start=True, stop=False, skip_group_check=True)
            pe.matmul(GU[1][:, 8:12], tri[:, 0:P], g_sel[:, 1], start=False, stop=True, skip_group_check=True).then_inc(count_psum, 1)
            pe.wait_ge(pick_ready, 1)
            for i, b in GATHERS:
                for k in range(KD):
                    for t in range(T):
                        m = pe.matmul(bank[b + k // 4][:, (k % 4) * P:(k % 4 + 1) * P], xn[:, t, k * P:(k + 1) * P], pick[:, t, i],
                                      start=t == 0, stop=t == T - 1, skip_group_check=True)
                    if k % 4 == 3:
                        m.then_inc(us_psum, 1)
            for i in range(3):
                for t in range(T):
                    dst = bank[6 + i // 2][:, (i % 2) * S + t * P:(i % 2) * S + (t + 1) * P]
                    pe.transpose(dst, pick[:, t, i], ident)
            pe.wait_ge(ew_ready, 1)
            for i in range(3):
                for t in range(T):
                    m = pe.matmul(bank[7][:, S + i * PER_GROUP:S + (i + 1) * PER_GROUP], pick[:, t, i], e_w[:, t],
                                  start=t == 0, stop=t == T - 1, skip_group_check=True)
            m.then_inc(pick_T_psum, 1)
            pe.wait_ge(usf_done_a, len(GATHERS))
            pe.wait_ge(usf_done_v, len(GATHERS))
            pe.wait_ge(pick_T_ready, 1)
            ffn(MOE_U0, MOE_F0, PER_GROUP, n6 + 1, None)

            def sparse_gate_up(u, i):
                seen = set()
                for k in range(KD):
                    need(u, seen, k * 512, 512, LAST_BEHIND)
                    m = mm3(GU[0][:, :], us_hi[i][:, k], us_lo[i][:, k], k * 512, 512, k == 0, k == KD - 1)
                    if k in (3, 7):
                        m.then_inc(used[k // 4], 1)

            def sparse_turn(f):
                pe.wait_ge(h_done, f * 2 + 2)
                for c in range(2):
                    m = pe.transpose(HT[:, c * P:(c + 1) * P], hid[:, 0, c * P:(c + 1) * P], ident)
                m.then_inc(hT_psum, 1)

            def sparse_down(u, f, order=LAST_BEHIND, done=None):
                pe.wait_ge(hT_ready, f + 1)
                need(u, set(), 2 * BLK, BLK, order)
                for c in range(2):
                    for h in range(2):
                        m = mm3(ACC[h][:, :], hTs_hi[:, c], hTs_lo[:, c], 2 * BLK + c * D + h * 512, 512, False, done is not None and c == 1)
                m.then_inc(used[2], 1)
                if done is not None:
                    pe.matmul(SPREAD[3][:, 0:1], zeros[:, 0:P], zeros[:, 0:1], start=done == 0, stop=True, skip_group_check=True).then_inc(ys_psum, 1)

            def clear_out():
                for h in range(2):
                    pe.matmul(ACC[h][:, :], zeros[:, 0:P], zeros[:, :], start=True, stop=False, skip_group_check=True)

            def spread(i):
                pe.wait_ge(ys_ready, i + 1)
                for t in range(T):
                    for h in range(2):
                        m = pe.matmul(SPREAD[2 * t + h][:, :], pick_T[:, i, tok(t)], y_s[i][:, h * 512:(h + 1) * 512],
                                      start=i == 0, stop=i == len(SPARSE) - 1, skip_group_check=True)
                    if i == len(SPARSE) - 1:
                        m.then_inc(first_tile if t == 0 else spread_done, 1)

            for s in SPARSE:
                u, f = MOE_U0 + s * PER_GROUP, MOE_F0 + s * PER_GROUP
                if s > 1:
                    sparse_turn(f - 1)
                pe.wait_ge(us_ready, s)
                sparse_gate_up(u, s - 1)
                if s > 1:
                    sparse_down(u - 1, f - 1, done=s - 2)
                sparse_turn(f)
                sparse_gate_up(u + 1, s - 1)
                if s > 1:
                    spread(s - 2)
                else:
                    pe.wait_ge(x_ready, 2 * (3 * DEPTH + 4))
                clear_out()
                sparse_down(u, f)
                with pe.Fori(2, PER_GROUP) as i:
                    sparse_turn(f + i - 1)
                    sparse_gate_up(u + i, s - 1)
                    sparse_down(u + i - 1, f + i - 1)
            sparse_turn(MOE_F0 + EXPERTS - 1)
            sparse_down(MOE_U0 + EXPERTS - 1, MOE_F0 + EXPERTS - 1, IN_LINE, done=len(SPARSE) - 1)
            spread(len(SPARSE) - 1)


def shape_constants():
    c = np.zeros((P, K_ALL), np.float32)
    q, k = np.arange(P)[:, None], np.arange(S)[None, :]
    c[:, K_ID:K_ID + 128] = np.eye(P)
    c[:, K_ONE:K_ONE + 128] = 1
    for t, (o, n) in enumerate(((0, P), (P, S))):
        d = (t * P + q) - k[:, :n]
        c[:, K_DIST + o:K_DIST + o + n] = np.where(d >= 0, -d, MASKED)
        c[:, K_MASK + o:K_MASK + o + n] = np.where(d >= 0, 0, MASKED)
    ends = np.arange(N_CMP) * CMP_STRIDE + CMP_BLOCK - 1
    b = np.zeros((P, 2, T, 4, 16), np.float32)
    for p in range(2):
        for t in range(T):
            for i in range(4):
                d = (t * P + q) - ends[None, :]
                b[:, p, t, i, :N_CMP] = np.where(d >= 0, -np.float32(SLOPES[2 * i + p]) * d.astype(np.float32), MASKED)
            c[:, K_VALID + t] = (t * P + np.arange(P)) >= CMP_BLOCK - 1
    c[:, K_CMPB:K_CMPB + 256] = b.reshape(P, 256)
    half = ROPE // 2
    inv = np.float32(10000.0) ** (-np.arange(half, dtype=np.float32) / half)
    ang = np.arange(S, dtype=np.float32)[:, None] * inv[None, :].astype(np.float32)
    for off, f in ((K_COS, np.cos), (K_SIN, np.sin)):
        v = np.tile(f(ang).astype(np.float32), (1, 2)).reshape(T, P, ROPE)
        c[:, off:off + 64] = v.transpose(1, 0, 2).reshape(P, 64)
    c[:, K_TRI:K_TRI + S] = (k >= q)
    c[:, K_TIE8:K_TIE8 + 64] = np.tril(np.ones((8, 8)), -1).reshape(1, 64)
    c[:, K_TIE4:K_TIE4 + 16] = np.tril(np.ones((4, 4)), -1).reshape(1, 16)
    c[:, K_PLACE:K_PLACE + P] = np.arange(P)
    c[:, K_BASE:] = 3 * PER_GROUP * np.arange(EXPERT_GROUPS)
    return c


def kernel(**inputs):
    import concourse.bacc as bacc
    from concourse.bass_utils import run_bass_kernel_spmd

    a = {n: np.asarray(v) for n, v in inputs.items()}

    def rows(w):
        return w.reshape(w.shape[0] // P, P, w.shape[1]).transpose(1, 0, 2)

    units = np.zeros((MOE_U0 + EXPERTS, P, UNIT), np.float32)
    at = [0]

    def put(*parts):
        o = 0
        for p_ in parts:
            flat = p_.reshape(P, -1)
            units[at[0], :, o:o + flat.shape[1]] = flat
            o += flat.shape[1]
        at[0] += 1

    def put_ffn(gate, up, down):
        gu = np.concatenate([rows(gate), rows(up)], axis=2)
        put(gu, rows(down))

    def put_merge(wa, wb, wo, tail=None):
        ra, rb, ro = rows(wa), rows(wb), rows(wo)
        put(ra, rb[:, 0:2])
        put(rb[:, 2:4], ro[:, 0:4])
        put(ro[:, 4:8], *([] if tail is None else [rows(tail)]))

    splits = np.cumsum([512, 128, 128, 128, 128, 128, 128, 24, 384, 256, 32])
    for l in range(DEPTH):
        for f in range(FFN_UNITS):
            s_ = slice(f * F_UNIT, (f + 1) * F_UNIT)
            put_ffn(a["ffn1_gate"][l][:, s_], a["ffn1_up"][l][:, s_], a["ffn1_down"][l][s_])
        q, kc, vc, ks, vs, kw, vw, gn, cq, ckv, kr, gm = np.split(a["w_in"][l], splits, axis=1)
        w = rows(np.concatenate([cq, ckv, kr, gn, kc, vc, ks, kw, q, vs, vw], axis=1))
        g = rows(gm)
        put(w[:, :, 0:768])
        put(w[:, :, 768:1536])
        put(w[:, :, 1536:], rows(a["mla_w_uq"][l]))
        sets = np.concatenate([g[:, :, i * 512:(i + 1) * 512].reshape(P, -1) for i in range(4)], axis=1)
        put(rows(a["mla_w_uk"][l]), rows(a["mla_w_uv"][l]), sets[:, :2 * BLK])
        put(sets[:, 2 * BLK:5 * BLK])
        put(sets[:, 5 * BLK:])
        put_merge(a["w_branch_a"][l], a["w_branch_b"][l], a["w_out"][l])
        for f in range(FFN_UNITS):
            s_ = slice(f * F_UNIT, (f + 1) * F_UNIT)
            put_ffn(a["ffn2_gate"][l][:, s_], a["ffn2_up"][l][:, s_], a["ffn2_down"][l][s_])
    xi, cb, cc, q, k, v, fl, ga, gb = np.split(a["w_in_2"][0], np.cumsum([512] * 6 + [8, D]), axis=1)
    w = rows(np.concatenate([xi, cc, cb, q, k, v, fl, ga, gb], axis=1))
    for m in range(HYB_IN_UNITS):
        put(w[:, :, 768 * m:768 * (m + 1)])
    put_merge(a["w_out_conv_2"][0], a["w_out_attn_2"][0], a["w_o_2"][0],
              np.concatenate([a["w_router_group_2"][0], a["w_router_expert_2"][0]], axis=1))
    for e in range(EXPERTS):
        put_ffn(a["w_gate_2"][0, e], a["w_up_2"][0, e], a["w_down_2"][0, e])
    assert at[0] == MOE_U0 + EXPERTS
    places = np.array([[3 * u + j for j in range(3)] for u in range(MOE_U0)])
    ffn_starts = [(l * LAYER_UNITS + o, FFN_UNITS) for l in range(DEPTH) for o in (0, LAYER_UNITS - FFN_UNITS)]
    for u0, n in ffn_starts:
        for u in range(u0, u0 + n + 1):
            for j in range(3):
                if (u, j) not in ((u0, 0), (u0, 1), (u0 + n, 2)):
                    places[u, j] = 3 * u + LAST_BEHIND[j]
    blocks = units.reshape(-1, P, 3, BLK).transpose(0, 2, 1, 3).reshape(-1, P, BLK)
    stream, experts = np.empty((MOE_U0 * 3, P, BLK), np.float32), np.ascontiguousarray(blocks[MOE_U0 * 3:])
    stream[places.reshape(-1)] = blocks[:MOE_U0 * 3]

    w_ada = np.concatenate([a["w_ada"].reshape(DEPTH, D, 3, 3 * D).transpose(0, 2, 1, 3).reshape(-1, D, 3 * D),
                            a["w_ada_2"][0].reshape(D, 2, 3 * D).transpose(1, 0, 2)], axis=0)
    ada = np.ascontiguousarray(w_ada.reshape(STAGES, P, KD, ADA_STEPS, ADA_COLS).transpose(0, 3, 1, 2, 4)
                               .reshape(STAGES * ADA_STEPS, P, KD, ADA_COLS))

    def cols(v):
        return v.reshape(-1, P).T

    vecs = np.zeros((P, V_ALL), np.float32)
    vecs[:, V_C:V_C + 8] = a["c"][0].reshape(P, KD)
    vecs[:, V_C + 8:V_C + 16] = a["c_2"][0].reshape(P, KD)
    vecs[:, V_BADA:V_BADA + STAGES * 24] = cols(np.concatenate([a["b_ada"].reshape(-1), a["b_ada_2"].reshape(-1)]))
    vecs[:, V_N1:V_N1 + 8] = cols(a["norm1_w_2"][0])
    vecs[:, V_N2:V_N2 + 8] = cols(a["norm2_w_2"][0])
    vecs[:, V_CONV:V_CONV + 12] = a["conv_w_2"][0].reshape(3, 4, P).transpose(2, 1, 0).reshape(P, 12)
    vecs[:, V_QN] = np.tile(a["q_norm_w_2"][0], 2)
    vecs[:, V_KN] = np.tile(a["k_norm_w_2"][0], 2)
    vecs[:, V_BF:V_BF + 8] = a["b_forget_2"][0][None, :]
    vecs[:, V_BR:V_BR + 36] = np.concatenate([a["b_router_group_2"][0], a["b_router_expert_2"][0]])[None, :]
    layer_vecs = np.zeros((DEPTH, P, L_ALL), np.float32)
    cmp_w1 = np.zeros((DEPTH, P, 2, CMP_STRIDE * DH), np.float32)
    for l in range(DEPTH):
        for k_, n in enumerate(("cmpk", "cmpv")):
            layer_vecs[l, :, L_PE + CMP_STRIDE * k_:L_PE + CMP_STRIDE * (k_ + 1)] = (
                a[n + "_pe"][l].reshape(2, CMP_STRIDE, DH).transpose(0, 2, 1).reshape(P, CMP_STRIDE))
            layer_vecs[l, :, L_W2 + DH * k_:L_W2 + DH * k_ + DH] = np.tile(a[n + "_w2"][l], (2, 1))
            w1 = a[n + "_w1"][l].reshape(2, CMP_STRIDE, DH, DH).transpose(0, 2, 1, 3)
            cmp_w1[l, :, k_] = w1.reshape(P, CMP_STRIDE * DH)
        layer_vecs[l, :, L_QN:L_QN + 3] = cols(a["mla_q_norm"][l])
        layer_vecs[l, :, L_KVN:L_KVN + 2] = cols(a["mla_kv_norm"][l])
    arrays = {
        "weight_stream": stream, "expert_blocks": experts, "ada_steps": ada, "shape_constants": shape_constants(), "vectors": vecs,
        "layer_vectors": layer_vecs, "compress_w1": cmp_w1,
        "final_norm_rows": np.ascontiguousarray(np.broadcast_to(a["final_norm"], (P, D))),
        "tokens": np.ascontiguousarray(a["x"][0]),
    }
    nc = bacc.Bacc("TRN2", target_bir_lowering=False, num_devices=1)
    args = [nc.dram_tensor(n, v_.shape, mybir.dt.from_np(v_.dtype), kind="ExternalInput").ap() for n, v_ in arrays.items()]
    out = nc.dram_tensor("out", (S, D), F32, kind="ExternalOutput").ap()
    program(nc, *args, out)
    r = run_bass_kernel_spmd(nc, [arrays], core_ids=[0])
    return r.results[0]["out"].reshape(1, S, D)
```

```python
import numpy as np
from contextlib import ExitStack

import concourse.bass as bass
from concourse import mybir

F32 = mybir.dt.float32
F32R = mybir.dt.float32r
BF16 = mybir.dt.bfloat16
ALU = mybir.AluOpType
ACT = mybir.ActivationFunctionType
AX = mybir.AxisListType

P = 128
S = 256
T = S // P
D = 1024
KD = D // P
DEPTH = 2
HEADS = 8
DH = 64
GROUPS = 2
F_UNIT = 256
D_FF = 2816
FFN_UNITS = D_FF // F_UNIT
EXPERTS = 32
EXPERT_GROUPS = 4
PER_GROUP = EXPERTS // EXPERT_GROUPS
CMP_BLOCK, CMP_STRIDE = 32, 16
N_CMP = S // CMP_STRIDE - 1
Q_RANK, KV_RANK, ROPE, NOPE = 384, 256, 32, 64
QK = NOPE + ROPE
EPS = 1e-6
MASKED = -1e30

BLK = 2048
UNIT = 3 * BLK
MIX_IN_UNITS, MERGE_UNITS = 6, 3
LAYER_UNITS = 2 * FFN_UNITS + MIX_IN_UNITS + MERGE_UNITS
HYB_IN_UNITS = 7
HYB_U0 = DEPTH * LAYER_UNITS
MOE_U0 = HYB_U0 + HYB_IN_UNITS + MERGE_UNITS
MOE_F0 = DEPTH * 2 * FFN_UNITS
TILE_GROUPS = EXPERT_GROUPS + 1

IN_LINE, LAST_BEHIND = (0, 1, 2), (-1, 0, 4)
LAST_UNIT = (-1, 0, 3)

ADA_COLS = 256
ADA_STEPS = 3 * D // ADA_COLS
STAGES = 3 * DEPTH + 2

C_CQ, C_CKV, C_KR, C_GN, C_KC, C_KS, C_KW, C_Q, C_V = 0, 384, 640, 672, 696, 952, 1080, 1208, 1720
PROJ = C_V
MIX_COLS = 1976
U2_COLS = MIX_COLS - 2 * 768
UQ_OFF = 3520
HYB_QKV = 1536

K_ID, K_ONE, K_DIST, K_MASK, K_CMPB, K_COS, K_SIN, K_VALID, K_TRI, K_TIE8, K_TIE4, K_PLACE, K_BASE = np.cumsum(
    [0, 128, 128, 384, 384, 256, 64, 64, 2, 256, 64, 16, 128]).tolist()
K_ALL = K_BASE + EXPERT_GROUPS
V_C, V_BADA, V_GAIN, V_HALF, V_N2, V_CONV, V_QN, V_KN, V_BF, V_BR = np.cumsum(
    [0, 16, STAGES * 24, 8 * DEPTH, DEPTH, 8, 12, 1, 1, 8]).tolist()
V_ALL = V_BR + 36
L_PE, L_W2, L_QN, L_KVN = 0, 32, 160, 163
L_ALL = 165

SLOPES = [2.0 ** (-8.0 * (h + 1) / HEADS) for h in range(HEADS)]
CHAIN_PER_LAYER = 64


def program(nc, stream, experts, ada, consts, vecs, layer_vecs, cmp_w1, fnorm, x_in, out):
    ctx = ExitStack()
    with ctx:
        def sb(name, shape, dt=F32):
            return ctx.enter_context(nc.sbuf_tensor(name, shape, dt))

        def sem(name):
            return ctx.enter_context(nc.semaphore(name))

        raw = sb("raw", [P, UNIT])
        w_hi = sb("w_hi", [P, UNIT], F32R)
        w_lo = sb("w_lo", [P, UNIT], F32R)
        x = sb("x", [P, T, D])
        uT_hi = sb("uT_hi", [P, KD, S], F32R)
        uT_lo = sb("uT_lo", [P, KD, S], F32R)
        gate_bc = sb("gate_bc", [P, D])
        ada_w = sb("ada_w", [P, 2, KD, ADA_COLS])
        ada_sum = sb("ada_sum", [P, ADA_COLS])
        cst = sb("cst", [P, K_ALL])
        vec = sb("vec", [P, V_ALL])
        c_act = sb("c_act", [P, 16])
        lvec = sb("lvec", [P, L_ALL])
        modf = sb("modf", [P, 24])
        stat = sb("stat", [P, 112])
        zeros = sb("zeros", [P, 512], BF16)
        cmpw = sb("cmpw", [P, 2, 2048])
        further = sb("further", [P, 2], mybir.dt.int32)
        r_arena = sb("r_arena", [P, 4096], F32R)
        arena = sb("arena", [P, 11776])

        def at(off, *shape, parts=P):
            n = int(np.prod(shape))
            v = arena[0:parts, off:off + n]
            if len(shape) == 2:
                return v.rearrange("p (a b) -> p a b", a=shape[0])
            if len(shape) == 3:
                return v.rearrange("p (a b c) -> p a b c", a=shape[0], b=shape[1])
            if len(shape) == 4:
                return v.rearrange("p (a b c d) -> p a b c d", a=shape[0], b=shape[1], c=shape[2])
            return v

        def rat(off, a, b):
            return r_arena[:, off:off + a * b].rearrange("p (a b) -> p a b", a=a)

        ident = cst[:, K_ID:K_ID + 128]
        ones = cst[:, K_ONE:K_ONE + 128]
        dist = [cst[:, K_DIST:K_DIST + 128], cst[:, K_DIST + 128:K_DIST + 384]]
        mask = [cst[:, K_MASK:K_MASK + 128], cst[:, K_MASK + 128:K_MASK + 384]]
        cmp_bias = cst[:, K_CMPB:K_CMPB + 256].rearrange("p (a q i n) -> p a q i n", a=2, q=2, i=4)
        cos2 = cst[:, K_COS:K_COS + 64].rearrange("p (t r) -> p t r", t=T)
        sin2 = cst[:, K_SIN:K_SIN + 64].rearrange("p (t r) -> p t r", t=T)
        cmp_valid = cst[:, K_VALID:K_VALID + 2]
        tri = cst[:, K_TRI:K_TRI + 256]
        tie8 = cst[:, K_TIE8:K_TIE8 + 64].rearrange("p (a b) -> p a b", a=8)
        tie4 = cst[:, K_TIE4:K_TIE4 + 16].rearrange("p (a b) -> p a b", a=4)

        ss, ms, sq, rstd = stat[:, 0:2], stat[:, 2:4], stat[:, 4:6], stat[:, 6:8]
        lss, lms, lsq, lrs = stat[:, 8:12], stat[:, 12:16], stat[:, 16:20], stat[:, 20:24]
        nmax = [stat[:, 24:28], stat[:, 28:32]]
        psum_row = [stat[:, 96 + 4 * i:100 + 4 * i] for i in range(4)]
        pad = stat[:, 32:33]
        rsum, coef = stat[:, 40:44], stat[:, 44:48]
        cmax, csum, crec, ccoef = (at(11136, 16), at(11152, 16), at(11168, 16), at(11184, 16))
        nsa_gate = stat[:, 48:96].rearrange("p (t h k) -> p t h k", t=T, h=HEADS)

        xn, uTf, diag = at(0, T, D), at(2048, KD, S), at(4096, KD, P)
        first_w = [at(5120, KD, ADA_COLS), at(5120 + BLK, KD, ADA_COLS), ada_w[:, 0], ada_w[:, 1], at(5120 + 2 * BLK, KD, ADA_COLS)]
        first_row = cmpw[0:1, :, :].rearrange("p k c -> p (k c)")
        act_g, hid = at(6144, T, F_UNIT), at(6656, T, F_UNIT)
        hT_hi, hT_lo = rat(0, 2, S), rat(512, 2, S)
        upd = at(2048, T, 2, 512)
        proj = at(0, T, PROJ)
        vsw = at(4096, T, 256)
        qT = at(4608, 4, S)
        kT = [at(5632, 2, S), at(6144, 2, S)]
        cT = at(9728, 2 * GROUPS, S)
        blocks = at(7168, 2 * GROUPS, CMP_STRIDE, N_CMP)
        p_cmp = at(7168, 16, 32)
        pT_cmp = at(7680, 4, P)
        hid_cmp, kT_cmp, v_cmp = at(8128, 2, GROUPS, 16), at(8192 + 96, 2, 16), at(8192 + 128, 2, DH)
        vm = at(8704, T, HEADS * DH)
        o_a, o_b = at(9728, T, 512), at(10752, T, 512)
        o_tmp = at(10752, 4, DH)
        lat_squares = at(9728, T, Q_RANK + KV_RANK)
        q_tok, k_tok = at(0, T, HEADS, QK), at(1536, T, HEADS, QK)
        rope_a, rope_b = at(9728, T, HEADS, ROPE), at(9728 + 512, T, HEADS, ROPE)
        kr_a, kr_b = at(10752, T, ROPE), at(10816, T, ROPE)
        qkT_m = cmpw[:, :, :].rearrange("p k (h s) -> p k h s", h=HEADS)
        scores = [at(0, 2, 2, S), at(1024, 2, 2, S)]
        pT = [at(2048, 2, 4, P), at(3072, 2, 4, P)]
        gates_m = [at(6656, T, 512), at(7680, T, 512), at(4096, T, 512), at(5120, T, 512)]
        y, ytmp = at(0, T, D), at(2048, T, 2, 512)
        cqT_hi, cqT_lo = rat(0, 5, S), rat(1280, 5, S)
        oT_hi = [rat(0, 4, S), rat(2048, 4, S)]
        oT_lo = [rat(1024, 4, S), rat(3072, 4, S)]
        yT_hi, yT_lo = uT_hi, uT_lo
        fn_bc = at(8192, D)
        xcb = at(0, T, 1536)
        qkv = at(4096, T, HYB_QKV)
        gates_h = at(7168, T, 2 * D)
        gate_sets_h = [gates_h[:, :, i * 512:(i + 1) * 512] for i in range(4)]
        f_row = at(11264, T, 8)
        f_e, f_l, f_cum = at(11280, T, 8), at(11296, T, 8), at(11312, T, 8)
        nlogf = at(11328, T, 8)
        qk_ss, qk_gain = at(11344, 32), at(11376, 4)
        qT_h = cmpw[:, 0, 0:1024].rearrange("p (c s) -> p c s", c=4)
        kT_h = cmpw[:, 0, 1024:2048].rearrange("p (c s) -> p c s", c=4)
        u_tok = cmpw[:, 1, 0:1024].rearrange("p (t s) -> p t s", t=T)
        squares = cmpw[:, 1, 1024:2048].rearrange("p (t s) -> p t s", t=T)
        uTc = at(0, 4, S + 2)
        conv = at(1056, 4, S)
        o_h = qkv[:, :, 0:512]
        r0 = 8192
        logits = at(r0, T, 36)
        g_gt, g_eq = at(r0 + 128, T, 4, 4), at(r0 + 160, T, 4, 4)
        g_rank, g_sel = at(r0 + 192, T, 4), at(r0 + 200, T, 4)
        g_max, g_exp, g_sum, p_sel = at(r0 + 208, T), at(r0 + 212, T, 4), at(r0 + 220, T), at(r0 + 224, T)
        le_m, le_g = at(r0 + 256, T, 4, 8), at(r0 + 320, T, 8)
        e_gt, e_eq = at(r0 + 384, T, 8, 8), at(r0 + 512, T, 8, 8)
        e_rank, e_max, e_exp, e_sum, e_w = (at(r0 + 640, T, 8), at(r0 + 656, T), at(r0 + 660, T, 8),
                                            at(r0 + 676, T), at(r0 + 680, T, 8))
        g_cum, g_total, g_over, g_base = at(r0 + 720, T, 4), at(r0 + 728, 4), at(r0 + 732, 4), at(r0 + 736, 4)
        own_place, over = at(r0 + 740, T), at(r0 + 742, 2)
        sparse_w = at(r0 + 848, EXPERT_GROUPS, PER_GROUP)
        pick, pick_T = at(9216, T, EXPERT_GROUPS, P), at(10240, EXPERT_GROUPS, S)
        usf = [at(2048 + i * D, KD, P) for i in range(EXPERT_GROUPS)]
        us_hi = [rat(1024, KD, P), uT_hi[:, :, 0:P], uT_hi[:, :, P:S], rat(1024, KD, P)]
        us_lo = [rat(2048, KD, P), uT_lo[:, :, 0:P], uT_lo[:, :, P:S], rat(2048, KD, P)]
        hTs_hi, hTs_lo = rat(0, 2, P), rat(512, 2, P)
        y_s = [at(2048 + (0, D, 0, D, D)[n], D) for n in range(TILE_GROUPS)]
        group_iota = cst[:, K_BASE:K_BASE + EXPERT_GROUPS]
        place_iota = cst[:, K_PLACE:K_PLACE + P]

        bank = [ctx.enter_context(nc.psum_tensor(f"bank{i}", [P, 512], F32)) for i in range(8)]
        ACC, GU, HT, MOD = bank[0:4], bank[4:6], bank[6], bank[7]
        YT = [(bank[4], bank[5]), (bank[6], bank[3])]
        SPREAD = [bank[2], bank[3], bank[5], bank[7]]

        landed = [sem(f"block_landed{r}") for r in range(3)]
        hi_done, split_done = sem("blocks_hi"), sem("blocks_split")
        used = [sem(f"block_used{j}") for j in range(3)]
        far_landed = [sem(f"far_block_landed{r}") for r in range(3)]
        x_landed, cst_landed, vec_landed, fn_landed = sem("x_landed"), sem("cst_landed"), sem("vec_landed"), sem("fn_landed")
        lvec_landed, out_landed = sem("lvec_landed"), sem("out_landed")
        ada_landed = [sem("ada_landed0"), sem("ada_landed1")]
        first_landed = [sem(f"first_landed{i}") for i in range(5)]
        first_used, first_psum, first_copied = sem("first_used"), sem("first_psum"), sem("first_copied")
        c_ready, ada_chain, ada_ready = sem("c_ready"), sem("ada_chain"), sem("ada_ready")
        mod_step, mod_ready = sem("mod_step"), sem("mod_ready")
        x_ready, ss_done, ms_done, sq_done = sem("x_ready"), sem("ss_done"), sem("ms_done"), sem("sq_done")
        rstd_done, xn_done = sem("rstd_done"), sem("xn_done")
        diag_done, gate_psum, gate_ready = sem("diag_done"), sem("gate_psum"), sem("gate_ready")
        uT_psum, uTf_done_a, uTf_done_v = sem("uT_psum"), sem("uTf_done_a"), sem("uTf_done_v")
        uT_hi_done, uT_ready = sem("uT_hi_done"), sem("uT_ready")
        gu0_done, silu_done, h_done = sem("gu0_done"), sem("silu_done"), sem("h_done")
        hT_psum, hT_hi_done, hT_ready = sem("hT_psum"), sem("hT_hi_done"), sem("hT_ready")
        chain = sem("vector_chain")
        w_done, w_evac_a, w_evac_v = sem("w_done"), sem("w_evac_a"), sem("w_evac_v")
        lat_ss, lat_ms, lat_sq, lat_ready = sem("lat_ss"), sem("lat_ms"), sem("lat_sq"), sem("lat_ready")
        nsa_gate_ready = sem("nsa_gate_ready")
        cqT_psum, cqT_hi_done, cqT_ready = sem("cqT_psum"), sem("cqT_hi_done"), sem("cqT_ready")
        q_psum, ks_psum, kw_psum, c_psum = sem("q_psum"), sem("ks_psum"), sem("kw_psum"), sem("c_psum")
        q_ready, ks_ready, kw_ready, blocks_ready = sem("q_ready"), sem("ks_ready"), sem("kw_ready"), sem("blocks_ready")
        hidc_psum, hidc_ready, kvc_psum, kvc_ready = sem("hidc_psum"), sem("hidc_ready"), sem("kvc_psum"), sem("kvc_ready")
        uq_psum, uk_psum, uv_psum = sem("uq_psum"), sem("uk_psum"), sem("uv_psum")
        uq_copied, uk_copied, uv_ready, rope_done = sem("uq_copied"), sem("uk_copied"), sem("uv_ready"), sem("rope_done")
        qm_psum, km_psum, qm_ready, km_ready = sem("qm_psum"), sem("km_psum"), sem("qm_ready"), sem("km_ready")
        cs_psum, cs_ready, cp_exp, cp_psum, cp_ready, co_psum, co_done = (
            sem("cs_psum"), sem("cs_ready"), sem("cp_exp"), sem("cp_psum"), sem("cp_ready"), sem("co_psum"), sem("co_done"))
        sc_done, bias_done, nmax_done, exp_done = sem("sc_done"), sem("bias_done"), sem("nmax_done"), sem("exp_done")
        pt_psum, pt_copied_a, pt_copied_v, pv_done, o_done = (
            sem("pt_psum"), sem("pt_copied_a"), sem("pt_copied_v"), sem("pv_done"), sem("o_done"))
        oT_psum, oT_hi_done, oT_ready = sem("oT_psum"), sem("oT_hi_done"), sem("oT_ready")
        pa_psum, ya_done, pb_psum, y_ready = sem("pa_psum"), sem("ya_done"), sem("pb_psum"), sem("y_ready")
        yT_psum, yT_hi_done, yT_ready = sem("yT_psum"), sem("yT_hi_done"), sem("yT_ready")
        u_ready, uc_psum, uc_ready, b_psum, ya_f32, ya_hi_done = (
            sem("u_ready"), sem("uc_psum"), sem("uc_ready"), sem("b_psum"), sem("ya_f32"), sem("ya_hi_done"))
        f_exp, f_exp_in, f_ln, f_ln_in, logf_ready, fcum_psum, fcum_ready = (
            sem("f_exp"), sem("f_exp_in"), sem("f_ln"), sem("f_ln_in"), sem("logf_ready"), sem("fcum_psum"), sem("fcum_ready"))
        qkn_ms, qkn_sq, qkn_ready, kh_psum, kh_ready = (
            sem("qkn_ms"), sem("qkn_sq"), sem("qkn_ready"), sem("kh_psum"), sem("kh_ready"))
        r_psum, r_exp_in, r_exp = sem("r_psum"), sem("r_exp_in"), sem("r_exp")
        sel_ready, count_psum, further_ready, pick_ready = sem("sel_ready"), sem("count_psum"), sem("further_ready"), sem("pick_ready")
        ew_ready, pick_T_psum, pick_T_ready = sem("ew_ready"), sem("pick_T_psum"), sem("pick_T_ready")
        sw_psum, sw_ready = sem("sparse_w_psum"), sem("sparse_w_ready")
        us_psum, usf_done_a, usf_done_v, us_hi_done, us_ready = (
            sem("us_psum"), sem("usf_done_a"), sem("usf_done_v"), sem("us_hi_done"), sem("us_ready"))
        ys_psum, ys_ready, spread_done = sem("ys_psum"), sem("ys_ready"), sem("spread_done")
        first_ready = sem("first_ready")
        first_tile = sem("first_tile")

        NSA_JOBS = [(k, qt, g) for k in (0, 1) for qt in (1, 0) for g in (0, 1)]
        MLA_JOBS = [(2, qt, g) for qt in (1, 0) for g in (0, 1)]
        JOBS = NSA_JOBS + MLA_JOBS
        HYB_JOBS = [(3, qt, g) for qt in (1, 0) for g in (0, 1)]
        NJ = len(JOBS)
        K_BANKS = (5, 6, 4, 5)
        GATE_CHUNKS = [[(j // 3, k) for k in ((0, 1, 2), (3, 4, 5), (6, 7))[j % 3]] for j in range(NJ)]
        JOB_SPLITS = {0: (4, 0), 2: (4, 1), 3: (4, 2), 5: (5, 0), 6: (5, 1), 8: (5, 2), 9: (6, 0), 11: (6, 1)}

        def gate_place(i, k):
            at_ = 3 * UNIT + BLK + (i * KD + k) * 512
            return at_ // UNIT, at_ % UNIT
        GATHER_BANKS = [(2, 3), (0, 1), (2, 3), (5, 7)]

        far = [ada_w[:, i].rearrange("p k c -> p (k c)") for i in range(2)] + [cmpw[:, 1]]

        def expert_place(half, odd, j, order):
            at_ = 3 * odd + order[j]
            r, turn_ = at_ % 6, half + at_ // 6
            if r < 3:
                return far[r], far_landed[r], turn_ * 16 + 16
            return raw[:, (r - 3) * BLK:(r - 2) * BLK], landed[r - 3], (MOE_U0 + turn_) * 16 + 16

        def after(half, odd):
            return (half, 1) if not odd else (half + 1, 0)

        def f32(ap):
            return ap.bitcast(F32)

        block = ctx.enter_context(nc.Block())

        @block.sync
        def _(sp):
            sp.dma_start(vec[:, :], vecs).then_inc(vec_landed, 16)
            for st in range(ADA_STEPS):
                slot = st % len(first_w)
                if st >= len(first_w):
                    sp.wait_ge(first_used, st - len(first_w) + 1)
                sp.dma_start(first_w[slot], ada[st]).then_inc(first_landed[slot], 16)
                if st == 2:
                    sp.dma_start(cst[:, :], consts).then_inc(cst_landed, 16)
                if st == 4:
                    sp.dma_start(x[:, :, :], x_in.rearrange("(t p) d -> p t d", p=P)).then_inc(x_landed, 16)
                if st in (7, 8):
                    j = st - 7
                    sp.dma_start(raw[:, j * BLK:(j + 1) * BLK], stream[j]).then_inc(landed[j], 16)
            sp.dma_start(raw[:, 2 * BLK:], stream[2]).then_inc(landed[2], 16)

            def load_stream(first, end):
                with sp.Fori(first, end) as i:
                    for r in range(3):
                        sp.wait_ge(split_done, i * 3 + r - 2)
                        sp.dma_start(raw[:, r * BLK:(r + 1) * BLK], stream[i * 3 + r]).then_inc(landed[r], 16)

            def load(half, odd, i, j, at_, order=LAST_BEHIND, again=True):
                if again:
                    sp.wait_ge(split_done, (MOE_U0 + half * 2 + odd) * 3 + order[j] - 5)
                place, sem_, _ = expert_place(half, odd, j, order)
                sp.dma_start(place, experts[at_ + (i * 3 + j)]).then_inc(sem_, 16)

            def load_first(half, at_, again):
                load(half, 0, 0, 0, at_, IN_LINE, again)
                load(half, 0, 0, 1, at_, IN_LINE, again)
                load(half, 1, 1, 0, at_, again=again)

            def load_rest(half, n, at_):
                with sp.Fori(0, n // 2 - 1) as i:
                    for odd in (1, 0):
                        v = i * 2 + (2 - odd)
                        load(i + (half + 1 - odd), odd, v, 1, at_)
                        load(i + half, 1 - odd, v - 1, 2, at_)
                        load(i + (half + 1), 1 - odd, v + 1, 0, at_)
                h = half + n // 2 - 1
                load(h, 1, n - 1, 1, at_)
                load(h, 0, n - 2, 2, at_)
                load(h, 1, n - 1, 2, at_, IN_LINE)

            load_stream(1, MOE_U0 - 2)
            sp.wait_ge(mod_step, STAGES * ADA_STEPS + 1)
            sp.wait_ge(uc_psum, 2)
            sp.wait_ge(qkn_ms, 1)
            load_first(0, 0, False)
            load_stream(MOE_U0 - 2, MOE_U0)
            load_rest(0, EXPERTS, 0)
            sp.wait_ge(further_ready, 1)
            first_block = sp.value_load(further[0:1, 0:1], min_val=0, max_val=3 * (EXPERTS - PER_GROUP))
            with sp.If(sp.value_load(further[0:1, 1:2], min_val=0, max_val=1) > 0):
                load_first(EXPERTS // 2, first_block, True)
                load_rest(EXPERTS // 2, PER_GROUP, first_block)
                sp.wait_ge(x_ready, 2 * (3 * DEPTH + 5))
            sp.wait_ge(x_ready, 2 * (3 * DEPTH + 4))
            sp.dma_start(out.rearrange("(t p) d -> p t d", p=P), x[:, :, :]).then_inc(out_landed, 16)
            sp.wait_ge(out_landed, 16)

        @block.gpsimd
        def _(pool):
            first_pair = ADA_STEPS // 2

            def load(n, slot):
                pool.dma_start(ada_w[:, slot], ada[n]).then_inc(ada_landed[slot], 16)

            def step(pair, slot, c0, ahead):
                n = pair * 2 + slot
                w = ada_w[:, slot]
                done = (pair - first_pair) * 2 + slot
                pool.wait_ge(ada_landed[slot], (pair - first_pair) * 16 + 16)
                nc.gpsimd.tensor_tensor(w, w, c_act[:, c0:c0 + 8].unsqueeze(2).to_broadcast([P, KD, ADA_COLS]),
                                        ALU.mult).then_inc(ada_chain, 1)
                pool.wait_ge(ada_chain, done * 3 + 1)
                nc.gpsimd.tensor_tensor(w[:, 0:4], w[:, 0:4], w[:, 4:8], ALU.add).then_inc(ada_chain, 1)
                pool.wait_ge(ada_chain, done * 3 + 2)
                nc.gpsimd.tensor_tensor(w[:, 0:2], w[:, 0:2], w[:, 2:4], ALU.add).then_inc(ada_chain, 1)
                pool.wait_ge(ada_chain, done * 3 + 3)
                pool.wait_ge(mod_step, n + 1)
                nc.gpsimd.tensor_tensor(ada_sum[:, :], w[:, 0], w[:, 1], ALU.add).then_inc(ada_ready, 1)
                if ahead:
                    pool.wait_ge(ada_ready, done + 1)
                    load(n + 2, slot)

            for slot in range(2):
                pool.wait_ge(first_used, ADA_STEPS - 4 + slot)
                load(ADA_STEPS + slot, slot)
            pool.wait_ge(c_ready, 1)
            c2_pair, end_pair = DEPTH * 3 * ADA_STEPS // 2, STAGES * ADA_STEPS // 2
            with pool.Fori(first_pair, c2_pair) as pair:
                for slot in range(2):
                    step(pair, slot, 0, True)
            with pool.Fori(c2_pair, end_pair - 1) as pair:
                for slot in range(2):
                    step(pair, slot, 8, True)
            for slot in range(2):
                step(end_pair - 1, slot, 8, False)

        @block.scalar
        def _(act):
            def split(u, js, order=IN_LINE):
                for j in js:
                    r = (order[j] + 3) % 3
                    act.wait_ge(landed[r], (u + (order[j] - r) // 3) * 16 + 16)
                    act.wait_ge(used[j], u + 1)
                    act.activation(w_hi[:, j * BLK:(j + 1) * BLK], raw[:, r * BLK:(r + 1) * BLK], ACT.Copy).then_inc(hi_done, 1)

            def expert_split(half, odd, js, order=LAST_BEHIND):
                for j in js:
                    place, sem_, count = expert_place(half, odd, j, order)
                    act.wait_ge(sem_, count)
                    act.wait_ge(used[j], half * 2 + (MOE_U0 + odd + 1))
                    act.activation(w_hi[:, j * BLK:(j + 1) * BLK], place, ACT.Copy).then_inc(hi_done, 1)

            def sqrt_ahead(i):
                act.activation(stat[:, 33 + i:34 + i], ones[:, 0:1], ACT.Sqrt)

            def rms_squares(q, late=None):
                for t in range(T):
                    act.wait_ge(x_ready, 2 * q + t + 1)
                    act.activation(xn[:, t], x[:, t], ACT.Square, accum_out=ss[:, t:t + 1]).then_inc(ss_done, 1)
                    act.wait_ge(ms_done, 2 * q + t + 1)
                    act.activation(sq[:, t:t + 1], ms[:, t:t + 1], ACT.Sqrt).then_inc(sq_done, 1)
                    if late is not None:
                        split(late, (t,))

            def norm(q, n, late=None):
                rms_squares(q, late)
                act.wait_ge(mod_ready, n + 1)
                for b in range(4):
                    if b % 2 == 0:
                        act.wait_ge(uT_psum, 4 * n + b + 2)
                        for k in (2 * b + 2, 2 * b + 3):
                            e = act.activation(uTf[:, k], ACC[b + 1][:, (k % 2) * S:(k % 2) * S + S], ACT.Identity,
                                               scale=modf[:, 8 + k:9 + k], bias=modf[:, k:k + 1])
                        e.then_inc(uTf_done_a, 1)
                        act.wait_ge(uTf_done_v, 2 * n + b // 2 + 1)
                    else:
                        act.wait_ge(uTf_done_a, 2 * n + b // 2 + 1)
                    act.activation(uT_hi[:, 2 * b:2 * b + 2], uTf[:, 2 * b:2 * b + 2], ACT.Copy).then_inc(uT_hi_done, 1)
                for h, g in enumerate((HT, GU[1])):
                    act.wait_ge(gate_psum, 2 * n + h + 1)
                    act.activation(gate_bc[:, h * 512:(h + 1) * 512], g[:, :], ACT.Copy).then_inc(gate_ready, 1)

            def silu(u, f):
                act.wait_ge(gu0_done, f + 1)
                act.activation(act_g[:, 0], GU[0][:, 0:F_UNIT], ACT.Silu).then_inc(silu_done, 1)
                act.wait_ge(used[1], u + 2)
                act.activation(act_g[:, 1], GU[1][:, 0:F_UNIT], ACT.Silu).then_inc(silu_done, 1)

            def h_split(f):
                act.wait_ge(hT_psum, f + 1)
                act.activation(hT_hi[:, :, :], HT[:, :].rearrange("p (f s) -> p f s", f=2), ACT.Copy).then_inc(hT_hi_done, 1)

            def ffn(u0, f0, n):
                split(u0 + 1, (0,), LAST_BEHIND)
                silu(u0, f0)
                split(u0 + 1, (1,), LAST_BEHIND)
                split(u0, (2,), LAST_BEHIND)
                with act.Fori(1, n - 1) as i:
                    h_split(f0 + i - 1)
                    split(u0 + i + 1, (0,), LAST_BEHIND)
                    silu(u0 + i, f0 + i)
                    split(u0 + i + 1, (1,), LAST_BEHIND)
                    split(u0 + i, (2,), LAST_BEHIND)
                h_split(f0 + n - 2)
                split(u0 + n, (0,), LAST_BEHIND)
                split(u0 + n - 1, (2,), LAST_UNIT)
                silu(u0 + n - 1, f0 + n - 1)
                h_split(f0 + n - 1)
                split(u0 + n, (1,))
                sqrt_ahead(1)

            def merge(u0, m):
                split(u0, (2,))
                split(u0 + 1, (0, 1))
                for t in range(T):
                    for b in range(2):
                        act.wait_ge(yT_psum, 4 * m + 2 * t + b + 1)
                        act.activation(yT_hi[:, 4 * b:4 * b + 4, t * P:(t + 1) * P], YT[t][b][:, :].rearrange("p (k s) -> p k s", k=4),
                                       ACT.Copy).then_inc(yT_hi_done, 1)
                    if t == 0:
                        split(u0 + 1, (2,))
                        split(u0 + 2, (0,))
                split(u0 + 2, (1, 2))
                sqrt_ahead(2)

            def job_exp(j0, jobs, j):
                kind, qt, g = jobs[j]
                nk = (qt + 1) * P
                sc = scores[j % 2]
                act.wait_ge(nmax_done, j0 + j + 1)
                for h in range(4):
                    v = sc[:, h // 2, h % 2, 0:nk]
                    e = act.activation(v, v, ACT.Exp, bias=nmax[j % 2][:, h:h + 1], accum_out=psum_row[j % 4][:, h:h + 1])
                e.then_inc(exp_done, 1)

            def jobs_run(j0, jobs, beside=lambda j: None):
                job_exp(j0, jobs, 0)
                for j, (kind, qt, g) in enumerate(jobs):
                    beside(j)
                    act.wait_ge(pt_psum, j0 + j + 1)
                    if j >= 2:
                        act.wait_ge(pv_done, j0 + j - 1)
                    act.activation(pT[j % 2][:, 0], bank[4][:, :].rearrange("p (h q) -> p h q", h=4), ACT.Copy).then_inc(pt_copied_a, 1)
                    if j + 1 < len(jobs):
                        job_exp(j0, jobs, j + 1)

            act.wait_ge(vec_landed, 16)
            act.activation(c_act[:, :], vec[:, V_C:V_C + 16], ACT.Silu).then_inc(c_ready, 1)
            for b in range(ADA_STEPS // 2):
                act.wait_ge(first_psum, b + 1)
                act.activation(first_row[:, b * 512:(b + 1) * 512], bank[b][0:1, :], ACT.Copy).then_inc(first_copied, 1)
                if b in (2, 3):
                    j = b - 2
                    act.wait_ge(landed[j], 16)
                    act.activation(w_hi[:, j * BLK:(j + 1) * BLK], raw[:, j * BLK:(j + 1) * BLK], ACT.Copy).then_inc(hi_done, 1)
            act.wait_ge(cst_landed, 16)

            with act.Fori(0, DEPTH) as l:
                u_mix = l * LAYER_UNITS + FFN_UNITS
                sqrt_ahead(0)
                norm(l * 3, l * 3)
                act.dma_start(lvec[:, :], layer_vecs[l]).then_inc(lvec_landed, 16)
                act.dma_start(cmpw[:, :, 0:CMP_STRIDE * DH], cmp_w1[l]).then_inc(lvec_landed, 16)
                ffn(l * LAYER_UNITS, l * 2 * FFN_UNITS, FFN_UNITS)

                norm(l * 3 + 1, l * 3 + 1)
                split(u_mix, (2,))
                split(u_mix + 1, (0, 1))
                act.wait_ge(w_done, l * 7 + 1)
                act.activation(proj[:, 0, 0:512], bank[0][:, :], ACT.Copy).then_inc(w_evac_a, 1)
                act.activation(proj[:, :, 512:768], bank[2][:, :].rearrange("p (t c) -> p t c", t=T), ACT.Copy).then_inc(w_evac_a, 1)
                split(u_mix + 1, (2,))
                act.wait_ge(w_evac_a, l * 9 + 2)
                act.wait_ge(w_evac_v, l * 3 + 1)
                for t in range(T):
                    act.activation(lat_squares[:, t, 0:Q_RANK], proj[:, t, C_CQ:C_CKV], ACT.Square, accum_out=lss[:, t:t + 1]).then_inc(lat_ss, 1)
                    act.activation(lat_squares[:, t, Q_RANK:], proj[:, t, C_CKV:C_KR], ACT.Square, accum_out=lss[:, 2 + t:3 + t]).then_inc(lat_ss, 1)
                act.wait_ge(lat_ms, l + 1)
                act.activation(lsq, lms, ACT.Sqrt).then_inc(lat_sq, 1)
                act.activation(nsa_gate.rearrange("p t h k -> p t (h k)"), proj[:, :, C_GN:C_KC], ACT.Sigmoid).then_inc(nsa_gate_ready, 1)
                split(u_mix + 2, (0, 1))
                act.wait_ge(w_done, l * 7 + 2)
                act.activation(proj[:, 0, 768:1280], bank[3][:, :], ACT.Copy).then_inc(w_evac_a, 1)
                act.activation(proj[:, :, 1280:1536], bank[5][:, :].rearrange("p (t c) -> p t c", t=T), ACT.Copy).then_inc(w_evac_a, 1)
                split(u_mix + 2, (2,))
                act.wait_ge(w_done, l * 7 + 3)
                act.activation(proj[:, 0, 1536:PROJ], bank[0][:, 0:184], ACT.Copy)
                act.activation(vsw[:, 0], bank[0][:, 184:440], ACT.Copy).then_inc(w_evac_a, 1)
                split(u_mix + 3, (0,))
                act.wait_ge(lvec_landed, l * 32 + 32)
                for b, cs in enumerate(((0, 1), (2, 3), (4,))):
                    act.wait_ge(cqT_psum, l * 3 + b + 1)
                    for i, c in enumerate(cs):
                        e = act.activation(cqT_hi[:, c], bank[2 + b][:, i * S:(i + 1) * S], ACT.Copy,
                                           scale=lvec[:, L_QN + c:L_QN + c + 1])
                    e.then_inc(cqT_hi_done, 1)
                for b in range(2):
                    act.wait_ge(q_psum, l * 2 + b + 1)
                    act.activation(qT[:, 2 * b:2 * b + 2], bank[5 + b][:, :].rearrange("p (c s) -> p c s", c=2), ACT.Copy,
                                   scale=DH ** -0.5).then_inc(q_ready, 1)
                act.wait_ge(ks_psum, l + 1)
                act.activation(kT[0][:, :, :], bank[0][:, :].rearrange("p (g s) -> p g s", g=2), ACT.Copy).then_inc(ks_ready, 1)
                act.wait_ge(hidc_psum, l + 1)
                act.activation(hid_cmp[:, :, :, 0:N_CMP], bank[4][:, 0:64].rearrange("p (k g n) -> p k g n", k=2, g=GROUPS)[:, :, :, 0:N_CMP],
                               ACT.Gelu_apprx_tanh).then_inc(hidc_ready, 1)
                act.wait_ge(cs_ready, l + 1)
                act.activation(p_cmp[:, :, 0:N_CMP], p_cmp[:, :, 0:N_CMP], ACT.Exp).then_inc(cp_exp, 1)
                for b in range(4):
                    act.wait_ge(uq_psum, l * 4 + b + 1)
                    act.activation(q_tok[:, b // 2, 4 * (b % 2):4 * (b % 2) + 4].rearrange("p h c -> p (h c)"), bank[b][:, 0:384],
                                   ACT.Copy).then_inc(uq_copied, 1)
                act.wait_ge(cp_psum, l + 1)
                act.activation(pT_cmp[:, :, :], bank[6][:, :].rearrange("p (a q) -> p a q", a=4), ACT.Copy).then_inc(cp_ready, 1)
                split(u_mix + 3, (1, 2))
                for b in range(4):
                    act.wait_ge(qm_psum, l * 4 + b + 1)
                    act.activation(qkT_m[0:QK, 0, 2 * b:2 * b + 2], bank[b][0:QK, :].rearrange("p (h s) -> p h s", h=2),
                                   ACT.Copy).then_inc(qm_ready, 1)

                def beside(j):
                    if j in JOB_SPLITS:
                        m, b = JOB_SPLITS[j]
                        split(u_mix + m, (b,))
                    if j % 3 == 2:
                        act.wait_ge(w_done, l * 7 + 4 + j // 3)
                        if j // 3 == 2:
                            act.wait_ge(pv_done, l * NJ + len(NSA_JOBS))
                        for t in range(T):
                            e = act.activation(gates_m[j // 3][:, t], bank[2 + t][:, :], ACT.Sigmoid)
                        e.then_inc(w_evac_a, 1)

                jobs_run(l * NJ, JOBS, beside)
                for b in range(4):
                    act.wait_ge(oT_psum, l * 4 + b + 1)
                    act.activation(oT_hi[b // 2][:, 2 * (b % 2):2 * (b % 2) + 2], bank[3 + b][:, :].rearrange("p (c s) -> p c s", c=2),
                                   ACT.Copy).then_inc(oT_hi_done, 1)
                merge(u_mix + MIX_IN_UNITS, l)

                norm(l * 3 + 2, l * 3 + 2, late=u_mix + MIX_IN_UNITS + MERGE_UNITS)
                ffn(l * LAYER_UNITS + FFN_UNITS + MIX_IN_UNITS + MERGE_UNITS, l * 2 * FFN_UNITS + FFN_UNITS, FFN_UNITS)

            q6, n6 = 3 * DEPTH, 3 * DEPTH
            act.wait_ge(x_ready, 2 * q6 + 1)
            act.dma_start(fn_bc, fnorm).then_inc(fn_landed, 16)
            rms_squares(q6)
            norm(q6 + 1, n6)
            u = HYB_U0
            split(u, (2,))
            for m in range(HYB_IN_UNITS):
                if m + 1 < HYB_IN_UNITS:
                    split(u + m + 1, (0, 1))
                act.wait_ge(w_done, DEPTH * 7 + m + 1)
                b0, n2 = 3 * (m % 2), 256 if m < 6 else 8
                if m < 4:
                    dst, c0 = (xcb, 768 * m) if m < 2 else (qkv, 768 * (m - 2))
                    act.activation(dst[:, 0, c0:c0 + 512], bank[b0][:, :], ACT.Copy).then_inc(w_evac_a, 1)
                    act.activation(dst[:, :, c0 + 512:c0 + 768], bank[b0 + 2][:, :].rearrange("p (t c) -> p t c", t=T),
                                   ACT.Copy).then_inc(w_evac_a, 1)
                elif m == 4:
                    for t in range(T):
                        act.activation(f_row[:, t], bank[b0 + t][:, 0:8], ACT.Copy)
                        act.activation(gates_h[:, t, 0:504], bank[b0 + t][:, 8:512], ACT.Sigmoid)
                    act.activation(gates_h[:, :, 504:760], bank[b0 + 2][:, :].rearrange("p (t c) -> p t c", t=T),
                                   ACT.Sigmoid).then_inc(w_evac_a, 1)
                else:
                    c0 = 760 + 768 * (m - 5)
                    for t in range(T):
                        act.activation(gates_h[:, t, c0:c0 + 512], bank[b0 + t][:, :], ACT.Sigmoid)
                    act.activation(gates_h[:, :, c0 + 512:c0 + 512 + n2],
                                   bank[b0 + 2][:, 0:2 * n2].rearrange("p (t c) -> p t c", t=T), ACT.Sigmoid).then_inc(w_evac_a, 1)
                if m + 1 < HYB_IN_UNITS:
                    split(u + m + 1, (2,))
            act.wait_ge(qkn_ms, 1)
            act.activation(qk_ss, qk_ss, ACT.Sqrt).then_inc(qkn_sq, 1)
            act.wait_ge(f_exp_in, 1)
            act.activation(f_e[:, :, :], f_e[:, :, :], ACT.Exp).then_inc(f_exp, 1)
            act.wait_ge(f_ln_in, 1)
            act.activation(f_l[:, :, :], f_l[:, :, :], ACT.Ln).then_inc(f_ln, 1)
            for b in range(2):
                act.wait_ge(ya_f32, b + 1)
                act.activation(oT_hi[0][:, 2 * b:2 * b + 2], conv[:, 2 * b:2 * b + 2], ACT.Copy).then_inc(ya_hi_done, 1)
            for b in range(2):
                act.wait_ge(q_psum, DEPTH * 2 + b + 1)
                act.activation(qT_h[:, 2 * b:2 * b + 2], bank[b][:, :].rearrange("p (c s) -> p c s", c=2), ACT.Copy,
                               scale=qk_gain[:, 0:1]).then_inc(q_ready, 1)
            for b in range(2):
                act.wait_ge(kh_psum, b + 1)
                act.activation(kT_h[:, 2 * b:2 * b + 2], bank[2 + 2 * b][:, :].rearrange("p (c s) -> p c s", c=2), ACT.Copy,
                               scale=vec[:, V_KN:V_KN + 1]).then_inc(kh_ready, 1)
            jobs_run(DEPTH * NJ, HYB_JOBS)
            um = u + HYB_IN_UNITS
            split(um, (0, 1))
            for b in range(2):
                act.wait_ge(oT_psum, DEPTH * 4 + b + 1)
                act.activation(oT_hi[1][:, 2 * b:2 * b + 2], bank[5 + b][:, :].rearrange("p (c s) -> p c s", c=2),
                               ACT.Copy).then_inc(oT_hi_done, 1)
            merge(um, DEPTH)
            norm(q6 + 2, n6 + 1)
            expert_split(0, 0, (0, 1), IN_LINE)
            act.wait_ge(r_exp_in, 1)
            act.activation(g_exp[:, :, :], g_exp[:, :, :], ACT.Exp)
            act.activation(e_exp[:, :, :], e_exp[:, :, :], ACT.Exp).then_inc(r_exp, 1)

            def gathered(n, i):
                act.wait_ge(us_psum, 2 * n + 1)
                for k in range(4):
                    e = act.activation(usf[i][:, k], bank[GATHER_BANKS[i][0]][:, k * P:(k + 1) * P], ACT.Identity,
                                       scale=modf[:, 8 + k:9 + k], bias=modf[:, k:k + 1])
                e.then_inc(usf_done_a, 1)

            def gathered_hi(n, i):
                act.wait_ge(usf_done_a, n + 1)
                act.activation(us_hi[i][:, 0:4], usf[i][:, 0:4], ACT.Copy).then_inc(us_hi_done, 1)
                act.wait_ge(usf_done_v, n + 1)
                act.activation(us_hi[i][:, 4:8], usf[i][:, 4:8], ACT.Copy).then_inc(us_hi_done, 1)

            def picks_out(n, tiles):
                act.wait_ge(pick_T_psum, n + 1)
                for i in range(0, tiles, 2):
                    w = min(tiles - i, 2)
                    e = act.activation(pick_T[:, i:i + w], bank[6 + i // 2][:, 0:w * S].rearrange("p (i s) -> p i s", i=w), ACT.Copy)
                e.then_inc(pick_T_ready, 1)
                act.wait_ge(sw_psum, n + 1)
                act.activation(sparse_w[:, 0:tiles], GU[1][:, 64:64 + tiles * PER_GROUP].rearrange("p (i e) -> p i e", i=tiles),
                               ACT.Copy).then_inc(sw_ready, 1)

            def sparse_h_split(f):
                act.wait_ge(hT_psum, f + 1)
                act.activation(hTs_hi, HT[:, 0:S].rearrange("p (c s) -> p c s", c=2), ACT.Copy).then_inc(hT_hi_done, 1)

            def sparse_unit(half, odd, first=False, last=False):
                if not first:
                    sparse_h_split(half * 2 + (MOE_F0 + odd - 1))
                if not last:
                    expert_split(*after(half, odd), (0,))
                act.wait_ge(used[1], half * 2 + (MOE_U0 + odd + 2))
                act.activation(act_g[:, 0], GU[0][:, 0:F_UNIT], ACT.Silu).then_inc(silu_done, 2)
                if not last:
                    expert_split(*after(half, odd), (1,))
                expert_split(half, odd, (2,), IN_LINE if last else LAST_BEHIND)

            def sparse_out(n):
                act.wait_ge(ys_psum, n + 1)
                for h in range(2):
                    e = act.activation(y_s[n][:, h * 512:(h + 1) * 512], ACC[h][:, :], ACT.Copy)
                e.then_inc(ys_ready, 1)

            def expert_group(n, beside, first=False, last=False):
                half, halves = n * PER_GROUP // 2, PER_GROUP // 2
                sparse_unit(half, 0, first=first)
                if not first:
                    sparse_out(n - 1)
                beside()
                with act.Fori(0, halves - 1) as i:
                    sparse_unit(i + half, 1)
                    sparse_unit(i + (half + 1), 0)
                sparse_unit(half + halves - 1, 1, last=last)
                if last:
                    sparse_h_split(MOE_F0 + (n + 1) * PER_GROUP - 1)
                    sparse_out(n)

            def later_tiles():
                gathered(2, 2)
                gathered(3, 3)
                gathered_hi(1, 1)
                gathered_hi(2, 2)

            gathered(0, 0)
            gathered_hi(0, 0)
            picks_out(0, EXPERT_GROUPS)
            gathered(1, 1)
            beside = [later_tiles, lambda: gathered_hi(3, 3), lambda: None, lambda: None]
            for n in range(EXPERT_GROUPS):
                expert_group(n, beside[n], n == 0, n == EXPERT_GROUPS - 1)
            act.wait_ge(further_ready, 1)
            with act.If(act.value_load(further[0:1, 1:2], min_val=0, max_val=1) > 0):
                expert_split(EXPERTS // 2, 0, (0, 1), IN_LINE)
                gathered(EXPERT_GROUPS, 0)
                gathered_hi(EXPERT_GROUPS, 0)
                picks_out(1, 1)
                expert_group(EXPERT_GROUPS, lambda: None, True, True)

        @block.vector
        def _(dve):
            V = nc.vector
            links = [0, 0]

            def link(ins, layer=None):
                links[0] += 1
                ins.then_inc(chain, 1)
                dve.wait_ge(chain, links[1] + links[0])

            def split(u, js, order=IN_LINE):
                for j in js:
                    b, r = slice(j * BLK, (j + 1) * BLK), (order[j] + 3) % 3
                    dve.wait_ge(hi_done, u * 3 + order[j] + 1)
                    V.tensor_tensor(w_lo[:, b], raw[:, r * BLK:(r + 1) * BLK], f32(w_hi[:, b]), ALU.subtract).then_inc(split_done, 1)

            def expert_split(half, odd, js, order=LAST_BEHIND):
                for j in js:
                    b, place = slice(j * BLK, (j + 1) * BLK), expert_place(half, odd, j, order)[0]
                    dve.wait_ge(hi_done, (half * 2 + (MOE_U0 + odd)) * 3 + (order[j] + 1))
                    V.tensor_tensor(w_lo[:, b], place, f32(w_hi[:, b]), ALU.subtract).then_inc(split_done, 1)

            def rms(q, t):
                c = slice(t, t + 1)
                dve.wait_ge(ss_done, 2 * q + t + 1)
                V.tensor_scalar(ms[:, c], ss[:, c], 1.0 / D, EPS, ALU.mult, ALU.add).then_inc(ms_done, 1)
                dve.wait_ge(sq_done, 2 * q + t + 1)
                V.reciprocal(rstd[:, c], sq[:, c]).then_inc(rstd_done, 1)
                dve.wait_ge(rstd_done, 2 * q + t + 1)

            def modulation(n, gain=None, half=1.0):
                dve.wait_ge(mod_step, n * ADA_STEPS + ADA_STEPS + 1)
                link(V.tensor_tensor(modf[:, :], MOD[:, 0:24], vec[:, bass.ds(V_BADA + n * 24, 24)], ALU.add))
                e = V.tensor_scalar(modf[:, 8:16], modf[:, 8:16], 1.0, None, ALU.add)
                if gain is not None:
                    link(e)
                    e = V.tensor_tensor(modf[:, 8:16], modf[:, 8:16], gain, ALU.mult)
                e.then_inc(mod_ready, 1)
                for k in range(KD):
                    d = V.tensor_scalar(diag[:, k], ident, modf[:, 16 + k:17 + k], half, ALU.mult, ALU.mult)
                d.then_inc(diag_done, 1)
                dve.wait_ge(mod_ready, n + 1)

            def norm_tile(q, t):
                rms(q, t)
                V.tensor_scalar(xn[:, t], x[:, t], rstd[:, t:t + 1], None, ALU.mult).then_inc(xn_done, 1)

            def norm(q, n, tiles=range(T), late=None):
                for t in tiles:
                    norm_tile(q, t)
                for b in (0, 2):
                    dve.wait_ge(uT_psum, 4 * n + b + 1)
                    for k in (2 * b, 2 * b + 1):
                        e = V.tensor_scalar(uTf[:, k], ACC[b][:, (k % 2) * S:(k % 2) * S + S], modf[:, 8 + k:9 + k], modf[:, k:k + 1],
                                            ALU.mult, ALU.add)
                    e.then_inc(uTf_done_v, 1)
                for b in range(4):
                    dve.wait_ge(uT_hi_done, 4 * n + b + 1)
                    V.tensor_tensor(uT_lo[:, 2 * b:2 * b + 2], uTf[:, 2 * b:2 * b + 2], f32(uT_hi[:, 2 * b:2 * b + 2]),
                                    ALU.subtract).then_inc(uT_ready, 1)
                if late is not None:
                    split(late, (1,))

            def hidden(f):
                for t in range(T):
                    dve.wait_ge(silu_done, f * 2 + t + 1)
                    V.tensor_tensor(hid[:, t], act_g[:, t], GU[t][:, F_UNIT:2 * F_UNIT], ALU.mult).then_inc(h_done, 1)

            def h_split(f):
                dve.wait_ge(hT_hi_done, f + 1)
                V.tensor_tensor(hT_lo[:, :, :], HT[:, :].rearrange("p (f s) -> p f s", f=2), f32(hT_hi[:, :, :]),
                                ALU.subtract).then_inc(hT_ready, 1)

            def x_update(n, done, banks=ACC, between=lambda: None):
                for t in range(T):
                    if t == 0:
                        dve.wait_ge(first_tile, n + 1)
                    else:
                        between()
                        dve.wait_ge(*done)
                    for h in range(2):
                        m = V.tensor_tensor(upd[:, t, h], banks[2 * t + h][:, :], gate_bc[:, h * 512:(h + 1) * 512], ALU.mult)
                    link(m)
                    xt = x[:, t].rearrange("p (h c) -> p h c", h=2)
                    V.tensor_tensor(xt, xt, upd[:, t], ALU.add).then_inc(x_ready, 1)

            def ffn(u0, f0, n, stage, following, between):
                split(u0 + 1, (0,), LAST_BEHIND)
                hidden(f0)
                split(u0 + 1, (1,), LAST_BEHIND)
                split(u0, (2,), LAST_BEHIND)
                with dve.Fori(1, n - 1) as i:
                    h_split(f0 + i - 1)
                    split(u0 + i + 1, (0,), LAST_BEHIND)
                    hidden(f0 + i)
                    split(u0 + i + 1, (1,), LAST_BEHIND)
                    split(u0 + i, (2,), LAST_BEHIND)
                h_split(f0 + n - 2)
                split(u0 + n, (0,), LAST_BEHIND)
                following()
                split(u0 + n - 1, (2,), LAST_UNIT)
                hidden(f0 + n - 1)
                h_split(f0 + n - 1)
                split(u0 + n, (1,))
                x_update(stage, (used[2], u0 + n + 1), between=between)

            def merge(u0, m, stage, gates, following, between, more=True):
                split(u0, (2,))
                for t in range(T):
                    dve.wait_ge(pa_psum, 2 * m + t + 1)
                    for h in range(2):
                        e = V.tensor_tensor(y[:, t, h * 512:(h + 1) * 512], gates[h][:, t], ACC[2 * t + h][:, :], ALU.mult)
                    e.then_inc(ya_done, 1)
                    split(u0 + 1, (t,))
                for t in range(T):
                    dve.wait_ge(pb_psum, 2 * m + t + 1)
                    for h in range(2):
                        e = V.tensor_tensor(ytmp[:, t, h], gates[2 + h][:, t], ACC[2 * t + h][:, :], ALU.mult)
                    link(e)
                    yt = y[:, t].rearrange("p (h c) -> p h c", h=2)
                    V.tensor_tensor(yt, yt, ytmp[:, t], ALU.add).then_inc(y_ready, 1)
                    if t == 1:
                        split(u0 + 2, (0,))
                    for b in range(2):
                        dve.wait_ge(yT_hi_done, 4 * m + 2 * t + b + 1)
                        V.tensor_tensor(yT_lo[:, 4 * b:4 * b + 4, t * P:(t + 1) * P], YT[t][b][:, :].rearrange("p (k s) -> p k s", k=4),
                                        f32(yT_hi[:, 4 * b:4 * b + 4, t * P:(t + 1) * P]), ALU.subtract).then_inc(yT_ready, 1)
                    if t == 0:
                        split(u0 + 1, (2,))
                split(u0 + 2, (1,))
                following()
                split(u0 + 2, (2,))

                x_update(stage, (used[1], u0 + 4), between=between)
                if more:
                    split(u0 + 3, (0,))

            def job_bias(j0, jobs, j):
                kind, qt, g = jobs[j]
                nk = (qt + 1) * P
                sc, sp = scores[j % 2], bank[0:2]
                dve.wait_ge(sc_done, j0 + j + 1)
                for p in range(2):
                    ps = sp[p][:, :].rearrange("p (i s) -> p i s", i=2)
                    if kind == 2:
                        e = V.scalar_tensor_tensor(sc[:, p, :, 0:nk], ps[:, :, 0:nk], QK ** -0.5,
                                                   mask[qt].unsqueeze(1).to_broadcast([P, 2, nk]), ALU.mult, ALU.add)
                        continue
                    for i in range(2):
                        h = 4 * g + 2 * i + p
                        if kind == 3:
                            e = V.scalar_tensor_tensor(sc[:, p, i, 0:nk], ps[:, i, 0:nk], f_cum[:, qt, h:h + 1], mask[qt], ALU.add, ALU.add)
                        else:
                            e = V.scalar_tensor_tensor(sc[:, p, i, 0:nk], dist[qt], SLOPES[h], ps[:, i, 0:nk], ALU.mult, ALU.add)
                e.then_inc(bias_done, 1)
                dve.wait_ge(bias_done, j0 + j + 1)
                V.tensor_reduce(nmax[j % 2].rearrange("p (a i) -> p a i", a=2), sc[:, :, :, 0:nk], AX.X, ALU.max,
                                negate=True).then_inc(nmax_done, 1)

            def job_out(j0, jobs, j):
                kind, qt, g = jobs[j]
                dve.wait_ge(pv_done, j0 + j + 1)
                o_ps = HT[:, 0:4 * DH].rearrange("p (a i d) -> p a i d", a=2, i=2)
                link(V.reciprocal(rsum, psum_row[j % 4]))
                r = rsum.rearrange("p (a i) -> p a i", a=2)
                if kind < 2:
                    gate = nsa_gate[:, qt, 4 * g:4 * g + 4, 1 + kind].rearrange("p (i a) -> p a i", a=2)
                    link(V.tensor_tensor(coef.rearrange("p (a i) -> p a i", a=2), r, gate, ALU.mult))
                    r = coef.rearrange("p (a i) -> p a i", a=2)
                dst = o_h if kind == 3 else o_a if kind < 2 else o_b
                ov = dst[:, qt, 256 * g:256 * g + 256].rearrange("p (i a d) -> p a i d", i=2, a=2)
                if kind >= 2:
                    for a in range(2):
                        e = V.tensor_tensor(ov[:, a], o_ps[:, a], r[:, a].unsqueeze(2).to_broadcast([P, 2, DH]), ALU.mult)
                    e.then_inc(o_done, 1)
                else:
                    tv = o_tmp.rearrange("p (a i) d -> p a i d", a=2)
                    for a in range(2):
                        e = V.tensor_tensor(tv[:, a], o_ps[:, a], r[:, a].unsqueeze(2).to_broadcast([P, 2, DH]), ALU.mult)
                    e.then_inc(o_done, 1)
                    dve.wait_ge(o_done, j0 + j + 1)
                    for a in range(2):
                        e = V.tensor_tensor(ov[:, a], ov[:, a], tv[:, a], ALU.add)
                    link(e)

            def jobs_run(j0, jobs, beside=lambda j: None):
                job_bias(j0, jobs, 0)
                for j, (kind, qt, g) in enumerate(jobs):
                    if j + 1 < len(jobs):
                        job_bias(j0, jobs, j + 1)
                    beside(j)
                    if qt:
                        dve.wait_ge(pt_psum, j0 + j + 1)
                        V.tensor_copy(pT[j % 2][:, 1], bank[5][:, :].rearrange("p (h q) -> p h q", h=4)).then_inc(pt_copied_v, 1)
                    if j:
                        job_out(j0, jobs, j - 1)
                job_out(j0, jobs, len(jobs) - 1)

            V.memset(zeros[:, :], 0.0).then_inc(first_ready, 1)
            for j in range(2):
                b = slice(j * BLK, (j + 1) * BLK)
                dve.wait_ge(hi_done, j + 1)
                V.tensor_tensor(w_lo[:, b], raw[:, b], f32(w_hi[:, b]), ALU.subtract).then_inc(split_done, 1)
            dve.wait_ge(x_landed, 16)
            dve.wait_ge(cst_landed, 16)
            dve.wait_ge(vec_landed, 16)
            V.memset(stat[:, 0:2], 0.0).then_inc(x_ready, 2)

            norm_tile(0, 0)
            modulation(0, half=0.5)
            links_before = links[0]

            with dve.Fori(0, DEPTH) as l:
                links[:] = [0, l * CHAIN_PER_LAYER + links_before]
                u_mix = l * LAYER_UNITS + FFN_UNITS
                norm(l * 3, l * 3, (1,))
                ffn(l * LAYER_UNITS, l * 2 * FFN_UNITS, FFN_UNITS, l * 3, lambda: modulation(l * 3 + 1),
                    lambda: None)

                norm(l * 3 + 1, l * 3 + 1)
                split(u_mix, (2,))
                split(u_mix + 1, (0, 1))
                dve.wait_ge(w_done, l * 7 + 1)
                V.tensor_copy(proj[:, 1, 0:512], bank[1][:, :]).then_inc(w_evac_v, 1)
                split(u_mix + 1, (2,))
                dve.wait_ge(lat_ss, l * 4 + 4)
                V.tensor_scalar(lms[:, 0:2], lss[:, 0:2], 1.0 / Q_RANK, EPS, ALU.mult, ALU.add)
                V.tensor_scalar(lms[:, 2:4], lss[:, 2:4], 1.0 / KV_RANK, EPS, ALU.mult, ALU.add).then_inc(lat_ms, 1)
                dve.wait_ge(lat_sq, l + 1)
                link(V.reciprocal(lrs, lsq))
                for t in range(T):
                    V.tensor_scalar(proj[:, t, C_CQ:C_CKV], proj[:, t, C_CQ:C_CKV], lrs[:, t:t + 1], None, ALU.mult)
                    e = V.tensor_scalar(proj[:, t, C_CKV:C_KR], proj[:, t, C_CKV:C_KR], lrs[:, 2 + t:3 + t], None, ALU.mult)
                e.then_inc(lat_ready, 1)
                kr = proj[:, :, C_KR:C_GN]
                V.tensor_tensor(kr_a[:, :, :], kr, cos2, ALU.mult)
                link(V.tensor_tensor(kr_b[:, :, :], kr, sin2, ALU.mult))
                split(u_mix + 2, (0, 1))
                dve.wait_ge(w_done, l * 7 + 2)
                V.tensor_copy(proj[:, 1, 768:1280], bank[4][:, :]).then_inc(w_evac_v, 1)
                split(u_mix + 2, (2,))
                dve.wait_ge(w_done, l * 7 + 3)
                V.tensor_copy(proj[:, 1, 1536:PROJ], bank[1][:, 0:184])
                V.tensor_copy(vsw[:, 1], bank[1][:, 184:440]).then_inc(w_evac_v, 1)
                split(u_mix + 3, (0,))
                dve.wait_ge(lvec_landed, l * 32 + 32)
                for b, cs in enumerate(((0, 1), (2, 3), (4,))):
                    dve.wait_ge(cqT_hi_done, l * 3 + b + 1)
                    for i, c in enumerate(cs):
                        e = V.scalar_tensor_tensor(cqT_lo[:, c], bank[2 + b][:, i * S:(i + 1) * S], lvec[:, L_QN + c:L_QN + c + 1],
                                                   f32(cqT_hi[:, c]), ALU.mult, ALU.subtract)
                    e.then_inc(cqT_ready, 1)
                dve.wait_ge(kw_psum, l + 1)
                V.tensor_copy(kT[1][:, :, :], bank[1][:, :].rearrange("p (g s) -> p g s", g=2)).then_inc(kw_ready, 1)
                dve.wait_ge(c_psum, l + 1)
                for k in range(2):
                    both = bank[2 + k][:, :].rearrange("p (g s) -> p g s", g=GROUPS)
                    V.tensor_copy(cT[0:DH, 2 * k:2 * k + 2], both[0:DH])
                    e = V.tensor_copy(cT[DH:P, 2 * k:2 * k + 2, 0:S - CMP_STRIDE], both[DH:P, :, CMP_STRIDE:S])
                link(e)
                for k in range(2):
                    place_k = lvec[:, L_PE + CMP_STRIDE * k:L_PE + CMP_STRIDE * (k + 1)].unsqueeze(2).to_broadcast([P, CMP_STRIDE, N_CMP])
                    for g in range(GROUPS):
                        tok = cT[:, 2 * k + g].rearrange("p (n j) -> p j n", j=CMP_STRIDE)
                        e = V.tensor_tensor(blocks[:, 2 * k + g], tok[:, :, 0:N_CMP], place_k, ALU.add)
                e.then_inc(blocks_ready, 1)
                dve.wait_ge(kvc_psum, l + 1)
                for g in range(GROUPS):
                    V.tensor_copy(kT_cmp[:, g, 0:N_CMP], bank[4 + g][:, 0:N_CMP])
                    for i in range(4):
                        e = V.tensor_copy(v_cmp[32 * i:32 * i + N_CMP, g], bank[4 + g][32 * i:32 * i + N_CMP, 64:128])
                e.then_inc(kvc_ready, 1)
                link(V.memset(p_cmp[:, :, :], 0.0))
                dve.wait_ge(cs_psum, l + 1)
                pc = p_cmp.rearrange("p (a q i) n -> p a q i n", a=2, q=2)
                for p in range(2):
                    for qt in range(2):
                        e = V.tensor_tensor(pc[:, p, qt, :, 0:N_CMP], bank[4 + p][:, 64 * qt:64 * qt + 64].rearrange("p (i n) -> p i n", i=4)[:, :, 0:N_CMP],
                                            cmp_bias[:, p, qt, :, 0:N_CMP], ALU.add)
                link(e)
                link(V.tensor_reduce(cmax, p_cmp[:, :, 0:N_CMP], AX.X, ALU.max))
                V.tensor_tensor(p_cmp[:, :, 0:N_CMP], p_cmp[:, :, 0:N_CMP], cmax.unsqueeze(2).to_broadcast([P, 16, N_CMP]),
                                ALU.subtract).then_inc(cs_ready, 1)
                H2 = ROPE // 2
                bc = [P, HEADS, H2]
                for t in range(T):
                    V.tensor_tensor(k_tok[:, t, :, NOPE:NOPE + H2], kr_a[:, t, 0:H2].unsqueeze(1).to_broadcast(bc),
                                    kr_b[:, t, H2:ROPE].unsqueeze(1).to_broadcast(bc), ALU.subtract)
                    V.tensor_tensor(k_tok[:, t, :, NOPE + H2:QK], kr_b[:, t, 0:H2].unsqueeze(1).to_broadcast(bc),
                                    kr_a[:, t, H2:ROPE].unsqueeze(1).to_broadcast(bc), ALU.add)
                dve.wait_ge(cp_exp, l + 1)
                link(V.tensor_reduce(csum, p_cmp[:, :, 0:N_CMP], AX.X, ALU.add))
                link(V.reciprocal(crec, csum))
                dve.wait_ge(nsa_gate_ready, l + 1)
                for qt in range(2):
                    g0 = nsa_gate[:, qt, :, 0].rearrange("p (i a) -> p a i", a=2)
                    cc = ccoef.rearrange("p (a q i) -> p a q i", a=2, q=2)[:, :, qt]
                    cr = crec.rearrange("p (a q i) -> p a q i", a=2, q=2)[:, :, qt]
                    e = V.scalar_tensor_tensor(cc, cr, cmp_valid[:, qt:qt + 1], g0, ALU.mult, ALU.mult)
                link(e)
                dve.wait_ge(uq_copied, l * 4 + 4)
                qr = q_tok[:, :, :, NOPE:QK]
                for t in range(T):
                    V.tensor_tensor(rope_a[:, t], qr[:, t], cos2[:, t].unsqueeze(1).to_broadcast([P, HEADS, ROPE]), ALU.mult)
                    e = V.tensor_tensor(rope_b[:, t], qr[:, t], sin2[:, t].unsqueeze(1).to_broadcast([P, HEADS, ROPE]), ALU.mult)
                link(e)
                V.tensor_tensor(q_tok[:, :, :, NOPE:NOPE + H2], rope_a[:, :, :, 0:H2], rope_b[:, :, :, H2:ROPE], ALU.subtract)
                V.tensor_tensor(q_tok[:, :, :, NOPE + H2:QK], rope_b[:, :, :, 0:H2], rope_a[:, :, :, H2:ROPE], ALU.add).then_inc(rope_done, 1)
                for t in range(T):
                    dve.wait_ge(uk_psum, l * 2 + t + 1)
                    V.tensor_copy(k_tok[:, t, :, 0:NOPE], bank[4 + t][:, :].rearrange("p (h c) -> p h c", h=HEADS)).then_inc(uk_copied, 1)
                split(u_mix + 3, (1,))
                dve.wait_ge(co_psum, l + 1)
                dve.wait_ge(rope_done, l + 1)
                oav = o_a.rearrange("p t (i a d) -> p t i a d", i=4, a=2)
                for i in range(4):
                    for qt in range(2):
                        cc = ccoef.rearrange("p (a q i) -> p a q i", a=2, q=2)[:, :, qt, i]
                        e = V.tensor_tensor(oav[:, qt, i], bank[i][:, 128 * qt:128 * qt + 128].rearrange("p (a d) -> p a d", a=2),
                                            cc.unsqueeze(2).to_broadcast([P, 2, DH]), ALU.mult)
                e.then_inc(co_done, 1)
                dve.wait_ge(co_done, l + 1)
                for t in range(T):
                    dve.wait_ge(uv_psum, l * 2 + t + 1)
                    V.tensor_copy(vm[:, t], bank[6 - 2 * t][:, :]).then_inc(uv_ready, 1)
                split(u_mix + 3, (2,))
                for b in range(4):
                    dve.wait_ge(km_psum, l * 4 + b + 1)
                    V.tensor_copy(qkT_m[0:QK, 1, 2 * b:2 * b + 2], bank[K_BANKS[b]][0:QK, :].rearrange("p (h s) -> p h s", h=2)).then_inc(km_ready, 1)

                def beside(j):
                    if j in JOB_SPLITS:
                        m, b = JOB_SPLITS[j]
                        split(u_mix + m, (b,))

                jobs_run(l * NJ, JOBS, beside)
                for b in range(4):
                    dve.wait_ge(oT_hi_done, l * 4 + b + 1)
                    V.tensor_tensor(oT_lo[b // 2][:, 2 * (b % 2):2 * (b % 2) + 2], bank[3 + b][:, :].rearrange("p (c s) -> p c s", c=2),
                                    f32(oT_hi[b // 2][:, 2 * (b % 2):2 * (b % 2) + 2]), ALU.subtract).then_inc(oT_ready, 1)
                dve.wait_ge(w_evac_a, l * 9 + 9)
                merge(u_mix + MIX_IN_UNITS, l, l * 3 + 1, gates_m, lambda: modulation(l * 3 + 2, half=0.5), lambda: norm_tile(l * 3 + 2, 0))

                norm(l * 3 + 2, l * 3 + 2, (1,), late=u_mix + MIX_IN_UNITS + MERGE_UNITS)
                ffn(l * LAYER_UNITS + FFN_UNITS + MIX_IN_UNITS + MERGE_UNITS, l * 2 * FFN_UNITS + FFN_UNITS, FFN_UNITS,
                    l * 3 + 2, lambda: modulation(l * 3 + 3, gain=vec[:, bass.ds(V_GAIN + l * 8, 8)], half=vec[:, bass.ds(V_HALF + l, 1)]),
                    lambda: None)
                norm_tile(l * 3 + 3, 0)
                assert links[0] <= CHAIN_PER_LAYER
                if links[0] < CHAIN_PER_LAYER:
                    V.memset(pad, 0.0).then_inc(chain, CHAIN_PER_LAYER - links[0])

            links[:] = [0, DEPTH * CHAIN_PER_LAYER + links_before]
            q6, n6 = 3 * DEPTH, 3 * DEPTH
            dve.wait_ge(fn_landed, 16)
            for t in range(T):
                if t > 0:
                    norm_tile(q6, t)
                dve.wait_ge(xn_done, 2 * q6 + t + 1)
                V.tensor_tensor(x[:, t], xn[:, t], fn_bc, ALU.mult).then_inc(x_ready, 1)
            dve.wait_ge(x_ready, 2 * (q6 + 2))
            norm(q6 + 1, n6)
            u = HYB_U0
            split(u, (2,))
            for m in range(HYB_IN_UNITS):
                if m + 1 < HYB_IN_UNITS:
                    split(u + m + 1, (0, 1))
                if m < 4:
                    dve.wait_ge(w_done, DEPTH * 7 + m + 1)
                    dst, c0 = (xcb, 768 * m) if m < 2 else (qkv, 768 * (m - 2))
                    V.tensor_copy(dst[:, 1, c0:c0 + 512], bank[3 * (m % 2) + 1][:, :]).then_inc(w_evac_v, 1)
                if m + 1 < HYB_IN_UNITS:
                    split(u + m + 1, (2,))
            dve.wait_ge(w_evac_a, DEPTH * 9 + 4)
            dve.wait_ge(w_evac_v, DEPTH * 3 + 2)
            V.tensor_tensor(u_tok[:, :, :], xcb[:, :, 0:512], xcb[:, :, 512:1024], ALU.mult).then_inc(u_ready, 1)
            dve.wait_ge(w_evac_a, DEPTH * 9 + 8)
            dve.wait_ge(w_evac_v, DEPTH * 3 + 4)
            qk_s = qk_ss.rearrange("p (i t h) -> p i t h", i=2, t=T)
            for i in range(2):
                v = qkv[:, :, 512 * i:512 * i + 512]
                link(V.tensor_tensor(squares[:, :, :], v, v, ALU.mult))
                link(V.tensor_reduce(qk_s[:, i], squares.rearrange("p t (h d) -> p t h d", h=HEADS), AX.X, ALU.add))
            V.tensor_scalar(qk_gain[:, 0:1], vec[:, V_QN:V_QN + 1], DH ** -0.5, None, ALU.mult)
            V.tensor_scalar(qk_ss, qk_ss, 1.0 / DH, EPS, ALU.mult, ALU.add).then_inc(qkn_ms, 1)
            dve.wait_ge(w_evac_a, DEPTH * 9 + 9)
            bf = vec[:, V_BF:V_BF + 8].unsqueeze(1).to_broadcast([P, T, 8])
            link(V.tensor_tensor(f_row[:, :, :], f_row[:, :, :], bf, ALU.add))
            V.tensor_scalar(f_cum[:, :, :], f_row[:, :, :], 0.0, None, ALU.min)
            V.scalar_tensor_tensor(f_e[:, :, :], f_row[:, :, :], -1.0, f_row[:, :, :], ALU.mult, ALU.min).then_inc(f_exp_in, 1)
            dve.wait_ge(qkn_sq, 1)
            link(V.reciprocal(qk_ss, qk_ss))
            for i in range(2):
                for t in range(T):
                    v = qkv[:, t, 512 * i:512 * i + 512].rearrange("p (h d) -> p h d", h=HEADS)
                    e = V.tensor_tensor(v, v, qk_s[:, i, t].unsqueeze(2).to_broadcast([P, HEADS, DH]), ALU.mult)
            e.then_inc(qkn_ready, 1)
            dve.wait_ge(f_exp, 1)
            V.tensor_scalar(f_l[:, :, :], f_e[:, :, :], 1.0, None, ALU.add).then_inc(f_ln_in, 1)
            dve.wait_ge(f_ln, 1)
            V.tensor_tensor(nlogf[:, :, :], f_l[:, :, :], f_cum[:, :, :], ALU.subtract).then_inc(logf_ready, 1)
            dve.wait_ge(uc_psum, 2)
            dve.wait_ge(b_psum, 1)
            V.memset(uTc[:, :, 0:2], 0.0)
            for b in range(2):
                e = V.tensor_copy(uTc[:, 2 * b:2 * b + 2, 2:S + 2], bank[4 + b][:, :].rearrange("p (c s) -> p c s", c=2))
            e.then_inc(uc_ready, 1)
            dve.wait_ge(uc_ready, 1)
            for j in range(3):
                for c in range(4):
                    w = vec[:, V_CONV + 3 * c + j:V_CONV + 3 * c + j + 1]
                    if j == 0:
                        e = V.tensor_scalar(conv[:, c], uTc[:, c, 0:S], w, None, ALU.mult)
                    else:
                        e = V.scalar_tensor_tensor(conv[:, c], uTc[:, c, j:j + S], w, conv[:, c], ALU.mult, ALU.add)
                link(e)
            for b in range(2):
                V.tensor_tensor(conv[:, 2 * b:2 * b + 2], conv[:, 2 * b:2 * b + 2],
                                bank[6 - 3 * b][:, :].rearrange("p (c s) -> p c s", c=2), ALU.mult).then_inc(ya_f32, 1)
            for b in range(2):
                dve.wait_ge(ya_hi_done, b + 1)
                V.tensor_tensor(oT_lo[0][:, 2 * b:2 * b + 2], conv[:, 2 * b:2 * b + 2], f32(oT_hi[0][:, 2 * b:2 * b + 2]),
                                ALU.subtract).then_inc(oT_ready, 1)
            dve.wait_ge(fcum_psum, 1)
            V.tensor_scalar(f_cum[:, :, :], bank[5][:, 0:16].rearrange("p (t h) -> p t h", t=T), -1.0, None, ALU.mult).then_inc(fcum_ready, 1)
            dve.wait_ge(fcum_ready, 1)
            jobs_run(DEPTH * NJ, HYB_JOBS)
            um = u + HYB_IN_UNITS
            split(um, (0, 1))
            for b in range(2):
                dve.wait_ge(oT_hi_done, DEPTH * 4 + b + 1)
                V.tensor_tensor(oT_lo[1][:, 2 * b:2 * b + 2], bank[5 + b][:, :].rearrange("p (c s) -> p c s", c=2),
                                f32(oT_hi[1][:, 2 * b:2 * b + 2]), ALU.subtract).then_inc(oT_ready, 1)
            dve.wait_ge(w_evac_a, DEPTH * 9 + 11)
            merge(um, DEPTH, n6, gate_sets_h, lambda: modulation(n6 + 1, gain=vec[:, V_N2:V_N2 + 8]),
                  lambda: norm_tile(q6 + 2, 0), more=False)
            norm(q6 + 2, n6 + 1, (1,))
            def gathered(n, i):
                dve.wait_ge(us_psum, 2 * n + 2)
                for k in range(4, KD):
                    e = V.tensor_scalar(usf[i][:, k], bank[GATHER_BANKS[i][1]][:, (k - 4) * P:(k - 3) * P], modf[:, 8 + k:9 + k], modf[:, k:k + 1],
                                        ALU.mult, ALU.add)
                e.then_inc(usf_done_v, 1)

            def gathered_lo(n, i):
                for h in range(2):
                    dve.wait_ge(us_hi_done, 2 * n + h + 1)
                    V.tensor_tensor(us_lo[i][:, 4 * h:4 * h + 4], usf[i][:, 4 * h:4 * h + 4], f32(us_hi[i][:, 4 * h:4 * h + 4]),
                                    ALU.subtract).then_inc(us_ready, 1)

            expert_split(0, 0, (0, 1), IN_LINE)
            dve.wait_ge(r_psum, 1)
            br = vec[:, V_BR:V_BR + 36].unsqueeze(1).to_broadcast([P, T, 36])
            link(V.tensor_tensor(logits[:, :, :], HT[:, 0:128].rearrange("p (t c) -> p t c", t=T)[:, :, 0:36], br, ALU.add))
            lg = logits[:, :, 0:4]

            def ranks(v, n, gt, eq, tie, rank):
                for t in range(T):
                    mine = v[:, t].unsqueeze(2).to_broadcast([P, n, n])
                    other = v[:, t].unsqueeze(1).to_broadcast([P, n, n])
                    V.tensor_tensor(gt[:, t], other, mine, ALU.is_gt)
                    e = V.tensor_tensor(eq[:, t], other, mine, ALU.is_equal)
                link(e)
                for t in range(T):
                    e = V.tensor_tensor(eq[:, t], eq[:, t], tie, ALU.mult)
                link(e)
                link(V.tensor_tensor(gt[:, :], gt[:, :], eq[:, :], ALU.add))
                link(V.tensor_reduce(rank[:, :, :], gt[:, :], AX.X, ALU.add))

            ranks(lg, 4, g_gt, g_eq, tie4, g_rank)
            V.tensor_scalar(g_sel[:, :, :], g_rank[:, :, :], 0.0, None, ALU.is_equal).then_inc(sel_ready, 1)
            link(V.tensor_reduce(g_max, lg, AX.X, ALU.max))
            V.tensor_tensor(g_exp[:, :, :], lg, g_max.unsqueeze(2).to_broadcast([P, T, 4]), ALU.subtract)
            dve.wait_ge(sel_ready, 1)
            for t in range(T):
                e = V.tensor_tensor(le_m[:, t], logits[:, t, 4:36].rearrange("p (g e) -> p g e", g=4),
                                    g_sel[:, t].unsqueeze(2).to_broadcast([P, 4, 8]), ALU.mult)
            link(e)
            dve.wait_ge(count_psum, 1)
            V.tensor_copy(g_total, GU[1][:, 0:4])
            link(V.tensor_tensor(g_cum[:, :, :], GU[1][:, 4:12].rearrange("p (t g) -> p t g", t=T), g_sel[:, :, :], ALU.mult))
            for g in range(EXPERT_GROUPS):
                for t in range(T):
                    e = V.tensor_scalar(pick[:, t, g], place_iota, g_cum[:, t, g:g + 1], None, ALU.is_equal)
                if g in (0, EXPERT_GROUPS - 1):
                    e.then_inc(pick_ready, 1)
            link(V.tensor_reduce(le_g[:, :, :], le_m.rearrange("p t g e -> p t e g"), AX.X, ALU.add))
            link(V.tensor_reduce(e_max, le_g[:, :, :], AX.X, ALU.max))
            V.tensor_tensor(e_exp[:, :, :], le_g[:, :, :], e_max.unsqueeze(2).to_broadcast([P, T, 8]), ALU.subtract).then_inc(r_exp_in, 1)
            ranks(le_g, 8, e_gt, e_eq, tie8, e_rank)
            gathered(0, 0)
            link(V.tensor_scalar(e_rank[:, :, :], e_rank[:, :, :], 2.0, None, ALU.is_lt))
            dve.wait_ge(r_exp, 1)
            V.tensor_reduce(g_sum, g_exp[:, :, :], AX.X, ALU.add)
            link(V.tensor_tensor(e_exp[:, :, :], e_exp[:, :, :], e_rank[:, :, :], ALU.mult))
            link(V.tensor_reduce(e_sum, e_exp[:, :, :], AX.X, ALU.add))
            V.reciprocal(p_sel, g_sum)
            link(V.reciprocal(e_sum, e_sum))
            link(V.tensor_tensor(e_sum, e_sum, p_sel, ALU.mult))
            V.tensor_tensor(e_w[:, :, :], e_exp[:, :, :], e_sum.unsqueeze(2).to_broadcast([P, T, 8]), ALU.mult).then_inc(ew_ready, 1)
            dve.wait_ge(ew_ready, 1)
            link(V.tensor_scalar(g_over, g_total, float(P), None, ALU.is_gt))
            V.tensor_reduce(over[:, 1:2], g_over, AX.X, ALU.add)
            link(V.tensor_tensor(g_base, g_over, group_iota, ALU.mult))
            link(V.tensor_reduce(over[:, 0:1], g_base, AX.X, ALU.add))
            V.tensor_copy(further[:, :], over).then_inc(further_ready, 1)

            def sparse_h_split(f):
                dve.wait_ge(hT_hi_done, f + 1)
                V.tensor_tensor(hTs_lo, HT[:, 0:S].rearrange("p (c s) -> p c s", c=2), f32(hTs_hi), ALU.subtract).then_inc(hT_ready, 1)

            def sparse_unit(half, odd, i, e, first=False, last=False):
                if not first:
                    sparse_h_split(half * 2 + (MOE_F0 + odd - 1))
                if not last:
                    expert_split(*after(half, odd), (0,))
                dve.wait_ge(silu_done, (half * 2 + (MOE_F0 + odd)) * 2 + 2)
                V.scalar_tensor_tensor(hid[:, 0], act_g[:, 0], sparse_w[:, i, bass.ds(e, 1)], GU[0][:, F_UNIT:2 * F_UNIT],
                                       ALU.mult, ALU.mult).then_inc(h_done, 2)
                if not last:
                    expert_split(*after(half, odd), (1,))
                expert_split(half, odd, (2,), IN_LINE if last else LAST_BEHIND)

            def expert_group(n, i, beside, first=False, last=False):
                half, halves = n * PER_GROUP // 2, PER_GROUP // 2
                sparse_unit(half, 0, i, 0, first=first)
                beside()
                with dve.Fori(0, halves - 1) as e:
                    sparse_unit(e + half, 1, i, e * 2 + 1)
                    sparse_unit(e + (half + 1), 0, i, e * 2 + 2)
                sparse_unit(half + halves - 1, 1, i, PER_GROUP - 1, last=last)
                if last:
                    sparse_h_split(MOE_F0 + (n + 1) * PER_GROUP - 1)

            def later_tiles():
                gathered(2, 2)
                gathered(3, 3)
                gathered_lo(1, 1)
                gathered_lo(2, 2)

            gathered_lo(0, 0)
            gathered(1, 1)
            dve.wait_ge(sw_ready, 1)
            beside = [later_tiles, lambda: gathered_lo(3, 3), lambda: None, lambda: None]
            for n in range(EXPERT_GROUPS):
                expert_group(n, n, beside[n], n == 0, n == EXPERT_GROUPS - 1)
            x_update(n6 + 1, (spread_done, 1), SPREAD)
            with dve.If(dve.value_load(further[0:1, 1:2], min_val=0, max_val=1) > 0):
                expert_split(EXPERTS // 2, 0, (0, 1), IN_LINE)
                link(V.tensor_reduce(own_place, g_cum[:, :, :], AX.X, ALU.add))
                link(V.tensor_scalar(own_place, own_place, float(P), None, ALU.subtract))
                for t in range(T):
                    e = V.tensor_scalar(pick[:, t, 0], place_iota, own_place[:, t:t + 1], None, ALU.is_equal)
                e.then_inc(pick_ready, 1)
                gathered(EXPERT_GROUPS, 0)
                gathered_lo(EXPERT_GROUPS, 0)
                dve.wait_ge(sw_ready, 2)
                expert_group(EXPERT_GROUPS, 0, lambda: None, True, True)
                x_update(n6 + 2, (spread_done, 2), SPREAD)

        @block.tensor
        def _(pe):
            def release(s_):
                pe.matmul(MOD[:, 64:65], zeros[:, 0:P], zeros[:, 0:1], start=True, stop=True, skip_group_check=True).then_inc(s_, 1)

            def carry_waits():
                pe.matmul(MOD[:, 64:65], zeros[:, 0:P], zeros[:, 0:1], start=True, stop=True, skip_group_check=True)

            def keep_warm(n, dst):
                for _ in range(n):
                    pe.matmul(dst, zeros[:, 0:P], zeros[:, 0:dst.shape[1]], start=True, stop=True, skip_group_check=True)

            def need(u, seen, off, n, order=IN_LINE):
                for j in range(off // BLK, (off + n - 1) // BLK + 1):
                    if j not in seen:
                        pe.wait_ge(split_done, u * 3 + order[j] + 1)
                        seen.add(j)

            def mm3(dst, xh, xl, off, n, first, last):
                pe.matmul(dst, xh, w_hi[:, off:off + n], start=first, stop=False, skip_group_check=True)
                pe.matmul(dst, xh, w_lo[:, off:off + n], start=False, stop=False, skip_group_check=True)
                return pe.matmul(dst, xl, w_hi[:, off:off + n], start=False, stop=last, skip_group_check=True)

            def tok(t):
                return slice(t * P, (t + 1) * P)

            def ada_step(n, col, first=None):
                if first is not None:
                    pe.wait_ge(mod_ready, first)
                pe.wait_ge(ada_ready, n - ADA_STEPS + 1)
                for h in range(2):
                    m = pe.matmul(MOD[:, bass.ds(col + h, 1)], ada_sum[:, h * P:(h + 1) * P], ones[:, 0:1],
                                  start=True, stop=True, skip_group_check=True)
                m.then_inc(mod_step, 1)

            def columns(u, ncol, b0, ada_n=None, ada_c=0, stage=None, ada_steps=2, off0=0, close=(0, 1, 2), first_of=None):
                seen, n2 = set(), ncol - 512
                m = None
                for k in range(KD):
                    off = off0 + k * ncol
                    need(u, seen, off, ncol)
                    if first_of is not None and k % 2 == 0:
                        pe.wait_ge(uT_ready, 4 * first_of + k // 2 + 1)
                    for t in range(T):
                        m = mm3(bank[b0 + t][:, 0:min(512, ncol)], uT_hi[:, k, tok(t)], uT_lo[:, k, tok(t)], off, min(512, ncol),
                                k == 0, k == KD - 1)
                        if n2 > 0:
                            dst = bank[b0 + 2][:, t * n2:(t + 1) * n2]
                            m = mm3(dst, uT_hi[:, k, tok(t)], uT_lo[:, k, tok(t)], off + 512, n2, k == 0 and t == 0, k == KD - 1)
                    for j in close:
                        if k < KD - 1 and off < (j + 1) * BLK <= off + ncol:
                            m.then_inc(used[j], 1)
                    if ada_n is not None and k == 3:
                        ada_step(ada_n, ada_c, stage)
                m.then_inc(w_done, 1)
                for j in close:
                    if (j + 1) * BLK > off0 + (KD - 1) * ncol:
                        release(used[j])
                if ada_n is not None and ada_steps > 1:
                    ada_step(ada_n + 1, ada_c + 2)

            def norm(n, q):
                keep_warm(16, GU[0][:, :])
                pe.wait_ge(x_ready, 2 * q + 2)
                for t in range(T):
                    pe.wait_ge(xn_done, 2 * q + t + 1)
                    for b in range(4):
                        for k in (2 * b, 2 * b + 1):
                            m = pe.transpose(ACC[b][:, (k % 2) * S + t * P:(k % 2) * S + (t + 1) * P], xn[:, t, k * P:(k + 1) * P], ident)
                        if t == T - 1:
                            m.then_inc(uT_psum, 1)
                pe.wait_ge(diag_done, n + 1)
                for h, b in enumerate((HT, GU[1])):
                    pe.matmul(b[:, :], ones, diag[:, 4 * h:4 * h + 4], start=True, stop=True).then_inc(gate_psum, 1)

            def gate_up(u, first_of=None, middle=None):
                seen = set()
                order = [(k, t) for k in range(KD) for t in range(T)] if first_of is None else [(k, t) for t in range(T) for k in range(KD)]
                for k, t in order:
                    if middle is not None and (k, t) == (KD // 2, 0):
                        middle()
                    need(u, seen, k * 512, 512, LAST_BEHIND if first_of is None else IN_LINE)
                    if first_of is not None and t == 0 and k % 2 == 0:
                        pe.wait_ge(uT_ready, 4 * first_of + k // 2 + 1)
                    if first_of is not None and t == 1 and k == 0:
                        pe.wait_ge(gate_ready, 2 * first_of + 2)
                    m = mm3(GU[t][:, :], uT_hi[:, k, tok(t)], uT_lo[:, k, tok(t)], k * 512, 512, k == 0, k == KD - 1)
                    if k == KD - 1 and t == 0:
                        m.then_inc(gu0_done, 1)
                    if t == T - 1 and k in (3, 7):
                        m.then_inc(used[k // 4], 1)

            def turn(f):
                pe.wait_ge(h_done, f * 2 + 2)
                for t in range(T):
                    for c in range(2):
                        m = pe.transpose(HT[:, c * S + t * P:c * S + (t + 1) * P], hid[:, t, c * P:(c + 1) * P], ident)
                m.then_inc(hT_psum, 1)

            def down(u, f, last=False):
                pe.wait_ge(hT_ready, f + 1)
                need(u, set(), 2 * BLK, BLK, LAST_UNIT if last else LAST_BEHIND)
                for t, c in [(t, c) for t in range(T) for c in range(2)]:
                    for h in range(2):
                        m = mm3(ACC[2 * t + h][:, :], hT_hi[:, c, tok(t)], hT_lo[:, c, tok(t)], 2 * BLK + c * D + h * 512, 512,
                                False, last and c == 1)
                    if last and (t, c) == (0, 1):
                        m.then_inc(first_tile, 1)
                m.then_inc(used[2], 1)

            def ffn(u0, f0, n, nn, stage):
                ada_step(stage * ADA_STEPS, 0, stage)
                gate_up(u0, nn)
                ada_step(stage * ADA_STEPS + 1, 2)
                for b in range(4):
                    pe.matmul(ACC[b][:, :], zeros[:, 0:P], zeros[:, :], start=True, stop=False, skip_group_check=True)
                with pe.Fori(1, n - 1) as i:
                    turn(f0 + i - 1)
                    gate_up(u0 + i)
                    ada_step(stage * ADA_STEPS + i + 1, i * 2 + 2)
                    down(u0 + i - 1, f0 + i - 1)

                def finish():
                    ada_step(stage * ADA_STEPS + n, 2 * n)
                    down(u0 + n - 2, f0 + n - 2)

                turn(f0 + n - 2)
                gate_up(u0 + n - 1, middle=finish)
                turn(f0 + n - 1)
                down(u0 + n - 1, f0 + n - 1, last=True)

            def half_product(lhs, chunks, closes, ready, done, late=lambda: None):
                seen = {}
                for t in range(T):
                    pe.wait_ge(*ready[t])
                    for k, (u, off) in enumerate(chunks):
                        if (t, k) == (T - 1, 2):
                            late()
                        need(u, seen.setdefault(str(u), set()), off, D)
                        for h in range(2):
                            e = mm3(ACC[2 * t + h][:, :], lhs[0][:, k, tok(t)], lhs[1][:, k, tok(t)], off + h * 512, 512, k == 0, k == 3)
                        if t == T - 1 and k in closes:
                            e.then_inc(used[closes[k]], 1)
                    release(done)

            def turn_y(m, t):
                pe.wait_ge(y_ready, 2 * m + t + 1)
                for b in range(2):
                    for i in range(4):
                        k = 4 * b + i
                        e = pe.transpose(YT[t][b][:, i * P:(i + 1) * P], y[:, t, k * P:(k + 1) * P], ident)
                    e.then_inc(yT_psum, 1)

            def merge(u0, m, close2):
                u1, u2 = u0 + 1, u0 + 2
                half_product((oT_hi[0], oT_lo[0]), [(u0, k * D) for k in range(4)], {1: 0, 3: 1}, [(oT_ready, 4 * m + 2)] * T, pa_psum)
                pe.wait_ge(oT_ready, 4 * m + 4)
                half_product((oT_hi[1], oT_lo[1]), [(u0, 4 * D), (u0, 5 * D), (u1, 0), (u1, D)], {1: 2, 3: 0},
                             [(ya_done, 2 * m + t + 1) for t in range(T)], pb_psum, lambda: turn_y(m, 0))
                seen = {}
                for half in range(2):
                    for t in range(T):
                        for k in range(4 * half, 4 * half + 4):
                            u, off = (u1, BLK + k * D) if k < 4 else (u2, (k - 4) * D)
                            need(u, seen.setdefault(str(u), set()), off, D)
                            if (t, k) == (0, 0):
                                pe.wait_ge(yT_ready, 4 * m + 2)
                            if (t, k) == (0, 3):
                                turn_y(m, 1)
                            if (t, k) == (1, 0):
                                pe.wait_ge(yT_ready, 4 * m + 4)
                            for h in range(2):
                                e = mm3(ACC[2 * t + h][:, :], yT_hi[:, k, tok(t)], yT_lo[:, k, tok(t)], off + h * 512, 512, k == 0, k == KD - 1)
                            if (t, k) == (0, KD - 1):
                                e.then_inc(first_tile, 1)
                            elif t == T - 1 and k % 2 == 1:
                                e.then_inc(used[off // BLK], 1)
                            elif (t, k) == (T - 1, 6) and close2:
                                e.then_inc(used[2], 1)

            def sc_job(j0, jobs, j):
                kind, qt, g = jobs[j]
                nk = (qt + 1) * P
                if j >= 1:
                    pe.wait_ge(bias_done, j0 + j)
                for p in range(2):
                    half = slice(DH * p, DH * p + DH)
                    for i in range(2):
                        h, c = 4 * g + 2 * i + p, 2 * g + i
                        dst = bank[p][:, i * S:i * S + nk]
                        if kind == 2:
                            m = pe.matmul(dst, qkT_m[0:QK, 0, h, tok(qt)], qkT_m[0:QK, 1, h, 0:nk], start=True, stop=True, skip_group_check=True)
                        elif kind == 3:
                            pe.matmul(dst, nlogf[:, 0, h:h + 1].to_broadcast([P, P]), tri[:, 0:nk], start=True, stop=False, skip_group_check=True)
                            if qt:
                                pe.matmul(bank[p][:, i * S + P:i * S + nk], nlogf[:, 1, h:h + 1].to_broadcast([P, P]), tri[:, 0:P],
                                          start=False, stop=False, skip_group_check=True)
                            m = pe.matmul(dst, qT_h[half, c, tok(qt)], kT_h[half, c, 0:nk], start=False, stop=True, skip_group_check=True)
                        else:
                            m = pe.matmul(dst, qT[half, c, tok(qt)], kT[kind][half, g, 0:nk], start=True, stop=True, skip_group_check=True)
                m.then_inc(sc_done, 1)

            def pv_job(j0, jobs, j, v_copied):
                kind, qt, g = jobs[j]
                pe.wait_ge(pt_copied_a, j0 + j + 1)
                if v_copied is not None:
                    pe.wait_ge(pt_copied_v, v_copied)
                if j >= 1:
                    pe.wait_ge(o_done, j0 + j)
                for a in range(4):
                    h = 4 * g + 2 * (a % 2) + a // 2
                    for kt in range(qt + 1):
                        if kind < 2:
                            v = vsw[:, kt, P * kind + DH * g:P * kind + DH * g + DH]
                        elif kind == 2:
                            v = vm[:, kt, DH * h:DH * h + DH]
                        else:
                            v = qkv[:, kt, 1024 + DH * h:1024 + DH * h + DH]
                        m = pe.matmul(HT[:, a * DH:(a + 1) * DH], pT[j % 2][:, kt, a], v, start=kt == 0, stop=kt == qt, skip_group_check=True)
                m.then_inc(pv_done, 1)

            def jobs_run(j0, v0, jobs, beside=lambda j: None):
                nv = 0
                sc_job(j0, jobs, 0)
                for j, (kind, qt, g) in enumerate(jobs):
                    if j + 1 < len(jobs):
                        sc_job(j0, jobs, j + 1)
                    beside(j)
                    pe.wait_ge(exp_done, j0 + j + 1)
                    if j >= 1:
                        pe.wait_ge(pt_copied_a, j0 + j)
                    if nv:
                        pe.wait_ge(pt_copied_v, v0 + nv)
                    for kt in range(qt + 1):
                        for h in range(4):
                            m = pe.transpose(bank[4 + kt][:, h * P:(h + 1) * P], scores[j % 2][:, h // 2, h % 2, tok(kt)], ident)
                    m.then_inc(pt_psum, 1)
                    if j:
                        pv_job(j0, jobs, j - 1, v0 + nv if jobs[j - 1][1] else None)
                    nv += qt
                pv_job(j0, jobs, len(jobs) - 1, v0 + nv if jobs[-1][1] else None)

            def turn_rows(dst, src, cols, parts=P):
                for t in range(T):
                    m = pe.transpose(dst[0:parts, t * P:(t + 1) * P], src(t, cols), ident)
                return m

            pe.wait_ge(first_ready, 1)
            for s_ in used + [mod_step]:
                release(s_)

            def turn_first(b):
                pe.wait_ge(first_copied, b + 1)
                for c in range(4 * b, 4 * b + 4):
                    m = pe.matmul(MOD[:, c:c + 1], first_row[:, c * P:(c + 1) * P], ones[0:1, 0:1], start=True, stop=True, skip_group_check=True)
                    if c % 2:
                        m.then_inc(mod_step, 1)

            pe.wait_ge(c_ready, 1)
            for st in range(ADA_STEPS):
                slot, b = st % len(first_w), st // 2
                pe.wait_ge(first_landed[slot], 16 * (st // len(first_w)) + 16)
                for k in range(KD):
                    m = pe.matmul(bank[b][0:1, (st % 2) * ADA_COLS:(st % 2 + 1) * ADA_COLS], c_act[:, k:k + 1], first_w[slot][:, k],
                                  start=k == 0, stop=k == KD - 1, skip_group_check=True)
                m.then_inc(first_used, 1)
                if st % 2:
                    release(first_psum)
                    if b == 0:
                        pe.wait_ge(cst_landed, 16)
                    else:
                        turn_first(b - 1)
            turn_first(ADA_STEPS // 2 - 1)

            with pe.Fori(0, DEPTH) as l:
                u_mix = l * LAYER_UNITS + FFN_UNITS
                norm(l * 3, l * 3)
                ffn(l * LAYER_UNITS, l * 2 * FFN_UNITS, FFN_UNITS, l * 3, l * 3 + 1)

                norm(l * 3 + 1, l * 3 + 1)
                stage = l * 3 + 2
                for m in range(2):
                    if m == 1:
                        pe.wait_ge(gate_ready, l * 6 + 4)
                    columns(u_mix + m, 768, 3 * m, stage * ADA_STEPS + 2 * m, 4 * m, stage if m == 0 else None,
                            first_of=l * 3 + 1 if m == 0 else None)
                pe.wait_ge(w_evac_a, l * 9 + 2)
                pe.wait_ge(w_evac_v, l * 3 + 1)
                columns(u_mix + 2, U2_COLS, 0, stage * ADA_STEPS + 4, 8, ada_steps=1, close=(0,))
                src = lambda t, cols: proj[:, t, cols]
                pe.wait_ge(lat_ready, l + 1)
                pe.wait_ge(w_evac_a, l * 9 + 4)
                pe.wait_ge(w_evac_v, l * 3 + 2)
                for c in range(5):
                    m = turn_rows(bank[2 + c // 2][:, (c % 2) * S:(c % 2) * S + S], src, slice(C_CQ + c * P, C_CQ + c * P + P))
                    if c in (1, 3, 4):
                        m.then_inc(cqT_psum, 1)
                pe.wait_ge(w_evac_a, l * 9 + 5)
                pe.wait_ge(w_evac_v, l * 3 + 3)
                for c in range(4):
                    m = turn_rows(bank[5 + c // 2][:, (c % 2) * S:(c % 2) * S + S], src, slice(C_Q + c * P, C_Q + c * P + P))
                    if c % 2:
                        m.then_inc(q_psum, 1)
                for kind, (c0, s_) in enumerate(((C_KS, ks_psum), (C_KW, kw_psum))):
                    for g in range(GROUPS):
                        for t in range(T):
                            for p in range(2):
                                m = pe.matmul(bank[kind][DH * p:DH * p + DH, g * S + t * P:g * S + (t + 1) * P],
                                              proj[:, t, c0 + g * DH:c0 + g * DH + DH], ident, start=True, stop=True,
                                              skip_group_check=True)
                    m.then_inc(s_, 1)
                pe.wait_ge(cqT_ready, l * 3 + 2)
                for k in range(2):
                    for g in range(GROUPS):
                        for t in range(T):
                            for p in range(2):
                                m = pe.matmul(bank[2 + k][DH * p:DH * p + DH, g * S + t * P:g * S + (t + 1) * P],
                                              proj[:, t, C_KC + (2 * k + g) * DH:C_KC + (2 * k + g + 1) * DH], ident,
                                              start=True, stop=True, skip_group_check=True)
                m.then_inc(c_psum, 1)
                ada_step(stage * ADA_STEPS + 5, 10)
                keep_warm(16, MOD[:, 64:512])
                pe.wait_ge(blocks_ready, l + 1)
                pe.wait_ge(cqT_ready, l * 3 + 3)
                carry_waits()
                hidden_cmp = bank[4][:, 0:64].rearrange("p (c n) -> p c n", c=2 * GROUPS)
                for j in range(CMP_STRIDE):
                    m = pe.matmul(hidden_cmp[:, :, 0:N_CMP], cmpw[:, j // 8, (j % 8) * 2 * DH:(j % 8 + 1) * 2 * DH], blocks[:, :, j],
                                  start=j == 0, stop=j == CMP_STRIDE - 1, skip_group_check=True)
                m.then_inc(hidc_psum, 1)
                pe.wait_ge(hidc_ready, l + 1)
                pe.wait_ge(q_ready, l * 2 + 2)
                carry_waits()
                for g in range(GROUPS):
                    for p in range(2):
                        pe.matmul(bank[4 + g][DH * p:DH * p + DH, 0:N_CMP], lvec[0:DH, L_W2:L_W2 + DH], hid_cmp[0:DH, 0, g, 0:N_CMP],
                                  start=True, stop=True, skip_group_check=True)
                    for i in range(4):
                        m = pe.matmul(bank[4 + g][32 * i:32 * i + N_CMP, 64:128], hid_cmp[DH:P, 1, g, 0:N_CMP], lvec[DH:P, L_W2 + DH:L_W2 + 2 * DH],
                                      start=True, stop=True, skip_group_check=True)
                m.then_inc(kvc_psum, 1)
                keep_warm(8, MOD[:, 64:512])
                pe.wait_ge(kvc_ready, l + 1)
                for p in range(2):
                    half = slice(DH * p, DH * p + DH)
                    for qt in range(2):
                        for i in range(4):
                            m = pe.matmul(bank[4 + p][:, 64 * qt + 16 * i:64 * qt + 16 * i + N_CMP], qT[half, i, tok(qt)], kT_cmp[half, i // 2, 0:N_CMP],
                                          start=True, stop=True, skip_group_check=True)
                m.then_inc(cs_psum, 1)
                pe.wait_ge(ks_ready, l + 1)
                pe.wait_ge(kw_ready, l + 1)
                seen = set()
                for b in range(4):
                    for k in range(3):
                        off = UQ_OFF + k * 768 + (b % 2) * 384
                        need(u_mix + 2, seen, off, 384)
                        m = mm3(bank[b][:, 0:384], cqT_hi[:, k, tok(b // 2)], cqT_lo[:, k, tok(b // 2)], off, 384, k == 0, k == 2)
                    m.then_inc(uq_psum, 1)
                for j in (1, 2):
                    release(used[j])
                pe.wait_ge(cp_exp, l + 1)
                for a in range(4):
                    m = pe.transpose(bank[6][:, a * P:(a + 1) * P], p_cmp[:, 4 * a:4 * a + 4, :], ident)
                m.then_inc(cp_psum, 1)
                need(u_mix + 3, set(), 0, BLK)
                for t in range(T):
                    for k in range(2):
                        m = mm3(bank[4 + t][:, :], cqT_hi[:, 3 + k, tok(t)], cqT_lo[:, 3 + k, tok(t)], k * 512, 512, k == 0, k == 1)
                    m.then_inc(uk_psum, 1)
                pe.wait_ge(cp_ready, l + 1)
                pe.wait_ge(uq_copied, l * 4 + 4)
                for i in range(4):
                    rows = slice(32 * i, 32 * i + N_CMP)
                    for qt in range(2):
                        for p in range(2):
                            m = pe.matmul(bank[i][:, 128 * qt + 64 * p:128 * qt + 64 * p + 64], pT_cmp[rows, 2 * p + qt], v_cmp[rows, i // 2],
                                          start=True, stop=True, skip_group_check=True)
                m.then_inc(co_psum, 1)
                for t in range(T):
                    if t == 1:
                        pe.wait_ge(uk_copied, l * 2 + 1)
                    for k in range(2):
                        m = mm3(bank[6 - 2 * t][:, :], cqT_hi[:, 3 + k, tok(t)], cqT_lo[:, 3 + k, tok(t)], 1024 + k * 512, 512, k == 0, k == 1)
                    m.then_inc(uv_psum, 1)
                release(used[0])
                pe.wait_ge(rope_done, l + 1)
                pe.wait_ge(co_done, l + 1)
                for b in range(4):
                    for i in range(2):
                        m = turn_rows(bank[b][:, i * S:i * S + S], lambda t, h: q_tok[:, t, h], 2 * b + i, QK)
                    m.then_inc(qm_psum, 1)
                pe.wait_ge(uk_copied, l * 2 + 2)
                for b in range(4):
                    if b == 1:
                        pe.wait_ge(uv_ready, l * 2 + 2)
                    if b == 3:
                        pe.wait_ge(km_ready, l * 4 + 1)
                    for i in range(2):
                        m = turn_rows(bank[K_BANKS[b]][:, i * S:i * S + S], lambda t, h: k_tok[:, t, h], 2 * b + i, QK)
                    m.then_inc(km_psum, 1)
                pe.wait_ge(qm_ready, l * 4 + 4)
                seen = {m: set() for m in (3, 4, 5)}

                def beside(j):
                    if j == 0:
                        pe.wait_ge(km_ready, l * 4 + 4)
                    if j % 3 == 0 and j:
                        pe.wait_ge(w_evac_a, l * 9 + 5 + j // 3)
                    for i, k in GATE_CHUNKS[j]:
                        m, off = gate_place(i, k)
                        need(u_mix + m, seen[m], off, 512)
                        for t in range(T):
                            e = mm3(bank[2 + t][:, :], uT_hi[:, k, tok(t)], uT_lo[:, k, tok(t)], off, 512, k == 0, k == KD - 1)
                        if k % 4 == 3:
                            e.then_inc(used[off // BLK], 1)
                        if k == KD - 1:
                            release(w_done)
                    if j % 2 == 1:
                        ada_step(stage * ADA_STEPS + 6 + j // 2, 12 + j - 1)

                jobs_run(l * NJ, l * 6, JOBS, beside)
                pe.wait_ge(w_evac_a, l * 9 + 9)
                pe.wait_ge(o_done, l * NJ + NJ)
                for b in range(4):
                    o = o_a if b < 2 else o_b
                    for i in range(2):
                        c = 2 * (b % 2) + i
                        m = turn_rows(bank[3 + b][:, i * S:i * S + S], lambda t, c_: o[:, t, c_], slice(c * P, c * P + P))
                    m.then_inc(oT_psum, 1)
                merge(u_mix + MIX_IN_UNITS, l, True)

                norm(l * 3 + 2, l * 3 + 2)
                ffn(l * LAYER_UNITS + FFN_UNITS + MIX_IN_UNITS + MERGE_UNITS, l * 2 * FFN_UNITS + FFN_UNITS, FFN_UNITS, l * 3 + 2, l * 3 + 3)

            n6, u = 3 * DEPTH, HYB_U0
            norm(n6, n6 + 1)
            evac_a = [2, 4, 6, 8, 9, 10, 11]
            for m in range(HYB_IN_UNITS):
                if m == 1:
                    pe.wait_ge(gate_ready, 2 * n6 + 2)
                if m >= 2:
                    pe.wait_ge(w_evac_a, DEPTH * 9 + evac_a[m - 2])
                    pe.wait_ge(w_evac_v, DEPTH * 3 + min(m - 1, 4))
                columns(u + m, 768 if m < 6 else 520, 3 * (m % 2), (n6 + 1) * ADA_STEPS + 2 * m if m < 6 else None, 4 * m,
                        n6 + 1 if m == 0 else None, first_of=n6 if m == 0 else None)
            pe.wait_ge(w_evac_a, DEPTH * 9 + 11)
            pe.wait_ge(u_ready, 1)
            for c in range(4):
                m = turn_rows(bank[4 + c // 2][:, (c % 2) * S:(c % 2) * S + S], lambda t, c_: u_tok[:, t, c_], slice(c * P, c * P + P))
                if c % 2:
                    m.then_inc(uc_psum, 1)
            for c in range(4):
                m = turn_rows(bank[6 - 3 * (c // 2)][:, (c % 2) * S:(c % 2) * S + S], lambda t, c_: xcb[:, t, c_],
                              slice(1024 + c * P, 1024 + c * P + P))
            m.then_inc(b_psum, 1)
            pe.wait_ge(qkn_ready, 1)
            for c in range(4):
                m = turn_rows(bank[c // 2][:, (c % 2) * S:(c % 2) * S + S], lambda t, c_: qkv[:, t, c_], slice(c * P, c * P + P))
                if c % 2:
                    m.then_inc(q_psum, 1)
            pe.wait_ge(uc_ready, 1)
            for c in range(4):
                m = turn_rows(bank[2 + 2 * (c // 2)][:, (c % 2) * S:(c % 2) * S + S], lambda t, c_: qkv[:, t, c_],
                              slice(512 + c * P, 512 + c * P + P))
                if c % 2:
                    m.then_inc(kh_psum, 1)
            pe.wait_ge(logf_ready, 1)
            pe.matmul(bank[5][:, 0:8], tri[:, 0:P], nlogf[:, 0], start=True, stop=True, skip_group_check=True)
            pe.matmul(bank[5][:, 8:16], ones, nlogf[:, 0], start=True, stop=False, skip_group_check=True)
            pe.matmul(bank[5][:, 8:16], tri[:, 0:P], nlogf[:, 1], start=False, stop=True, skip_group_check=True).then_inc(fcum_psum, 1)
            pe.wait_ge(q_ready, DEPTH * 2 + 2)
            pe.wait_ge(kh_ready, 2)
            pe.wait_ge(ya_hi_done, 2)
            pe.wait_ge(oT_ready, DEPTH * 4 + 2)
            pe.wait_ge(fcum_ready, 1)
            jobs_run(DEPTH * NJ, DEPTH * 6, HYB_JOBS)
            um = u + HYB_IN_UNITS
            pe.wait_ge(o_done, DEPTH * NJ + len(HYB_JOBS))
            for b in range(2):
                for i in range(2):
                    c = 2 * b + i
                    m = turn_rows(bank[5 + b][:, i * S:i * S + S], lambda t, c_: o_h[:, t, c_], slice(c * P, c * P + P))
                m.then_inc(oT_psum, 1)
            merge(um, DEPTH, False)
            norm(n6 + 1, n6 + 2)
            pe.wait_ge(uT_ready, 4 * n6 + 8)
            pe.wait_ge(gate_ready, 2 * n6 + 4)
            need(um + 2, set(), 2 * BLK, BLK)
            for t in range(T):
                for k in range(KD):
                    m = mm3(HT[:, 64 * t:64 * t + 36], uT_hi[:, k, tok(t)], uT_lo[:, k, tok(t)], 2 * BLK + 36 * k, 36, k == 0, k == KD - 1)
            m.then_inc(r_psum, 1)
            release(used[2])
            pe.wait_ge(sel_ready, 1)
            pe.matmul(GU[1][:, 0:4], ones, g_sel[:, 0], start=True, stop=False, skip_group_check=True)
            pe.matmul(GU[1][:, 0:4], ones, g_sel[:, 1], start=False, stop=True, skip_group_check=True)
            pe.matmul(GU[1][:, 4:8], tri[:, 0:P], g_sel[:, 0], start=True, stop=True, skip_group_check=True)
            pe.matmul(GU[1][:, 8:12], ones, g_sel[:, 0], start=True, stop=False, skip_group_check=True)
            pe.matmul(GU[1][:, 8:12], tri[:, 0:P], g_sel[:, 1], start=False, stop=True, skip_group_check=True).then_inc(count_psum, 1)
            def gather(i):
                for k in range(KD):
                    for t in range(T):
                        m = pe.matmul(bank[GATHER_BANKS[i][k // 4]][:, (k % 4) * P:(k % 4 + 1) * P], xn[:, t, k * P:(k + 1) * P], pick[:, t, i],
                                      start=t == 0, stop=t == T - 1, skip_group_check=True)
                    if k % 4 == 3:
                        m.then_inc(us_psum, 1)

            def turn_picks(tiles):
                for i in range(tiles):
                    for t in range(T):
                        m = pe.transpose(bank[6 + i // 2][:, (i % 2) * S + t * P:(i % 2) * S + (t + 1) * P], pick[:, t, i], ident)
                m.then_inc(pick_T_psum, 1)

            def gather_weights(tiles):
                for i in range(tiles):
                    for t in range(T):
                        m = pe.matmul(GU[1][:, 64 + i * PER_GROUP:64 + (i + 1) * PER_GROUP], pick[:, t, i], e_w[:, t],
                                      start=t == 0, stop=t == T - 1, skip_group_check=True)
                m.then_inc(sw_psum, 1)

            def sparse_gate_up(u, n, i, first=False):
                seen = set()
                for k in range(KD):
                    need(u, seen, k * 512, 512, IN_LINE if first else LAST_BEHIND)
                    if k % 4 == 0:
                        pe.wait_ge(us_ready, 2 * n + k // 4 + 1)
                    m = mm3(GU[0][:, :], us_hi[i][:, k], us_lo[i][:, k], k * 512, 512, k == 0, k == KD - 1)
                    if k in (3, 7):
                        m.then_inc(used[k // 4], 1)

            def sparse_turn(f):
                pe.wait_ge(h_done, f * 2 + 2)
                for c in range(2):
                    m = pe.transpose(HT[:, c * P:(c + 1) * P], hid[:, 0, c * P:(c + 1) * P], ident)
                m.then_inc(hT_psum, 1)

            def sparse_down(u, f, order=LAST_BEHIND, done=False, clear=False):
                pe.wait_ge(hT_ready, f + 1)
                need(u, set(), 2 * BLK, BLK, order)
                for c in range(2):
                    for h in range(2):
                        m = mm3(ACC[h][:, :], hTs_hi[:, c], hTs_lo[:, c], 2 * BLK + c * D + h * 512, 512, False, done and c == 1)
                m.then_inc(used[2], 1)
                if done:
                    pe.matmul(SPREAD[3][:, 0:1], zeros[:, 0:P], zeros[:, 0:1], start=clear, stop=True, skip_group_check=True).then_inc(ys_psum, 1)

            def clear_out():
                for h in range(2):
                    pe.matmul(ACC[h][:, :], zeros[:, 0:P], zeros[:, :], start=True, stop=False, skip_group_check=True)

            def spread(n, i, first, last):
                pe.wait_ge(ys_ready, n + 1)
                for t in range(T):
                    for h in range(2):
                        m = pe.matmul(SPREAD[2 * t + h][:, :], pick_T[:, i, tok(t)], y_s[n][:, h * 512:(h + 1) * 512],
                                      start=first, stop=last, skip_group_check=True)
                    if last:
                        m.then_inc(first_tile if t == 0 else spread_done, 1)

            def expert_group(n, i, beside, first=False, last=False):
                u, f = MOE_U0 + n * PER_GROUP, MOE_F0 + n * PER_GROUP
                if not first:
                    sparse_turn(f - 1)
                sparse_gate_up(u, n, i, first)
                if not first:
                    sparse_down(u - 1, f - 1, done=True, clear=n == 1)
                beside()
                sparse_turn(f)
                sparse_gate_up(u + 1, n, i)
                if not first:
                    spread(n - 1, i - 1, n == 1, False)
                clear_out()
                sparse_down(u, f)
                with pe.Fori(2, PER_GROUP) as e:
                    sparse_turn(f + e - 1)
                    sparse_gate_up(u + e, n, i)
                    sparse_down(u + e - 1, f + e - 1)
                if last:
                    sparse_turn(f + PER_GROUP - 1)
                    sparse_down(u + PER_GROUP - 1, f + PER_GROUP - 1, IN_LINE, done=True, clear=n == EXPERT_GROUPS)
                    spread(n, i, n == EXPERT_GROUPS, True)

            def later_tiles():
                pe.wait_ge(usf_done_a, 1)
                pe.wait_ge(usf_done_v, 1)
                gather(2)
                pe.wait_ge(pick_T_ready, 1)
                pe.wait_ge(sw_ready, 1)
                gather(3)
                pe.wait_ge(usf_done_a, 2)
                pe.wait_ge(usf_done_v, 2)

            def tiles_out():
                pe.wait_ge(usf_done_a, EXPERT_GROUPS)
                pe.wait_ge(usf_done_v, EXPERT_GROUPS)

            pe.wait_ge(pick_ready, 1)
            gather(0)
            pe.wait_ge(pick_ready, 2)
            turn_picks(EXPERT_GROUPS)
            gather(1)
            pe.wait_ge(ew_ready, 1)
            gather_weights(EXPERT_GROUPS)
            beside = [later_tiles, tiles_out, lambda: None, lambda: None]
            for n in range(EXPERT_GROUPS):
                expert_group(n, n, beside[n], n == 0, n == EXPERT_GROUPS - 1)
            pe.wait_ge(further_ready, 1)
            with pe.If(pe.value_load(further[0:1, 1:2], min_val=0, max_val=1) > 0):
                pe.wait_ge(x_ready, 2 * (3 * DEPTH + 4))
                pe.wait_ge(pick_ready, 3)
                gather(0)
                turn_picks(1)
                gather_weights(1)
                pe.wait_ge(pick_T_ready, 2)
                pe.wait_ge(sw_ready, 2)
                expert_group(EXPERT_GROUPS, 0, lambda: None, True, True)


def shape_constants():
    c = np.zeros((P, K_ALL), np.float32)
    q, k = np.arange(P)[:, None], np.arange(S)[None, :]
    c[:, K_ID:K_ID + 128] = np.eye(P)
    c[:, K_ONE:K_ONE + 128] = 1
    for t, (o, n) in enumerate(((0, P), (P, S))):
        d = (t * P + q) - k[:, :n]
        c[:, K_DIST + o:K_DIST + o + n] = np.where(d >= 0, -d, MASKED)
        c[:, K_MASK + o:K_MASK + o + n] = np.where(d >= 0, 0, MASKED)
    ends = np.arange(N_CMP) * CMP_STRIDE + CMP_BLOCK - 1
    b = np.zeros((P, 2, T, 4, 16), np.float32)
    for p in range(2):
        for t in range(T):
            for i in range(4):
                d = (t * P + q) - ends[None, :]
                b[:, p, t, i, :N_CMP] = np.where(d >= 0, -np.float32(SLOPES[2 * i + p]) * d.astype(np.float32), MASKED)
            c[:, K_VALID + t] = (t * P + np.arange(P)) >= CMP_BLOCK - 1
    c[:, K_CMPB:K_CMPB + 256] = b.reshape(P, 256)
    half = ROPE // 2
    inv = np.float32(10000.0) ** (-np.arange(half, dtype=np.float32) / half)
    ang = np.arange(S, dtype=np.float32)[:, None] * inv[None, :].astype(np.float32)
    for off, f in ((K_COS, np.cos), (K_SIN, np.sin)):
        v = np.tile(f(ang).astype(np.float32), (1, 2)).reshape(T, P, ROPE)
        c[:, off:off + 64] = v.transpose(1, 0, 2).reshape(P, 64)
    c[:, K_TRI:K_TRI + S] = (k >= q)
    c[:, K_TIE8:K_TIE8 + 64] = np.tril(np.ones((8, 8)), -1).reshape(1, 64)
    c[:, K_TIE4:K_TIE4 + 16] = np.tril(np.ones((4, 4)), -1).reshape(1, 16)
    c[:, K_PLACE:K_PLACE + P] = np.arange(P) + 1
    c[:, K_BASE:] = 3 * PER_GROUP * np.arange(EXPERT_GROUPS)
    return c


def kernel(**inputs):
    import concourse.bacc as bacc
    from concourse.bass_utils import run_bass_kernel_spmd

    a = {n: np.asarray(v) for n, v in inputs.items()}

    def rows(w):
        return w.reshape(w.shape[0] // P, P, w.shape[1]).transpose(1, 0, 2)

    units = np.zeros((MOE_U0 + EXPERTS, P, UNIT), np.float32)
    at = [0]

    def put(*parts):
        o = 0
        for p_ in parts:
            flat = p_.reshape(P, -1)
            units[at[0], :, o:o + flat.shape[1]] = flat
            o += flat.shape[1]
        at[0] += 1

    def put_ffn(gate, up, down):
        gu = np.concatenate([rows(gate), rows(up)], axis=2)
        put(gu, rows(down))

    def put_merge(wa, wb, wo, tail=None):
        ra, rb, ro = rows(wa), rows(wb), rows(wo)
        put(ra, rb[:, 0:2])
        put(rb[:, 2:4], ro[:, 0:4])
        put(ro[:, 4:8], *([] if tail is None else [rows(tail)]))

    splits = np.cumsum([512, 128, 128, 128, 128, 128, 128, 24, 384, 256, 32])
    for l in range(DEPTH):
        for f in range(FFN_UNITS):
            s_ = slice(f * F_UNIT, (f + 1) * F_UNIT)
            put_ffn(a["ffn1_gate"][l][:, s_], a["ffn1_up"][l][:, s_], a["ffn1_down"][l][s_])
        q, kc, vc, ks, vs, kw, vw, gn, cq, ckv, kr, gm = np.split(a["w_in"][l], splits, axis=1)
        w = rows(np.concatenate([cq, ckv, kr, gn, kc, vc, ks, kw, q, vs, vw], axis=1))
        g = rows(gm)
        put(w[:, :, 0:768])
        put(w[:, :, 768:1536])
        put(w[:, :, 1536:], rows(a["mla_w_uq"][l]))
        sets = np.concatenate([g[:, :, i * 512:(i + 1) * 512].reshape(P, -1) for i in range(4)], axis=1)
        put(rows(a["mla_w_uk"][l]), rows(a["mla_w_uv"][l]), sets[:, :2 * BLK])
        put(sets[:, 2 * BLK:5 * BLK])
        put(sets[:, 5 * BLK:])
        put_merge(a["w_branch_a"][l], a["w_branch_b"][l], a["w_out"][l])
        for f in range(FFN_UNITS):
            s_ = slice(f * F_UNIT, (f + 1) * F_UNIT)
            put_ffn(a["ffn2_gate"][l][:, s_], a["ffn2_up"][l][:, s_], a["ffn2_down"][l][s_])
    xi, cb, cc, q, k, v, fl, ga, gb = np.split(a["w_in_2"][0], np.cumsum([512] * 6 + [8, D]), axis=1)
    w = rows(np.concatenate([xi, cc, cb, q, k, v, fl, ga, gb], axis=1))
    for m in range(HYB_IN_UNITS):
        put(w[:, :, 768 * m:768 * (m + 1)])
    put_merge(a["w_out_conv_2"][0], a["w_out_attn_2"][0], a["w_o_2"][0],
              np.concatenate([a["w_router_group_2"][0], a["w_router_expert_2"][0]], axis=1))
    for e in range(EXPERTS):
        put_ffn(a["w_gate_2"][0, e], a["w_up_2"][0, e], a["w_down_2"][0, e])
    assert at[0] == MOE_U0 + EXPERTS
    places = np.array([[3 * u + j for j in range(3)] for u in range(MOE_U0)])
    ffn_starts = [(l * LAYER_UNITS + o, FFN_UNITS) for l in range(DEPTH) for o in (0, LAYER_UNITS - FFN_UNITS)]
    for u0, n in ffn_starts:
        for u in range(u0, u0 + n + 1):
            for j in range(3):
                if (u, j) not in ((u0, 0), (u0, 1), (u0 + n, 1), (u0 + n, 2)):
                    places[u, j] = 3 * u + (LAST_UNIT if u == u0 + n - 1 else LAST_BEHIND)[j]
    blocks = units.reshape(-1, P, 3, BLK).transpose(0, 2, 1, 3).reshape(-1, P, BLK)
    stream, experts = np.empty((MOE_U0 * 3, P, BLK), np.float32), np.ascontiguousarray(blocks[MOE_U0 * 3:])
    stream[places.reshape(-1)] = blocks[:MOE_U0 * 3]

    w_ada = np.concatenate([a["w_ada"].reshape(DEPTH, D, 3, 3 * D).transpose(0, 2, 1, 3).reshape(-1, D, 3 * D),
                            a["w_ada_2"][0].reshape(D, 2, 3 * D).transpose(1, 0, 2)], axis=0)
    ada = np.ascontiguousarray(w_ada.reshape(STAGES, P, KD, ADA_STEPS, ADA_COLS).transpose(0, 3, 1, 2, 4)
                               .reshape(STAGES * ADA_STEPS, P, KD, ADA_COLS))

    def cols(v):
        return v.reshape(-1, P).T

    vecs = np.zeros((P, V_ALL), np.float32)
    vecs[:, V_C:V_C + 8] = a["c"][0].reshape(P, KD)
    vecs[:, V_C + 8:V_C + 16] = a["c_2"][0].reshape(P, KD)
    vecs[:, V_BADA:V_BADA + STAGES * 24] = cols(np.concatenate([a["b_ada"].reshape(-1), a["b_ada_2"].reshape(-1)]))
    vecs[:, V_GAIN:V_HALF - 8], vecs[:, V_HALF - 8:V_HALF] = 1, cols(a["norm1_w_2"][0])
    vecs[:, V_HALF:V_HALF + DEPTH - 1], vecs[:, V_HALF + DEPTH - 1] = 0.5, 1
    vecs[:, V_N2:V_N2 + 8] = cols(a["norm2_w_2"][0])
    vecs[:, V_CONV:V_CONV + 12] = a["conv_w_2"][0].reshape(3, 4, P).transpose(2, 1, 0).reshape(P, 12)
    vecs[:, V_QN] = np.tile(a["q_norm_w_2"][0], 2)
    vecs[:, V_KN] = np.tile(a["k_norm_w_2"][0], 2)
    vecs[:, V_BF:V_BF + 8] = a["b_forget_2"][0][None, :]
    vecs[:, V_BR:V_BR + 36] = np.concatenate([a["b_router_group_2"][0], a["b_router_expert_2"][0]])[None, :]
    layer_vecs = np.zeros((DEPTH, P, L_ALL), np.float32)
    cmp_w1 = np.zeros((DEPTH, P, 2, CMP_STRIDE * DH), np.float32)
    for l in range(DEPTH):
        for k_, n in enumerate(("cmpk", "cmpv")):
            layer_vecs[l, :, L_PE + CMP_STRIDE * k_:L_PE + CMP_STRIDE * (k_ + 1)] = (
                a[n + "_pe"][l].reshape(2, CMP_STRIDE, DH).transpose(0, 2, 1).reshape(P, CMP_STRIDE))
            layer_vecs[l, :, L_W2 + DH * k_:L_W2 + DH * k_ + DH] = np.tile(a[n + "_w2"][l], (2, 1))
            w1 = a[n + "_w1"][l].reshape(2, CMP_STRIDE, DH, DH).transpose(0, 2, 1, 3)
            cmp_w1[l].reshape(P, CMP_STRIDE, 2, DH)[:, :, k_] = w1.reshape(P, CMP_STRIDE, DH)
        layer_vecs[l, :, L_QN:L_QN + 3] = cols(a["mla_q_norm"][l])
        layer_vecs[l, :, L_KVN:L_KVN + 2] = cols(a["mla_kv_norm"][l])
    arrays = {
        "weight_stream": stream, "expert_blocks": experts, "ada_steps": ada, "shape_constants": shape_constants(), "vectors": vecs,
        "layer_vectors": layer_vecs, "compress_w1": cmp_w1,
        "final_norm_rows": np.ascontiguousarray(np.broadcast_to(a["final_norm"], (P, D))),
        "tokens": np.ascontiguousarray(a["x"][0]),
    }
    nc = bacc.Bacc("TRN2", target_bir_lowering=False, num_devices=1)
    args = [nc.dram_tensor(n, v_.shape, mybir.dt.from_np(v_.dtype), kind="ExternalInput").ap() for n, v_ in arrays.items()]
    out = nc.dram_tensor("out", (S, D), F32, kind="ExternalOutput").ap()
    program(nc, *args, out)
    r = run_bass_kernel_spmd(nc, [arrays], core_ids=[0])
    return r.results[0]["out"].reshape(1, S, D)
```
